# Optimizing a Trainium2 kernel written in Bass

```python
import jax, jax.numpy as jnp
from jax import lax
import numpy as np

D_MODEL = 1024
BATCH = 1
SEQ = 256
DEPTH = 2

HEAD_DIM = 64
ROT_DIM = HEAD_DIM // 4
ROPE_THETA = 500000.0
A_HEADS = D_MODEL // HEAD_DIM
A_KV_HEADS = 4
A_GROUP = A_HEADS // A_KV_HEADS
CMP_BLOCK = 32
CMP_STRIDE = 16
CMP_HID = 256
SLC_BLOCK = 64
N_SEL = 16
NSA_WIN = 512
Q_BLOCK = 128
A_Q = A_HEADS * HEAD_DIM
A_KV = A_KV_HEADS * HEAD_DIM
A_SPLITS = tuple(A_Q + i * A_KV for i in range(7))
A_IN = A_Q + 6 * A_KV + 3 * A_HEADS
B_HEADS = D_MODEL // HEAD_DIM
B_KV_HEADS = 2
B_GROUP = B_HEADS // B_KV_HEADS
SWA_WIN = 128
SWA_BLOCK = 128
B_Q = B_HEADS * HEAD_DIM
B_KV = B_KV_HEADS * HEAD_DIM
D_FF = 2816
N_EXPERTS = 8
TOP_K = 2
D_FF_EXPERT = 3584
MOE_BLOCK = 128
N_A_LAYERS = DEPTH // 2
N_B_LAYERS = DEPTH - N_A_LAYERS
N_DENSE = (DEPTH + 1) // 2
N_MOE = DEPTH // 2
ALPHA = (2 * DEPTH) ** 0.25
BETA = (8 * DEPTH) ** -0.25
LN_EPS = 1e-5
NEG = -1e30
FORCE = 1e9

kernel_name = "yoco_nsa_swa_sink_moe_deepnorm"

def layer_norm(x, g, b):
    xf = x.astype(jnp.float32)
    mu = xf.mean(-1, keepdims=True)
    var = jnp.square(xf - mu).mean(-1, keepdims=True)
    return ((xf - mu) * lax.rsqrt(var + LN_EPS) * g + b).astype(x.dtype)

def rope_tables(positions):
    inv = ROPE_THETA ** (-jnp.arange(0, ROT_DIM, 2, dtype=jnp.float32) / ROT_DIM)
    ang = positions.astype(jnp.float32)[..., None] * inv
    return jnp.cos(ang), jnp.sin(ang)

def apply_partial_rope(x, cos, sin):
    xr = x[..., :ROT_DIM].astype(jnp.float32)
    x1, x2 = xr[..., :ROT_DIM // 2], xr[..., ROT_DIM // 2:]
    c, s = cos[:, :, None, :], sin[:, :, None, :]
    rot = jnp.concatenate([x1 * c - x2 * s, x2 * c + x1 * s], axis=-1)
    return jnp.concatenate([rot.astype(x.dtype), x[..., ROT_DIM:]], axis=-1)

def masked_softmax(s, mask):
    p = jax.nn.softmax(jnp.where(mask, s, NEG), axis=-1)
    return jnp.where(mask, p, 0.0)

gather_blocks = jax.vmap(jax.vmap(lambda blocks, ix: blocks[ix]))

def compress_blocks(t, pos, w1, w2):
    bsz, seq, g, dh = t.shape
    r = CMP_BLOCK // CMP_STRIDE
    chunks = t.reshape(bsz, seq // CMP_STRIDE, CMP_STRIDE, g, dh)
    n_cmp = seq // CMP_STRIDE - r + 1
    blocks = jnp.concatenate([chunks[:, i:i + n_cmp] for i in range(r)], axis=2)
    blocks = blocks + pos[:, None, :]
    flat = blocks.transpose(0, 1, 3, 2, 4).reshape(bsz, n_cmp, g, CMP_BLOCK * dh)
    return (jax.nn.gelu(flat @ w1) @ w2).transpose(0, 2, 1, 3)

def nsa_mixer(h, cos, sin, w_in, w_out, cmp_pos, cmp_w1, cmp_w2):
    bsz, seq, _ = h.shape
    G, R, dh = A_KV_HEADS, A_GROUP, HEAD_DIM
    q, kc, vc, ks, vs, kw, vw, gl = jnp.split(h @ w_in, A_SPLITS, axis=-1)
    q = q.reshape(bsz, seq, A_HEADS, dh)
    kc, vc, ks, vs, kw, vw = (t.reshape(bsz, seq, G, dh) for t in (kc, vc, ks, vs, kw, vw))
    q_rot = apply_partial_rope(q, cos, sin)
    ks = apply_partial_rope(ks, cos, sin)
    kw = apply_partial_rope(kw, cos, sin)
    kc = compress_blocks(kc, cmp_pos[0], cmp_w1[0], cmp_w2[0])
    vc = compress_blocks(vc, cmp_pos[1], cmp_w1[1], cmp_w2[1])
    n_cmp = kc.shape[2]
    n_slc = seq // SLC_BLOCK
    n_sel = min(N_SEL, n_slc)

    def to_heads(t):
        return t.reshape(bsz, seq, G, R, dh).transpose(0, 2, 3, 1, 4)

    def to_blocks(t):
        return t.reshape(bsz, n_slc, SLC_BLOCK, G, dh).transpose(0, 3, 1, 2, 4)

    def to_window(t):
        return jnp.pad(t.transpose(0, 2, 1, 3), ((0, 0), (0, 0), (NSA_WIN, 0), (0, 0)))

    qg, qg_rot = to_heads(q), to_heads(q_rot)
    ks_b, vs_b = to_blocks(ks), to_blocks(vs)
    kw_p, vw_p = to_window(kw), to_window(vw)
    gates = jax.nn.sigmoid(gl.astype(jnp.float32)).reshape(bsz, seq, 3, G, R).transpose(0, 3, 4, 1, 2)
    cmp_end = jnp.arange(n_cmp) * CMP_STRIDE + CMP_BLOCK - 1
    n_idx = jnp.arange(n_cmp)[:, None]
    j_idx = jnp.arange(n_slc)[None, :]
    overlap = (jnp.minimum(n_idx * CMP_STRIDE + CMP_BLOCK, j_idx * SLC_BLOCK + SLC_BLOCK)
               - jnp.maximum(n_idx * CMP_STRIDE, j_idx * SLC_BLOCK))
    cmp_to_slc = jnp.clip(overlap, 0).astype(jnp.float32) / CMP_BLOCK
    jj = jnp.arange(n_slc)
    scale = dh ** -0.5

    def query_block(i):
        q0 = i * Q_BLOCK
        t = q0 + jnp.arange(Q_BLOCK)
        qb = lax.dynamic_slice_in_dim(qg, q0, Q_BLOCK, axis=3)
        qbr = lax.dynamic_slice_in_dim(qg_rot, q0, Q_BLOCK, axis=3)
        gb = lax.dynamic_slice_in_dim(gates, q0, Q_BLOCK, axis=3)
        s_c = jnp.einsum('bgrtd,bgnd->bgrtn', qb, kc).astype(jnp.float32) * scale
        p_c = masked_softmax(s_c, cmp_end[None, :] <= t[:, None])
        o_c = jnp.einsum('bgrtn,bgnd->bgrtd', p_c.astype(vc.dtype), vc)
        imp = jnp.einsum('bgtn,nj->bgtj', p_c.sum(2), cmp_to_slc)
        cur = t // SLC_BLOCK
        forced = (jj[None, :] == 0) | (jj[None, :] == cur[:, None]) | (jj[None, :] == cur[:, None] - 1)
        score = jnp.where(jj[None, :] > cur[:, None], -1.0, jnp.where(forced, FORCE, imp))
        _, idx = lax.top_k(score, n_sel)
        k_sel = gather_blocks(ks_b, idx).reshape(bsz, G, Q_BLOCK, n_sel * SLC_BLOCK, dh)
        v_sel = gather_blocks(vs_b, idx).reshape(bsz, G, Q_BLOCK, n_sel * SLC_BLOCK, dh)
        sel_pos = (idx[..., None] * SLC_BLOCK + jnp.arange(SLC_BLOCK)).reshape(bsz, G, Q_BLOCK, -1)
        m_s = (sel_pos <= t[:, None])[:, :, None]
        s_s = jnp.einsum('bgrtd,bgtkd->bgrtk', qbr, k_sel).astype(jnp.float32) * scale
        p_s = masked_softmax(s_s, m_s)
        o_s = jnp.einsum('bgrtk,bgtkd->bgrtd', p_s.astype(v_sel.dtype), v_sel)
        kwb = lax.dynamic_slice_in_dim(kw_p, q0, Q_BLOCK + NSA_WIN, axis=2)
        vwb = lax.dynamic_slice_in_dim(vw_p, q0, Q_BLOCK + NSA_WIN, axis=2)
        spos = q0 - NSA_WIN + jnp.arange(Q_BLOCK + NSA_WIN)
        diff = t[:, None] - spos[None, :]
        m_w = (diff >= 0) & (diff < NSA_WIN) & (spos[None, :] >= 0)
        s_w = jnp.einsum('bgrtd,bgkd->bgrtk', qbr, kwb).astype(jnp.float32) * scale
        p_w = masked_softmax(s_w, m_w)
        o_w = jnp.einsum('bgrtk,bgkd->bgrtd', p_w.astype(vwb.dtype), vwb)
        o = gb[..., 0:1] * o_c + gb[..., 1:2] * o_s + gb[..., 2:3] * o_w
        return o.astype(h.dtype)

    out = lax.map(query_block, jnp.arange(seq // Q_BLOCK))
    out = out.transpose(1, 0, 4, 2, 3, 5).reshape(bsz, seq, A_Q)
    return out @ w_out

def shared_kv(h, cos, sin, w_kv):
    bsz, seq, _ = h.shape
    nb = seq // SWA_BLOCK
    kv = h @ w_kv
    k = apply_partial_rope(kv[..., :B_KV].reshape(bsz, seq, B_KV_HEADS, HEAD_DIM), cos, sin)
    v = kv[..., B_KV:].reshape(bsz, seq, B_KV_HEADS, HEAD_DIM)

    def band(t):
        tb = t.reshape(bsz, nb, SWA_BLOCK, B_KV_HEADS, HEAD_DIM)
        prev = jnp.concatenate([jnp.zeros_like(tb[:, :1]), tb[:, :-1]], axis=1)
        return jnp.concatenate([prev, tb], axis=2).transpose(1, 0, 2, 3, 4)

    return band(k), band(v)

def swa_sink_mixer(h, cos, sin, k_band, v_band, w_q, w_out, sinks):
    bsz, seq, _ = h.shape
    G, R, dh = B_KV_HEADS, B_GROUP, HEAD_DIM
    nb = seq // SWA_BLOCK
    q = apply_partial_rope((h @ w_q).reshape(bsz, seq, B_HEADS, dh), cos, sin)
    q = q.reshape(bsz, nb, SWA_BLOCK, G, R, dh).transpose(1, 0, 2, 3, 4, 5)
    sink = sinks.astype(jnp.float32).reshape(1, G, R, 1, 1)
    ii = jnp.arange(SWA_BLOCK)[:, None]
    jj = jnp.arange(2 * SWA_BLOCK)[None, :]
    diff = SWA_BLOCK + ii - jj
    band = (diff >= 0) & (diff < SWA_WIN)
    scale = dh ** -0.5

    def block(args):
        qb, kb, vb, n = args
        s = jnp.einsum('bigrd,bjgd->bgrij', qb, kb).astype(jnp.float32) * scale
        mask = band & ((n > 0) | (jj >= SWA_BLOCK))
        s = jnp.where(mask, s, NEG)
        m = jnp.maximum(s.max(-1, keepdims=True), sink)
        e = jnp.exp(s - m)
        p = e / (e.sum(-1, keepdims=True) + jnp.exp(sink - m))
        return jnp.einsum('bgrij,bjgd->bigrd', p.astype(vb.dtype), vb)

    out = lax.map(block, (q, k_band, v_band, jnp.arange(nb)))
    out = out.transpose(1, 0, 2, 3, 4, 5).reshape(bsz, seq, B_Q)
    return out @ w_out

def dense_swiglu(h, w_in, w_out):
    g, u = jnp.split(h @ w_in, 2, axis=-1)
    return (jax.nn.silu(g) * u) @ w_out

def moe_swiglu(h, w_router, w_in, w_out):
    bsz, seq, d = h.shape
    n_tok = bsz * seq
    n_asg = n_tok * TOP_K
    xt = h.reshape(n_tok, d)
    logits = (xt @ w_router).astype(jnp.float32)
    top_logit, top_e = lax.top_k(logits, TOP_K)
    gate = jax.nn.softmax(top_logit, axis=-1)
    e_flat = top_e.reshape(-1)
    tok_flat = jnp.repeat(jnp.arange(n_tok, dtype=jnp.int32), TOP_K)
    order = jnp.argsort(e_flat)
    e_s, tok_s, g_s = e_flat[order], tok_flat[order], gate.reshape(-1)[order]
    counts = jnp.bincount(e_flat, length=N_EXPERTS)
    padded = (counts + MOE_BLOCK - 1) // MOE_BLOCK * MOE_BLOCK
    start = jnp.cumsum(counts) - counts
    pad_end = jnp.cumsum(padded)
    pad_start = pad_end - padded
    dest = pad_start[e_s] + jnp.arange(n_asg) - start[e_s]
    cap = n_asg + N_EXPERTS * MOE_BLOCK
    cap = (cap + MOE_BLOCK - 1) // MOE_BLOCK * MOE_BLOCK
    n_blk = cap // MOE_BLOCK
    buf_tok = jnp.zeros((cap,), jnp.int32).at[dest].set(tok_s)
    buf_w = jnp.zeros((cap,), jnp.float32).at[dest].set(g_s)
    blk_e = jnp.clip(jnp.searchsorted(pad_end, jnp.arange(n_blk) * MOE_BLOCK, side='right'), 0, N_EXPERTS - 1)
    xb = xt[buf_tok].reshape(n_blk, MOE_BLOCK, d)

    def expert_block(args):
        xblk, e = args
        g, u = jnp.split(xblk @ w_in[e], 2, axis=-1)
        return (jax.nn.silu(g) * u) @ w_out[e]

    yb = lax.map(expert_block, (xb, blk_e)).reshape(cap, d)
    yb = (yb.astype(jnp.float32) * buf_w[:, None]).astype(h.dtype)
    out = jnp.zeros((n_tok, d), h.dtype).at[buf_tok].add(yb)
    return out.reshape(bsz, seq, d)

def setup_inputs(seed: int = 0) -> dict:
    key = jax.random.key(seed)
    ks = jax.random.split(key, 20)
    f32 = jnp.float32
    nrm = lambda k, shape, s: jax.random.normal(k, shape, f32) * s
    return {
        "x": nrm(ks[0], (BATCH, SEQ, D_MODEL), 1.0),
        "positions": jnp.arange(SEQ, dtype=jnp.int32)[None, :] + jax.random.randint(ks[1], (BATCH, 1), 0, 4096, dtype=jnp.int32),
        "w_in_a": nrm(ks[2], (N_A_LAYERS, D_MODEL, A_IN), D_MODEL ** -0.5),
        "w_out_a": nrm(ks[3], (N_A_LAYERS, A_Q, D_MODEL), BETA * A_Q ** -0.5),
        "cmp_pos": nrm(ks[4], (N_A_LAYERS, 2, CMP_BLOCK, HEAD_DIM), 0.1),
        "cmp_w1": nrm(ks[5], (N_A_LAYERS, 2, CMP_BLOCK * HEAD_DIM, CMP_HID), (CMP_BLOCK * HEAD_DIM) ** -0.5),
        "cmp_w2": nrm(ks[6], (N_A_LAYERS, 2, CMP_HID, HEAD_DIM), CMP_HID ** -0.5),
        "w_kv_shared": nrm(ks[7], (D_MODEL, 2 * B_KV), D_MODEL ** -0.5),
        "w_q_b": nrm(ks[8], (N_B_LAYERS, D_MODEL, B_Q), D_MODEL ** -0.5),
        "w_out_b": nrm(ks[9], (N_B_LAYERS, B_Q, D_MODEL), BETA * B_Q ** -0.5),
        "sinks_b": nrm(ks[10], (N_B_LAYERS, B_HEADS), 0.5),
        "ln_g": 1.0 + nrm(ks[11], (DEPTH, 2, D_MODEL), 0.02),
        "ln_b": nrm(ks[12], (DEPTH, 2, D_MODEL), 0.02),
        "dense_w_in": nrm(ks[13], (N_DENSE, D_MODEL, 2 * D_FF), D_MODEL ** -0.5),
        "dense_w_out": nrm(ks[14], (N_DENSE, D_FF, D_MODEL), BETA * D_FF ** -0.5),
        "moe_router": nrm(ks[15], (N_MOE, D_MODEL, N_EXPERTS), D_MODEL ** -0.5),
        "moe_w_in": nrm(ks[16], (N_MOE, N_EXPERTS, D_MODEL, 2 * D_FF_EXPERT), D_MODEL ** -0.5),
        "moe_w_out": nrm(ks[17], (N_MOE, N_EXPERTS, D_FF_EXPERT, D_MODEL), BETA * D_FF_EXPERT ** -0.5),
    }

def reference(x, positions, w_in_a, w_out_a, cmp_pos, cmp_w1, cmp_w2, w_kv_shared, w_q_b, w_out_b,
              sinks_b, ln_g, ln_b, dense_w_in, dense_w_out, moe_router, moe_w_in, moe_w_out):
    cos, sin = rope_tables(positions)
    h = x
    k_band = v_band = None
    for l in range(DEPTH):
        if l < N_A_LAYERS:
            mix = nsa_mixer(h, cos, sin, w_in_a[l], w_out_a[l], cmp_pos[l], cmp_w1[l], cmp_w2[l])
        else:
            b = l - N_A_LAYERS
            mix = swa_sink_mixer(h, cos, sin, k_band, v_band, w_q_b[b], w_out_b[b], sinks_b[b])
        h = layer_norm(ALPHA * h + mix, ln_g[l, 0], ln_b[l, 0])
        if l % 2 == 0:
            ffn = dense_swiglu(h, dense_w_in[l // 2], dense_w_out[l // 2])
        else:
            ffn = moe_swiglu(h, moe_router[l // 2], moe_w_in[l // 2], moe_w_out[l // 2])
        h = layer_norm(ALPHA * h + ffn, ln_g[l, 1], ln_b[l, 1])
        if l == N_A_LAYERS - 1:
            k_band, v_band = shared_kv(h, cos, sin, w_kv_shared)
    return h


_drawn_inputs = setup_inputs


def setup_inputs(seed=0):
    import zlib

    import numpy as np

    out = dict(_drawn_inputs(seed))
    spreads = {}
    factors = {'cmp_pos': 3.519, 'sinks_b': 8.0}
    for name, (base, spread) in spreads.items():
        noise = np.random.default_rng([zlib.crc32(name.encode()), seed]).standard_normal(out[name].shape)
        drawn = base * np.exp(spread * noise) if base else spread * noise
        out[name] = __import__('jax').numpy.asarray(drawn.astype(out[name].dtype))
    for name, factor in factors.items():
        out[name] = (out[name] * factor).astype(out[name].dtype)
    return out
```

```python
from contextlib import ExitStack

import concourse.bass as bass
from concourse import mybir
from concourse.bass import ds

F32 = mybir.dt.float32
BF16 = mybir.dt.bfloat16
I32 = mybir.dt.int32
ALU = mybir.AluOpType
ACT = mybir.ActivationFunctionType
X = mybir.AxisListType.X

P = 128
SEQ, D, HD = 256, 1024, 64
NT = SEQ // P
DC = D // P
ROT = HD // 4
ROPE_THETA = 500000.0
A_IN, A_KV = 2608, 256
CMP_STRIDE, CMP_HID = 16, 256
N_CMP = SEQ // CMP_STRIDE - 1
CMP_PAIRS = 16
FF, FFE, NE = 2816, 3584, 8
DENSE_COLS = 256
N_DENSE_IN = FF // DENSE_COLS
N_DENSE_OUT = -(-FF // (4 * P))
FT = FFE // 512
DEPTH = 2
ALPHA = float((2 * DEPTH) ** 0.25)
SCALE = HD ** -0.5
LN_EPS = 1e-5
NEG = -1e30
RING = 7
SLOT = 4096
TWO_PI_PARTS = (6.28125, 1.9350051879882812e-03, 3.0199159819e-07)


def weight_items():
    items = [("in_a", c) for c in (2, 3, 4, 5, 0, 1)]
    items += [("cmp", 0), ("cmp", 1), ("out_a", 0), ("out_a", 1)]
    items += [("dense_in", c) for c in range(N_DENSE_IN)]
    items += [("dense_out", c) for c in range(N_DENSE_OUT)]
    items += [("kv", 0), ("q_b", 0), ("q_b", 1), ("out_b", 0), ("out_b", 1)]
    return items


ITEMS = weight_items()
N_FIRST = len(ITEMS)
EXPERT = []
for _f in range(FT):
    EXPERT += [("g", _f), ("u", _f)]
    if _f >= 2:
        EXPERT.append(("o", _f - 2))
EXPERT += [("o", FT - 2), ("o", FT - 1)]
PER_EXPERT = len(EXPERT)
assert PER_EXPERT % RING == 0


def attention_jobs(branches):
    jobs = []
    for pb in range(2):
        for b in range(2):
            for tt in range(NT):
                mine = []
                for br in branches:
                    if br == "cmp" or tt == 0:
                        mine.append((br, pb, b, tt, 0, 4, P))
                    else:
                        mine += [(br, pb, b, tt, 0, 2, SEQ), (br, pb, b, tt, 2, 2, SEQ)]
                jobs += [(*j, n == 0, n == len(mine) - 1) for n, j in enumerate(mine)]
    return jobs


JOBS_A = attention_jobs(("cmp", "slc", "win"))
JOBS_B = attention_jobs(("swa",))
PROJ_A = [(k, n, tt, w) for n, (k, w) in enumerate(
    [("cmpkv", 512), ("slckv", 512), ("winkv", 512), ("gate", 48), ("q0", 512), ("q1", 512)]) for tt in range(NT)]
PROJ_B = [(k, n, tt, w) for n, (k, w) in enumerate([("kv", 256), ("qb0", 512), ("qb1", 512)]) for tt in range(NT)]
TURNS = {"cmpkv": 2, "slckv": 1, "winkv": 1, "gate": 0, "q0": 2, "q1": 2, "kv": 1, "qb0": 0, "qb1": 2}


def decoder_kernel(nc, x, positions, w_in_a, w_out_a, cmp_pos, cmp_w1, cmp_w2, w_kv_shared, w_q_b, w_out_b,
                   sinks_b, ln_g, ln_b, dense_w_in, dense_w_out, moe_router, moe_w_in, moe_w_out, out):
    ctx = ExitStack()
    with ctx:
        def sb(name, shape, dt=F32):
            return ctx.enter_context(nc.sbuf_tensor(name, shape, dt))

        def sem(name):
            return ctx.enter_context(nc.semaphore(name))

        ring = sb("ring", [P, RING, SLOT])
        h = sb("h", [P, NT, D])
        pre = sb("pre", [P, NT, D])
        hT = sb("hT", [P, DC, SEQ])
        lnp = sb("lnp", [P, 2, D])
        arena = sb("arena", [P, 12544])

        def room(at, *shape):
            n = 1
            for s in shape:
                n *= s
            v = arena[:, at:at + n]
            names = "abcd"[:len(shape)]
            if len(shape) > 1:
                v = v.rearrange(f"p ({' '.join(names)}) -> p {' '.join(names)}", **dict(zip(names[1:], shape[1:])))
            return v

        qT = room(0, 8, SEQ)
        qrT = room(2048, 8, SEQ)
        ksT = room(4096, 2, SEQ)
        kwT = room(4608, 2, SEQ)
        kcT = room(5120, P)
        vs = room(5248, NT, 256)
        vw = room(5760, NT, 256)
        vc = room(6272, P)
        stage = room(6400, 2, 1024)
        kcvT = room(8448, 2, 4, SEQ)
        cmp_in = room(10496, 2, CMP_PAIRS, 64)
        hid = pre[:, 0, 0:512].rearrange("p (v n) -> p v n", v=2)
        hidT = pre[:, 0, 512:1024].rearrange("p (v c n) -> p v c n", v=2, c=2)
        ex = room(8448, 3, 512)
        pT = room(9984, 2, 512)
        actT = room(0, FF // P, SEQ)
        silu = room(5632, 2, 512)
        xgT = room(0, DC, P)
        act = room(1024, 2, 512)
        eactT = room(2048, 2, 4, P)
        esilu = room(3072, 2, 512)
        ysb = room(4096, D)
        pick = room(5120, NT, P)
        put = room(5376, NT, P)
        putT = room(5632, NT, P)

        ident = sb("ident", [P, P])
        identb = sb("identb", [P, P], BF16)
        onesb = sb("onesb", [P, P], BF16)
        earlier = sb("earlier", [P, P], BF16)
        causal = sb("causal", [P, 2, P], BF16)
        window = sb("window", [P, 2, P], BF16)
        cmpmask = sb("cmpmask", [P, NT, 4, P], BF16)
        seen = sb("seen", [P, NT])
        slots = sb("slots", [P, P])
        order = sb("order", [P, NT, NE])
        freq = sb("freq", [P, ROT // 2])
        pos_i = sb("pos_i", [P, NT], I32)
        pos_f = sb("pos_f", [P, NT])
        ang = sb("ang", [P, 3, NT, ROT // 2])
        cc = sb("cc", [P, NT, ROT])
        ss = sb("ss", [P, NT, ROT])
        rot1 = sb("rot1", [P, 8, ROT])
        rot2 = sb("rot2", [P, 8, ROT])
        posr = sb("posr", [16, 2, P])
        posT = sb("posT", [P, 2, 16])
        w2 = sb("w2", [P, 2, 2, 2, HD])
        router = sb("router", [P, DC, NE])
        sink = sb("sink", [P, 16])
        nsink = sb("nsink", [P, 16])
        gates = sb("gates", [P, NT, 48])
        mx = sb("mx", [P, 4, 4])
        nb = sb("nb", [P, 4, 4])
        sn = sb("sn", [P, 4, 4])
        es = sb("es", [P, 4, 4])
        sums = sb("sums", [P, 4, 4])
        rg = sb("rg", [P, 4, 4])
        stats = sb("stats", [P, NT, 2, 6])
        mv = sb("mv", [P, NT, 2])
        std = sb("std", [P, NT, 2])
        lg = sb("lg", [P, 8, NT, NE])
        selb = sb("selb", [P, NT, NE], BF16)
        top = sb("top", [P, 12, NT, 1])
        slotx = sb("slotx", [P, NT, 17])
        gatex = sb("gatex", [P, NT, 17])
        cnt = sb("cnt", [P, 2])
        turns_i = sb("turns_i", [P, 1], I32)

        bank = [ctx.enter_context(nc.psum_tensor(f"bank{i}", [P, 512], F32)) for i in range(8)]

        landed = [sem(f"landed{i}") for i in range(RING)]
        x_landed = sem("x_landed")
        pos_landed = sem("pos_landed")
        small_landed = sem("small_landed")
        ln_landed = sem("ln_landed")
        consts = sem("consts")
        consts_step = sem("consts_step")
        dve_step = sem("dve_step")
        trig_in = sem("trig_in")
        trig = sem("trig")
        turned = sem("turned")
        moved_a = sem("moved_a")
        moved_v = sem("moved_v")
        post = sem("post")
        projected = sem("projected")
        staged_a = sem("staged_a")
        staged_v = sem("staged_v")
        cmp_built = sem("cmp_built")
        cmp_hid = sem("cmp_hid")
        cmp_act = sem("cmp_act")
        cmp_kv = sem("cmp_kv")
        kc_ready = sem("kc_ready")
        vc_ready = sem("vc_ready")
        scored = sem("scored")
        shifted = sem("shifted")
        sink_in = sem("sink_in")
        expd = sem("expd")
        normed = sem("normed")
        summed = sem("summed")
        heads_out = sem("heads_out")
        mixed = sem("mixed")
        added = sem("added")
        var_ready = sem("var_ready")
        std_ready = sem("std_ready")
        h_ready = sem("h_ready")
        gu_ready = sem("gu_ready")
        down_used = sem("down_used")
        silu_ready = sem("silu_ready")
        act_ready = sem("act_ready")
        routed = sem("routed")
        gap_ready = sem("gap_ready")
        gap_exp = sem("gap_exp")
        sel_ready = sem("sel_ready")
        ranked = sem("ranked")
        plan_ready = sem("plan_ready")
        e_pick = sem("e_pick")
        e_put = sem("e_put")
        e_g = sem("e_g")
        e_gu = sem("e_gu")
        e_o = sem("e_o")
        e_silu = sem("e_silu")
        e_act = sem("e_act")
        e_turned = sem("e_turned")
        e_moved_a = sem("e_moved_a")
        e_moved_v = sem("e_moved_v")
        e_putT = sem("e_putT")
        e_putT_moved = sem("e_putT_moved")
        e_rows = sem("e_rows")
        e_rows_a = sem("e_rows_a")
        e_rows_v = sem("e_rows_v")
        e_y = sem("e_y")
        e_y_a = sem("e_y_a")
        e_y_v = sem("e_y_v")
        e_back = sem("e_back")
        e_added = sem("e_added")
        done = sem("done")

        def slot_of(n):
            return n % RING

        def use_of(n):
            return n // RING + 1

        in_a = w_in_a[0].rearrange("(c p) n -> p c n", p=P)
        d_in = dense_w_in[0].rearrange("(c p) n -> p c n", p=P)
        d_out = dense_w_out[0].rearrange("(c p) n -> p c n", p=P)
        q_b = w_q_b[0].rearrange("(c p) n -> p c n", p=P)
        kv_w = w_kv_shared.rearrange("(c p) n -> p c n", p=P)
        e_in = moe_w_in[0].rearrange("e (c p) n -> e p c n", p=P)
        e_out = moe_w_out[0].rearrange("e (c p) n -> e p c n", p=P)
        out_a = w_out_a[0].rearrange("(a b r d) n -> b d a r n", a=2, b=2, r=4, d=HD)
        out_b = w_out_b[0].rearrange("(b r d) n -> b d r n", b=2, r=8, d=HD)

        def item(n, *shape):
            size = 1
            for s in shape:
                size *= s
            return ring[:, slot_of(n), 0:size].rearrange("p (c n) -> p c n", c=shape[0])

        def start_item(sp, n, kind, c):
            sig = landed[slot_of(n)]
            if kind == "in_a":
                w = min(512, A_IN - 512 * c)
                sp.dma_start(item(n, DC, w), in_a[:, :, 512 * c:512 * c + w]).then_inc(sig, 32)
            elif kind == "cmp":
                sp.dma_start(item(n, 16, 256), cmp_w1[0, c].rearrange("(j p) n -> p j n", p=P)).then_inc(sig, 32)
            elif kind in ("out_a", "out_b"):
                for b in range(2):
                    dst = ring[b * HD:(b + 1) * HD, slot_of(n), :].rearrange("p (r n) -> p r n", r=8)
                    cols = slice(512 * c, 512 * c + 512)
                    if kind == "out_a":
                        for a in range(2):
                            sp.dma_start(dst[:, 4 * a:4 * a + 4, :], out_a[b, :, a, :, cols]).then_inc(sig, 16)
                    else:
                        for a in range(2):
                            sp.dma_start(dst[:, 4 * a:4 * a + 4, :], out_b[b, :, 4 * a:4 * a + 4, cols]).then_inc(sig, 16)
            elif kind == "dense_in":
                v = item(n, DC, 512)
                for part in range(2):
                    at = part * FF + DENSE_COLS * c
                    sp.dma_start(v[:, :, part * 256:part * 256 + 256], d_in[:, :, at:at + 256]).then_inc(sig, 16)
            elif kind == "dense_out":
                k = min(4, FF // P - 4 * c)
                sp.dma_start(item(n, k, D), d_out[:, 4 * c:4 * c + k, :]).then_inc(sig, 32)
            elif kind == "kv":
                sp.dma_start(item(n, DC, 256), kv_w).then_inc(sig, 32)
            elif kind == "q_b":
                sp.dma_start(item(n, DC, 512), q_b[:, :, 512 * c:512 * c + 512]).then_inc(sig, 32)

        def weight(kind):
            return 64 if kind in ("out_a", "out_b") else 32

        def landed_value(n):
            return sum(weight(ITEMS[m][0]) for m in range(n + 1) if slot_of(m) == slot_of(n))

        BEFORE = [sum(weight(ITEMS[m][0]) for m in range(N_FIRST) if slot_of(m) == s) for s in range(RING)]

        def expert_slot(k):
            return slot_of(N_FIRST + k)

        def expert_landed(i, k):
            s = expert_slot(k)
            nth = sum(1 for j in range(k + 1) if expert_slot(j) == s)
            return BEFORE[s] + 16 * nth + 16 * (PER_EXPERT // RING) * i

        AT = {}
        for n, (kind, c) in enumerate(ITEMS):
            AT.setdefault(kind, n)

        def moved(eng, n):
            if n >= 0:
                eng.wait_ge(moved_v if n % 2 else moved_a, n // 2 + 1)

        T_X = 0
        T_A = T_X + 4
        first_a = [T_A + sum(TURNS[p[0]] for p in PROJ_A[:j]) for j in range(len(PROJ_A) + 1)]
        T_HID = first_a[-1]
        T_JA = T_HID + 1
        T_H1 = T_JA + len(JOBS_A)
        T_H2 = T_H1 + 4
        T_B = T_H2 + 4
        first_b = [T_B + sum(TURNS[p[0]] for p in PROJ_B[:j]) for j in range(len(PROJ_B) + 1)]
        T_JB = first_b[-1]
        T_H3 = T_JB + len(JOBS_B)
        T_END = T_H3 + 4

        def item_free(sp, n):
            kind, c = ITEMS[n]
            nth = n - AT[kind]
            if kind == "in_a":
                sp.wait_ge(projected, NT * (nth + 1))
            elif kind in ("kv", "q_b"):
                sp.wait_ge(projected, len(PROJ_A) + NT * (n - AT["kv"] + 1))
            elif kind == "cmp":
                sp.wait_ge(cmp_hid, c + 1)
            elif kind == "out_a":
                sp.wait_ge(mixed, NT * (c + 1))
            elif kind == "out_b":
                sp.wait_ge(mixed, 8 + NT * (c + 1))
            elif kind == "dense_in":
                sp.wait_ge(gu_ready, c + 1)
            elif c < N_DENSE_OUT - 1:
                sp.wait_ge(down_used, c + 1)
            else:
                sp.wait_ge(mixed, 8)

        def expert_free(sp, i, k):
            kind, f = EXPERT[k]
            if kind == "g":
                sp.wait_ge(e_g, i * FT + f + 1)
            elif kind == "u":
                sp.wait_ge(e_gu, i * FT + f + 1)
            elif f < FT - 1:
                sp.wait_ge(e_o, i * (FT - 1) + f + 1)
            else:
                sp.wait_ge(e_y, i + 1)

        block = ctx.enter_context(nc.Block())

        @block.sync
        def _(sp):
            for n, (kind, c) in enumerate(ITEMS):
                if n >= RING:
                    item_free(sp, n - RING)
                start_item(sp, n, kind, c)

            def expert_item(i, k, expert, peeled=False):
                kind, f = EXPERT[k]
                if k >= RING:
                    expert_free(sp, i, k - RING)
                elif peeled:
                    item_free(sp, N_FIRST + k - RING)
                else:
                    expert_free(sp, i - 1, k - RING + PER_EXPERT)
                s = expert_slot(k)
                if kind == "o":
                    src = e_out[ds(expert, 1), :, 4 * f:4 * f + 4, :].rearrange("e p c n -> (e p) c n")
                    dst = ring[:, s, :].rearrange("p (c n) -> p c n", c=4)
                else:
                    at = (kind == "u") * FFE + 512 * f
                    src = e_in[ds(expert, 1), :, :, at:at + 512].rearrange("e p c n -> (e p) c n")
                    dst = ring[:, s, :].rearrange("p (c n) -> p c n", c=DC)
                sp.dma_start(dst, src).then_inc(landed[s], 16)

            for k in range(PER_EXPERT):
                if k == RING:
                    sp.wait_ge(plan_ready, 1)
                    steps = sp.value_load(turns_i[0:1, 0:1], min_val=NE, max_val=2 * NE)
                expert_item(0, k, 0, True)
            with sp.Fori(1, steps) as i:
                for k in range(PER_EXPERT):
                    expert_item(i, k, i % NE)
            sp.wait_ge(h_ready, 4 * NT)
            sp.dma_start(out[0].rearrange("(t p) d -> p t d", p=P), h[:, :, :]).then_inc(done, 16)
            sp.wait_ge(done, 16)

        @block.gpsimd
        def _(pool):
            n = [0]

            def step(ins):
                n[0] += 1
                ins.then_inc(consts_step, 1)
                pool.wait_ge(consts_step, n[0])

            step(pool.memset(ident[:, :], 0.0))
            step(pool.affine_select(out=ident[:, :], in_=ident[:, :], compare_op=ALU.not_equal, fill=1.0, base=0,
                                    pattern=[[-1, P]], channel_multiplier=1))
            step(pool.tensor_copy(identb[:, :], ident[:, :]))
            for j in range(ROT // 2):
                step(pool.memset(freq[:, j:j + 1], float(ROPE_THETA ** (-2.0 * j / ROT))))
            step(pool.memset(causal[:, :, :], 0.0))
            step(pool.memset(window[:, :, :], 0.0))
            for m in (causal, window):
                step(pool.affine_select(out=m[:, 1, :], in_=m[:, 1, :], compare_op=ALU.is_ge, fill=NEG, base=0,
                                        pattern=[[-1, P]], channel_multiplier=1))
            step(pool.affine_select(out=window[:, 0, :], in_=window[:, 0, :], compare_op=ALU.is_ge, fill=NEG, base=-1,
                                    pattern=[[1, P]], channel_multiplier=-1))
            step(pool.memset(cmpmask[:, :, :, :], NEG))
            for tt in range(NT):
                for g in range(4):
                    part = cmpmask[:, tt, g, 16 * g:16 * g + 16]
                    step(pool.memset(part, 0.0))
                    step(pool.affine_select(out=part, in_=part, compare_op=ALU.is_ge, fill=NEG,
                                            base=P * tt - (2 * CMP_STRIDE - 1), pattern=[[-CMP_STRIDE, 16]],
                                            channel_multiplier=1))
            step(pool.memset(seen[:, :], 1.0))
            step(pool.affine_select(out=seen[:, 0:1], in_=seen[:, 0:1], compare_op=ALU.is_ge, fill=0.0,
                                    base=-(2 * CMP_STRIDE - 1), pattern=[[0, 1]], channel_multiplier=1))
            step(pool.memset(onesb[:, :], 1.0))
            step(pool.affine_select(out=earlier[:, :], in_=onesb[:, :], compare_op=ALU.is_ge, fill=0.0, base=-1,
                                    pattern=[[1, P]], channel_multiplier=-1))
            step(pool.iota(slots[:, :], [[1, P]], base=0, channel_multiplier=0, allow_small_or_imprecise_dtypes=True))
            step(pool.iota(order[:, :, :], [[0, NT], [-1, NE]], base=NE, channel_multiplier=0,
                           allow_small_or_imprecise_dtypes=True))
            step(pool.memset(cmp_in[:, :, :, :], 0.0))
            pool.memset(slotx[:, :, 16:17], -1.0).then_inc(consts, 1)
            pool.memset(gatex[:, :, 16:17], 0.0).then_inc(consts, 1)

        @block.scalar
        def _(act_e):
            act_e.dma_start(h[:, :, :], x[0].rearrange("(t p) d -> p t d", p=P)).then_inc(x_landed, 16)
            act_e.dma_start(pos_i[:, :], positions[0].rearrange("(t p) -> p t", p=P),
                            allow_slow_non_contiguous=True).then_inc(pos_landed, 16)
            act_e.dma_start(posr[:, :, :], cmp_pos[0].rearrange("v (j a) d -> j v (a d)", a=2)).then_inc(small_landed, 16)
            for kv in range(2):
                for twice in range(2):
                    act_e.dma_start(w2[:, kv, :, twice, :], cmp_w2[0, kv].rearrange("(c p) d -> p c d", p=P))\
                         .then_inc(small_landed, 16)
            act_e.dma_start(router[:, :, :], moe_router[0].rearrange("(c p) e -> p c e", p=P),
                            allow_slow_non_contiguous=True).then_inc(small_landed, 16)
            act_e.dma_start(sink[:, :], sinks_b[0:1, :].to_broadcast([P, 16])).then_inc(small_landed, 16)

            def load_norm(k):
                for part, src in enumerate((ln_g, ln_b)):
                    act_e.dma_start(lnp[:, part, :], src[k // 2, k % 2:k % 2 + 1, :].to_broadcast([P, D]))\
                         .then_inc(ln_landed, 16)

            load_norm(0)
            act_e.wait_ge(trig_in, 1)
            act_e.activation(ss[:, :, 0:8], ang[:, 1, :, :], ACT.Sin).then_inc(trig, 1)
            act_e.activation(cc[:, :, 0:8], ang[:, 2, :, :], ACT.Sin).then_inc(trig, 1)

            def copy_turned(n, dst):
                act_e.wait_ge(turned, n + 1)
                act_e.activation(dst, bank[4 + n % 2][:, :].rearrange("p (c n) -> p c n", c=dst.shape[1])
                                 if len(dst.shape) == 3 else bank[4 + n % 2][:, 0:dst.shape[1]], ACT.Copy)\
                     .then_inc(moved_a, 1)

            def turn_h(first):
                for n in range(first % 2, 4, 2):
                    tt, q = n // 2, n % 2
                    copy_turned(first + n, hT[:, 4 * q:4 * q + 4, tt * P:tt * P + P])

            turn_h(T_X)

            def stage_part(j, proj, base, nturn):
                kind, _, tt, w = proj[j]
                act_e.wait_ge(projected, base + j + 1)
                src = bank[j % 4]
                s = stage[:, j % 2, :]
                if j >= 2:
                    act_e.wait_ge(turned, nturn[j - 1])
                if kind == "cmpkv":
                    act_e.activation(s.rearrange("p (g a d) -> p g a d", g=8, a=2)[:, :, 0, :],
                                     src[:, :].rearrange("p (g d) -> p g d", g=8), ACT.Copy).then_inc(staged_a, 1)
                elif kind in ("slckv", "winkv", "kv"):
                    nk = w // 2
                    v = vw if kind == "winkv" else vs
                    act_e.activation(v[:, tt, 0:nk], src[:, nk:w], ACT.Copy)
                    act_e.activation(s[:, 0:nk].rearrange("p (g d) -> p g d", d=HD)[:, :, ROT:],
                                     src[:, 0:nk].rearrange("p (g d) -> p g d", d=HD)[:, :, ROT:], ACT.Copy)\
                         .then_inc(staged_a, 1)
                elif kind == "gate":
                    act_e.activation(gates[:, tt, :], src[:, 0:48], ACT.Sigmoid).then_inc(staged_a, 1)
                elif kind in ("q0", "q1"):
                    act_e.activation(s[:, 0:512].rearrange("p (r b d) -> p b r d", r=4, b=2),
                                     src[:, :].rearrange("p (b r d) -> p b r d", b=2, r=4), ACT.Copy)\
                         .then_inc(staged_a, 1)
                else:
                    b = int(kind[-1])
                    act_e.activation(s.rearrange("p (r b d) -> p b r d", r=8, b=2)[:, b, :, ROT:],
                                     src[:, :].rearrange("p (r d) -> p r d", r=8)[:, :, ROT:], ACT.Copy)\
                         .then_inc(staged_a, 1)

            def take_turned(j, proj, first):
                for t, n in enumerate(range(first[j], first[j + 1])):
                    if n % 2 == 0:
                        copy_projection(act_e, n, proj[j], t)

            def copy_projection(eng, n, p, t):
                kind, _, tt, _ = p
                eng.wait_ge(turned, n + 1)
                src = bank[4 + n % 2]
                cols = slice(tt * P, tt * P + P)
                if kind == "cmpkv":
                    act_e.activation(kcvT[0:64, t, :, cols], src[0:64, :].rearrange("p (g n) -> p g n", g=4), ACT.Copy)
                    lo = 1 if tt == 0 else 0
                    act_e.activation(kcvT[64:128, t, :, tt * P + lo - 1:tt * P + P - 1],
                                     src[64:128, :].rearrange("p (g n) -> p g n", g=4)[:, :, lo:], ACT.Copy)\
                         .then_inc(moved_a, 1)
                elif kind in ("slckv", "winkv"):
                    act_e.activation((ksT if kind == "slckv" else kwT)[:, :, cols],
                                     src[:, 0:256].rearrange("p (g n) -> p g n", g=2), ACT.Copy).then_inc(moved_a, 1)
                elif kind in ("q0", "q1"):
                    pb = int(kind[-1])
                    act_e.activation((qrT if t else qT)[:, 4 * pb:4 * pb + 4, cols],
                                     src[:, :].rearrange("p (g n) -> p g n", g=4), ACT.Copy).then_inc(moved_a, 1)
                elif kind == "kv":
                    act_e.activation(ksT[:, 0, cols], src[:, 0:P], ACT.Copy).then_inc(moved_a, 1)
                else:
                    act_e.activation(qrT[:, 4 * t:4 * t + 4, cols],
                                     src[:, :].rearrange("p (g n) -> p g n", g=4), ACT.Copy).then_inc(moved_a, 1)

            for j in range(len(PROJ_A) + 1):
                if j < len(PROJ_A):
                    stage_part(j, PROJ_A, 0, first_a)
                if j >= 1:
                    take_turned(j - 1, PROJ_A, first_a)

            act_e.wait_ge(cmp_hid, 2)
            act_e.activation(hid[0:64, :, :].rearrange("p a b -> p (a b)"), bank[6][0:64, :], ACT.Gelu_apprx_tanh)\
                 .then_inc(cmp_act, 1)
            if T_HID % 2 == 0:
                act_e.wait_ge(turned, T_HID + 1)
                for twice in range(2):
                    ins = act_e.activation(hidT.rearrange("p a c n -> p (a c) n")[:, :, 64 * twice:64 * twice + 64],
                                           bank[4][:, 0:256].rearrange("p (g n) -> p g n", g=4), ACT.Copy)
                ins.then_inc(moved_a, 1)
            act_e.wait_ge(cmp_kv, 1)
            act_e.activation(kcT, bank[7][:, 0:P], ACT.Copy).then_inc(kc_ready, 1)

            def attention(jobs, base, first, acc_base, swa):
                accs = acc_base
                for i in range(len(jobs) + 4):
                    if i < len(jobs):
                        _, pb, b, tt, h0, nh, w, _, _ = jobs[i]
                        act_e.wait_ge(shifted, base + i + 1)
                        if i >= 3:
                            act_e.wait_ge(turned, first + i - 2)
                        for k in range(nh):
                            ins = act_e.activation(ex[:, i % 3, k * w:k * w + w], bank[i % 4][:, k * w:k * w + w],
                                                   ACT.Exp, bias=nb[:, i % 4, k:k + 1], scale=SCALE,
                                                   accum_out=sums[:, i % 4, k:k + 1])
                        if swa:
                            ins = act_e.activation(es[:, i % 4, 0:nh], sn[:, i % 4, 0:nh], ACT.Exp)
                        ins.then_inc(expd, 1)
                    if 2 <= i < len(jobs) + 2 and (first + i - 2) % 2 == 0:
                        n = first + i - 2
                        act_e.wait_ge(turned, n + 1)
                        if i >= 4:
                            act_e.wait_ge(summed, base + i - 3)
                        act_e.activation(pT[:, n % 2, :], bank[4 + n % 2][:, :], ACT.Copy).then_inc(moved_a, 1)
                    if i >= 4:
                        _, pb, b, tt, _, _, _, _, closes = jobs[i - 4]
                        if closes:
                            act_e.wait_ge(summed, base + i - 3)
                            act_e.activation(hT[b * 64:b * 64 + 64, 4 * pb:4 * pb + 4, tt * P:tt * P + P],
                                             bank[6 + accs % 2][b * 64:b * 64 + 64, :].rearrange("p (r n) -> p r n", r=4),
                                             ACT.Copy).then_inc(heads_out, 1)
                            accs += 1

            def norm_part(k):
                for tt in range(NT):
                    act_e.wait_ge(var_ready, NT * k + tt + 1)
                    act_e.activation(std[:, tt, 0:1], std[:, tt, 1:2], ACT.Sqrt).then_inc(std_ready, 1)
                if k < 3:
                    act_e.wait_ge(h_ready, NT * (k + 1))
                    load_norm(k + 1)

            attention(JOBS_A, 0, T_JA, 0, False)
            norm_part(0)
            turn_h(T_H1)
            for c in range(N_DENSE_IN):
                act_e.wait_ge(gu_ready, c + 1)
                if c >= 2:
                    act_e.wait_ge(act_ready, c - 1)
                act_e.activation(silu[:, c % 2, :], bank[2 * (c % 2)][:, :], ACT.Silu).then_inc(silu_ready, 1)
            norm_part(1)
            turn_h(T_H2)
            for j in range(len(PROJ_B) + 1):
                if j < len(PROJ_B):
                    stage_part(j, PROJ_B, len(PROJ_A), first_b)
                if j >= 1:
                    for t, n in enumerate(range(first_b[j - 1], first_b[j])):
                        if n % 2 == 0:
                            copy_projection(act_e, n, PROJ_B[j - 1], t)
            attention(JOBS_B, len(JOBS_A), T_JB, 8, True)
            norm_part(2)
            turn_h(T_H3)
            act_e.wait_ge(gap_ready, 1)
            act_e.activation(top[:, 5, :, :], top[:, 4, :, :], ACT.Exp).then_inc(gap_exp, 1)

            def take_rows(value):
                act_e.wait_ge(e_rows, value)
                act_e.activation(xgT[:, 0:4, :], bank[2][:, :].rearrange("p (c n) -> p c n", c=4), ACT.Copy)\
                     .then_inc(e_rows_a, 1)

            act_e.wait_ge(plan_ready, 1)
            steps = act_e.value_load(turns_i[0:1, 0:1], min_val=NE, max_val=2 * NE)
            act_e.memzero(ysb[:, 0:512]).then_inc(e_y_a, 1)
            take_rows(1)
            with act_e.Fori(0, steps) as i:
                for f in range(FT + 1):
                    if f < FT:
                        act_e.wait_ge(e_gu, i * FT + f + 1)
                        act_e.wait_ge(e_act, i * FT + max(f - 1, 0) + 1)
                        act_e.activation(esilu[:, f % 2, :], bank[2 * (f % 2)][:, :], ACT.Silu).then_inc(e_silu, 1)
                    if f >= 1 and (f - 1) % 2 == 0:
                        act_e.wait_ge(e_turned, i * FT + f + 1)
                        act_e.activation(eactT[:, 0, :, :], bank[4][:, :].rearrange("p (c n) -> p c n", c=4), ACT.Copy)\
                             .then_inc(e_moved_a, 1)
                take_rows(i + 2)
                act_e.wait_ge(e_y, i + 1)
                act_e.activation(ysb[:, 0:512], bank[6][:, :], ACT.Copy).then_inc(e_y_a, 1)
            for tt in range(NT):
                act_e.wait_ge(var_ready, NT * 3 + tt + 1)
                act_e.activation(std[:, tt, 0:1], std[:, tt, 1:2], ACT.Sqrt).then_inc(std_ready, 1)

        @block.tensor
        def _(pe):
            def arrived(n):
                pe.wait_ge(landed[slot_of(n)], landed_value(n))

            def turn(n, sources):
                moved(pe, n - 2)
                b = bank[4 + n % 2]
                at = 0
                for src in sources:
                    rows, cols = src.shape[0], 1
                    ins = pe.transpose(b[:, at:at + rows], src, ident[0:rows, 0:rows])
                    at += rows
                ins.then_inc(turned, 1)

            def turn_h(first):
                for n in range(4):
                    tt, q = n // 2, n % 2
                    turn(first + n, [h[:, tt, (4 * q + c) * P:(4 * q + c + 1) * P] for c in range(4)])

            pe.wait_ge(consts, 2)
            pe.wait_ge(small_landed, 16 * 7)
            for kv in range(2):
                ins = pe.transpose(bank[7][:, 16 * kv:16 * kv + 16], posr[:, kv, :], ident[0:16, 0:16])
            ins.then_inc(post, 1)
            pe.wait_ge(x_landed, 16)
            turn_h(T_X)
            moved(pe, T_X + 2)
            moved(pe, T_X + 3)

            def project(j, proj, base, stage_item):
                kind, nth, tt, w = proj[j]
                n = stage_item + nth
                arrived(n)
                if base + j >= 4:
                    pe.wait_ge(staged_a, base + j - 3)
                    pe.wait_ge(staged_v, base + j - 3)
                wt = item(n, DC, w)
                for c in range(DC):
                    ins = pe.matmul(bank[j % 4][:, 0:w], hT[:, c, tt * P:tt * P + P], wt[:, c, :],
                                    start=(c == 0), stop=(c == DC - 1))
                ins.then_inc(projected, 1)

            def turn_projection(j, proj, base, first):
                kind, _, tt, w = proj[j]
                pe.wait_ge(staged_a, base + j + 1)
                pe.wait_ge(staged_v, base + j + 1)
                s = stage[:, j % 2, :]
                if kind == "cmpkv":
                    for kv in range(2):
                        turn(first[j] + kv, [s[:, (4 * kv + g) * P:(4 * kv + g + 1) * P] for g in range(4)])
                elif kind in ("slckv", "winkv"):
                    turn(first[j], [s[:, g * P:(g + 1) * P] for g in range(2)])
                elif kind in ("q0", "q1"):
                    for t in range(2):
                        turn(first[j] + t, [s[:, 512 * t + r * P:512 * t + (r + 1) * P] for r in range(4)])
                elif kind == "kv":
                    turn(first[j], [s[:, 0:P]])
                elif kind == "qb1":
                    for t in range(2):
                        turn(first[j] + t, [s[:, (4 * t + r) * P:(4 * t + r + 1) * P] for r in range(4)])

            def projections(proj, base, stage_item, first):
                for j in range(len(proj) + 1):
                    if j < len(proj):
                        project(j, proj, base, stage_item)
                    if j >= 1:
                        turn_projection(j - 1, proj, base, first)

            projections(PROJ_A, 0, AT["in_a"], first_a)

            for kv in range(2):
                pe.wait_ge(cmp_built, kv + 1)
                n = AT["cmp"] + kv
                arrived(n)
                for j in range(CMP_PAIRS):
                    ins = pe.matmul(bank[6][0:64, 256 * kv:256 * kv + 256], cmp_in[:, kv, j, :],
                                    item(n, 16, 256)[:, j, :], start=(j == 0), stop=(j == CMP_PAIRS - 1))
                ins.then_inc(cmp_hid, 1)
            pe.wait_ge(cmp_act, 1)
            turn(T_HID, [hid[0:64, kv, c * P:c * P + P] for kv in range(2) for c in range(2)])
            moved(pe, T_HID)
            for c in range(2):
                pe.matmul(bank[7][:, 0:P], w2[:, 0, c, :, :].rearrange("p a d -> p (a d)"), hidT[:, 0, c, :],
                          start=(c == 0), stop=(c == 1))
            for c in range(2):
                ins = pe.matmul(bank[7][:, P:2 * P], hidT[:, 1, c, :], w2[:, 1, c, :, :].rearrange("p a d -> p (a d)"),
                                start=(c == 0), stop=(c == 1))
            ins.then_inc(cmp_kv, 1)

            def attention(jobs, base, first, acc_base):
                accs = acc_base
                for i in range(len(jobs) + 3):
                    if i < len(jobs):
                        br, pb, b, tt, h0, nh, w, _, _ = jobs[i]
                        if base + i >= 4:
                            pe.wait_ge(expd, base + i - 3)
                        sc = bank[i % 4]
                        if br == "cmp":
                            mask = cmpmask[:, tt, 2 * pb + b, :]
                        else:
                            m = window if br == "swa" else causal
                            mask = m[:, 1, :] if tt == 0 else m[:, :, :].rearrange("p a n -> p (a n)")
                        mask = mask.rearrange("p (a n) -> p a n", a=1).to_broadcast([P, nh, w])
                        pe.matmul(sc[:, :], identb[:, :], mask, start=True, stop=False, skip_group_check=True)
                        q = qT if br == "cmp" else qrT
                        half = slice(64 * b, 64 * b + 64)
                        keys = {"cmp": kcT[half, :], "slc": ksT[half, pb, 0:w], "win": kwT[half, pb, 0:w],
                                "swa": ksT[half, 0, 0:w]}[br]
                        for k in range(nh):
                            ins = pe.matmul(sc[:, k * w:k * w + w], q[half, 4 * pb + h0 + k, tt * P:tt * P + P], keys,
                                            start=False, stop=(k == nh - 1), skip_group_check=True)
                        ins.then_inc(scored, 1)
                    if 2 <= i < len(jobs) + 2:
                        pe.wait_ge(normed, base + i - 1)
                        turn(first + i - 2, [ex[:, (i - 2) % 3, c * P:c * P + P] for c in range(4)])
                    if i >= 3:
                        br, pb, b, tt, h0, nh, w, opens, closes = jobs[i - 3]
                        n = first + i - 3
                        moved(pe, n)
                        if opens and accs >= 2:
                            pe.wait_ge(heads_out, accs - 1)
                        acc = bank[6 + accs % 2]
                        v = {"cmp": vc, "slc": vs, "win": vw, "swa": vs}[br]
                        cols = slice(0, P) if br in ("cmp", "swa") else slice(P * pb, P * pb + P)
                        if w == P:
                            lhs = v if br == "cmp" else v[:, 0, cols]
                            ins = pe.matmul(acc[:, :], lhs, pT[:, n % 2, :], start=opens, stop=closes,
                                            skip_group_check=True)
                        else:
                            p4 = pT[:, n % 2, :].rearrange("p (k c n) -> p c k n", k=2, c=2)
                            for c in range(2):
                                ins = pe.matmul(acc[:, h0 * P:h0 * P + 2 * P], v[:, c, cols], p4[:, c, :, :],
                                                start=(opens and c == 0), stop=(closes and c == 1),
                                                skip_group_check=True)
                        ins.then_inc(summed, 1)
                        accs += closes

            def mix_out(n0, heads, mixes):
                pe.wait_ge(heads_out, heads)
                for half in range(2):
                    arrived(n0 + half)
                    for tt in range(NT):
                        for r in range(DC):
                            ins = pe.matmul(bank[2 * half + tt][:, :], hT[:, r, tt * P:tt * P + P],
                                            item(n0 + half, 8, 512)[:, r, :], start=(r == 0), stop=(r == DC - 1))
                        ins.then_inc(mixed, 1)

            def next_h(k, first):
                pe.wait_ge(h_ready, NT * (k + 1))
                turn_h(first)
                moved(pe, first + 2)
                moved(pe, first + 3)

            pe.wait_ge(kc_ready, 1)
            pe.wait_ge(vc_ready, 1)
            attention(JOBS_A, 0, T_JA, 0)
            mix_out(AT["out_a"], 8, 0)
            next_h(0, T_H1)

            for c in range(N_DENSE_IN):
                n = AT["dense_in"] + c
                arrived(n)
                if c >= 2:
                    pe.wait_ge(act_ready, c - 1)
                w = item(n, DC, 512)
                for part in range(2):
                    for j in range(2):
                        for k in range(DC):
                            ins = pe.matmul(bank[2 * (c % 2) + part][:, 256 * j:256 * j + 256],
                                            w[:, k, 256 * part + P * j:256 * part + P * j + P], hT[:, k, :],
                                            start=(k == 0), stop=(k == DC - 1))
                ins.then_inc(gu_ready, 1)
            pe.wait_ge(act_ready, N_DENSE_IN)
            nfc = FF // P
            for c in range(N_DENSE_OUT):
                n = AT["dense_out"] + c
                arrived(n)
                k = min(4, nfc - 4 * c)
                for j in range(k):
                    fc = 4 * c + j
                    for half in range(2):
                        for tt in range(NT):
                            ins = pe.matmul(bank[4 + 2 * half + tt][:, :], actT[:, fc, tt * P:tt * P + P],
                                            item(n, k, D)[:, j, 512 * half:512 * half + 512],
                                            start=(fc == 0), stop=(fc == nfc - 1))
                            if fc == nfc - 1:
                                ins.then_inc(mixed, 1)
                if c < N_DENSE_OUT - 1:
                    ins.then_inc(down_used, 1)
            next_h(1, T_H2)

            projections(PROJ_B, len(PROJ_A), AT["kv"], first_b)
            moved(pe, T_JB - 1)
            moved(pe, T_JB - 2)
            attention(JOBS_B, len(JOBS_A), T_JB, 8)
            mix_out(AT["out_b"], 16, 8)
            next_h(2, T_H3)

            for tt in range(NT):
                for c in range(DC):
                    ins = pe.matmul(bank[6][:, NE * tt:NE * tt + NE], hT[:, c, tt * P:tt * P + P], router[:, c, :],
                                    start=(c == 0), stop=(c == DC - 1))
            ins.then_inc(routed, 1)
            pe.wait_ge(sel_ready, 1)
            pe.matmul(bank[7][:, 0:NE], earlier[:, :], selb[:, 0, :], start=True, stop=True)
            pe.matmul(bank[7][:, NE:2 * NE], onesb[:, :], selb[:, 0, :], start=True, stop=False)
            pe.matmul(bank[7][:, NE:2 * NE], earlier[:, :], selb[:, 1, :], start=False, stop=True)
            pe.matmul(bank[7][:, 2 * NE:3 * NE], onesb[:, :], selb[:, 0, :], start=True, stop=False)
            pe.matmul(bank[7][:, 2 * NE:3 * NE], onesb[:, :], selb[:, 1, :], start=False, stop=True)\
              .then_inc(ranked, 1)

            def gather(value):
                pe.wait_ge(e_pick, value)
                for c in range(DC):
                    for tt in range(NT):
                        ins = pe.matmul(bank[2 + c // 4][:, (c % 4) * P:(c % 4) * P + P], h[:, tt, c * P:c * P + P],
                                        pick[:, tt, :], start=(tt == 0), stop=(tt == NT - 1))
                ins.then_inc(e_rows, 1)

            def scatter(i):
                pe.wait_ge(e_putT_moved, i)
                pe.wait_ge(e_y_a, i)
                pe.wait_ge(e_y_v, i)
                for n in range(4):
                    tt, half = n // 2, n % 2
                    if n >= 2:
                        pe.wait_ge(e_added, 4 * i + n - 4)
                    pe.matmul(bank[4 + n % 2][:, :], putT[:, tt, :], ysb[:, 512 * half:512 * half + 512],
                              start=True, stop=True).then_inc(e_back, 1)

            pe.wait_ge(plan_ready, 1)
            steps = pe.value_load(turns_i[0:1, 0:1], min_val=NE, max_val=2 * NE)
            pe.sem_inc(e_turned, 1)
            pe.sem_inc(e_putT, 1)
            gather(1)
            with pe.Fori(0, steps) as i:
                for f in range(FT + 2):
                    if f < FT:
                        if f == 0:
                            pe.wait_ge(e_rows_a, i + 1)
                            pe.wait_ge(e_rows_v, i + 1)
                        pe.wait_ge(e_act, i * FT + max(f - 1, 0) + 1)
                        for part, kind in enumerate("gu"):
                            k = EXPERT.index((kind, f))
                            s = expert_slot(k)
                            pe.wait_ge(landed[s], expert_landed(i, k))
                            w = ring[:, s, :].rearrange("p (c n) -> p c n", c=DC)
                            for c in range(DC):
                                ins = pe.matmul(bank[2 * (f % 2) + part][:, :], xgT[:, c, :], w[:, c, :],
                                                start=(c == 0), stop=(c == DC - 1))
                            ins.then_inc(e_g if part == 0 else e_gu, 1)
                    if f == 0:
                        scatter(i + 1)
                    if f >= 2:
                        k = EXPERT.index(("o", f - 2))
                        s = expert_slot(k)
                        pe.wait_ge(landed[s], expert_landed(i, k))
                        if f % 2 == 0:
                            pe.wait_ge(e_moved_a, i * ((FT + 1) // 2) + (f - 2) // 2 + 1)
                        else:
                            pe.wait_ge(e_moved_v, i * (FT // 2) + (f - 3) // 2 + 1)
                        w = ring[:, s, :].rearrange("p (c n) -> p c n", c=4)
                        for j in range(4):
                            for half in range(2):
                                ins = pe.matmul(bank[6 + half][:, :], eactT[:, f % 2, j, :],
                                                w[:, j, 512 * half:512 * half + 512],
                                                start=(f == 2 and j == 0), stop=(f == FT + 1 and j == 3))
                        ins.then_inc(e_o if f - 2 < FT - 1 else e_y, 1)
                    if 1 <= f <= FT:
                        pe.wait_ge(e_act, i * FT + f + 1)
                        if f <= 2:
                            pe.wait_ge(e_added, 4 * i + 3 + f)
                        if f == 2:
                            pe.wait_ge(e_putT_moved, i + 1)
                        if f >= 3:
                            if f % 2:
                                pe.wait_ge(e_moved_a, i * ((FT + 1) // 2) + (f - 3) // 2 + 1)
                            else:
                                pe.wait_ge(e_moved_v, i * (FT // 2) + (f - 4) // 2 + 1)
                        for j in range(4):
                            ins = pe.transpose(bank[4 + (f - 1) % 2][:, j * P:j * P + P],
                                               act[:, (f - 1) % 2, j * P:j * P + P], ident[:, :])
                        ins.then_inc(e_turned, 1)
                    if f == FT:
                        pe.wait_ge(e_put, i + 1)
                        pe.wait_ge(e_moved_v, (i + 1) * (FT // 2))
                        for tt in range(NT):
                            ins = pe.transpose(bank[5][:, tt * P:tt * P + P], put[:, tt, :], ident[:, :])
                        ins.then_inc(e_putT, 1)
                        gather(i + 2)
            scatter(steps + 1)

        @block.vector
        def _(dve):
            n_step = [0]

            def step(ins):
                n_step[0] += 1
                ins.then_inc(dve_step, 1)
                dve.wait_ge(dve_step, n_step[0])

            dve.wait_ge(pos_landed, 16)
            dve.wait_ge(consts, 2)
            step(dve.tensor_copy(pos_f[:, :], pos_i[:, :]))
            for tt in range(NT):
                step(dve.tensor_scalar(ang[:, 0, tt, :], freq[:, :], pos_f[:, tt:tt + 1], None, ALU.mult))
            a, turns, r = ang[:, 0, :, :], ang[:, 1, :, :], ang[:, 2, :, :]
            step(dve.tensor_scalar(turns, a, 0.15915494309189535, 12582912.0, ALU.mult, ALU.add))
            step(dve.tensor_scalar(turns, turns, 12582912.0, None, ALU.subtract))
            for part in TWO_PI_PARTS:
                step(dve.scalar_tensor_tensor(out=a, in0=turns, scalar=-part, in1=a, op0=ALU.mult, op1=ALU.add))
            step(dve.tensor_scalar(turns, a, 3.1415925, -3.1415925, ALU.min, ALU.max))
            step(dve.tensor_scalar(r, turns, -1.0, None, ALU.mult))
            step(dve.tensor_tensor(r, turns, r, ALU.max))
            dve.tensor_scalar(r, r, -1.0, 1.5707963267948966, ALU.mult, ALU.add).then_inc(trig_in, 1)
            dve.wait_ge(trig, 2)
            dve.tensor_copy(cc[:, :, 8:16], cc[:, :, 0:8])
            step(dve.tensor_scalar(ss[:, :, 8:16], ss[:, :, 0:8], -1.0, None, ALU.mult))
            dve.wait_ge(post, 1)
            dve.tensor_copy(posT[:, :, :], bank[7][:, 0:32].rearrange("p (v j) -> p v j", v=2))
            dve.wait_ge(small_landed, 16 * 7)
            step(dve.tensor_scalar(nsink[:, :], sink[:, :], -1.0, None, ALU.mult))

            def copy_turned(n, dst):
                dve.wait_ge(turned, n + 1)
                dve.tensor_copy(dst, bank[5][:, :].rearrange("p (c n) -> p c n", c=4)).then_inc(moved_v, 1)

            def turn_h(first):
                for n in range(1 - first % 2, 4, 2):
                    tt, q = n // 2, n % 2
                    copy_turned(first + n, hT[:, 4 * q:4 * q + 4, tt * P:tt * P + P])

            turn_h(T_X)

            def rotate(src, dst, tt, heads):
                wide = [P, heads, ROT]
                c = cc[:, tt, :].rearrange("p (a n) -> p a n", a=1).to_broadcast(wide)
                s = ss[:, tt, :].rearrange("p (a n) -> p a n", a=1).to_broadcast(wide)
                dve.tensor_tensor(rot1[:, 0:heads, :], src, c, ALU.mult)
                step(dve.tensor_tensor(rot2[:, 0:heads, :], src, s, ALU.mult))
                dve.tensor_tensor(dst[..., 0:8], rot1_of(dst, heads, 0), rot2_of(dst, heads, 8), ALU.add)
                return dve.tensor_tensor(dst[..., 8:16], rot1_of(dst, heads, 8), rot2_of(dst, heads, 0), ALU.add)

            def rot1_of(dst, heads, at):
                v = rot1[:, 0:heads, at:at + 8]
                return v.rearrange("p (b r) d -> p b r d", b=2) if len(dst.shape) == 4 else v

            def rot2_of(dst, heads, at):
                v = rot2[:, 0:heads, at:at + 8]
                return v.rearrange("p (b r) d -> p b r d", b=2) if len(dst.shape) == 4 else v

            def stage_part(j, proj, base, nturn):
                kind, _, tt, w = proj[j]
                if j >= 1:
                    dve.wait_ge(staged_v, base + j)
                dve.wait_ge(staged_a, base + j + 1)
                src = bank[j % 4]
                s = stage[:, j % 2, :]
                if j >= 2:
                    dve.wait_ge(turned, nturn[j - 1])
                if kind == "cmpkv":
                    dve.tensor_copy(s.rearrange("p (g a d) -> p g a d", g=8, a=2)[:, :, 1, :],
                                    src[:, :].rearrange("p (g d) -> p g d", g=8)).then_inc(staged_v, 1)
                elif kind in ("slckv", "winkv", "kv"):
                    nk = w // 2
                    rotate(src[:, 0:nk].rearrange("p (g d) -> p g d", d=HD)[:, :, 0:ROT],
                           s[:, 0:nk].rearrange("p (g d) -> p g d", d=HD)[:, :, 0:ROT], tt, nk // HD)\
                        .then_inc(staged_v, 1)
                elif kind == "gate":
                    dve.tensor_scalar(gates[:, tt, 0:16], gates[:, tt, 0:16], seen[:, tt:tt + 1], None, ALU.mult)\
                       .then_inc(staged_v, 1)
                elif kind in ("q0", "q1"):
                    dst = s[:, 512:1024].rearrange("p (r b d) -> p b r d", r=4, b=2)
                    dve.tensor_copy(dst[:, :, :, ROT:],
                                    src[:, :].rearrange("p (b r d) -> p b r d", b=2, r=4)[:, :, :, ROT:])
                    rotate(src[:, :].rearrange("p (r d) -> p r d", r=8)[:, :, 0:ROT], dst[:, :, :, 0:ROT], tt, 8)\
                        .then_inc(staged_v, 1)
                else:
                    b = int(kind[-1])
                    rotate(src[:, :].rearrange("p (r d) -> p r d", r=8)[:, :, 0:ROT],
                           s.rearrange("p (r b d) -> p b r d", r=8, b=2)[:, b, :, 0:ROT], tt, 8).then_inc(staged_v, 1)

            def take_turned(j, proj, first):
                kind, _, tt, _ = proj[j]
                cols = slice(tt * P, tt * P + P)
                for t, n in enumerate(range(first[j], first[j + 1])):
                    if n % 2 == 0:
                        continue
                    dve.wait_ge(turned, n + 1)
                    src = bank[5]
                    four = src[:, :].rearrange("p (g n) -> p g n", g=4)
                    if kind == "cmpkv":
                        lo = 1 if tt == 0 else 0
                        dve.tensor_copy(kcvT[0:64, t, :, cols], four[0:64])
                        ins = dve.tensor_copy(kcvT[64:128, t, :, tt * P + lo - 1:tt * P + P - 1], four[64:128, :, lo:])
                    elif kind in ("slckv", "winkv"):
                        ins = dve.tensor_copy((ksT if kind == "slckv" else kwT)[:, :, cols],
                                              src[:, 0:256].rearrange("p (g n) -> p g n", g=2))
                    elif kind in ("q0", "q1"):
                        pb = int(kind[-1])
                        ins = dve.tensor_copy((qrT if t else qT)[:, 4 * pb:4 * pb + 4, cols], four)
                    elif kind == "kv":
                        ins = dve.tensor_copy(ksT[:, 0, cols], src[:, 0:P])
                    else:
                        ins = dve.tensor_copy(qrT[:, 4 * t:4 * t + 4, cols], four)
                    ins.then_inc(moved_v, 1)

            for j in range(len(PROJ_A) + 1):
                if j < len(PROJ_A):
                    stage_part(j, PROJ_A, 0, first_a)
                if j >= 1:
                    take_turned(j - 1, PROJ_A, first_a)

            moved(dve, first_a[2] - 1)
            moved(dve, first_a[2] - 2)
            for kv in range(2):
                for g in range(4):
                    by_row = kcvT[:, kv, g, :].rearrange("p (n s two) -> p s n two", s=8, two=2)[:, :, :, 0]
                    for upper in range(2):
                        n0 = upper
                        pos = posT[:, kv, 8 * upper:8 * upper + 8].rearrange("p (j n) -> p j n", n=1)\
                            .to_broadcast([P, 8, N_CMP])
                        ins = dve.tensor_tensor(cmp_in[:, kv, 8 * upper:8 * upper + 8, 16 * g:16 * g + N_CMP],
                                                by_row[:, :, n0:n0 + N_CMP], pos, ALU.add)
                ins.then_inc(cmp_built, 1)
            if T_HID % 2:
                dve.wait_ge(turned, T_HID + 1)
                for twice in range(2):
                    ins = dve.tensor_copy(hidT.rearrange("p a c n -> p (a c) n")[:, :, 64 * twice:64 * twice + 64],
                                          bank[5][:, 0:256].rearrange("p (g n) -> p g n", g=4))
                ins.then_inc(moved_v, 1)
            dve.wait_ge(kc_ready, 1)
            dve.tensor_copy(vc, bank[7][:, P:2 * P]).then_inc(vc_ready, 1)

            def attention(jobs, base, first, swa):
                for i in range(len(jobs) + 3):
                    if i < len(jobs):
                        br, pb, b, tt, h0, nh, w, _, _ = jobs[i]
                        dve.wait_ge(scored, base + i + 1)
                        step(dve.tensor_reduce(mx[:, i % 4, 0:nh], bank[i % 4][:, :].rearrange("p (k n) -> p k n", k=nh),
                                               X, ALU.max))
                        if swa:
                            h_at = 8 * b + 4 * pb + h0
                            step(dve.scalar_tensor_tensor(out=nb[:, i % 4, 0:nh], in0=mx[:, i % 4, 0:nh], scalar=-SCALE,
                                                          in1=nsink[:, h_at:h_at + nh], op0=ALU.mult, op1=ALU.min))
                            dve.tensor_tensor(sn[:, i % 4, 0:nh], sink[:, h_at:h_at + nh], nb[:, i % 4, 0:nh], ALU.add)\
                               .then_inc(shifted, 1)
                        else:
                            dve.tensor_scalar(nb[:, i % 4, 0:nh], mx[:, i % 4, 0:nh], -SCALE, None, ALU.mult)\
                               .then_inc(shifted, 1)
                    if 1 <= i <= len(jobs):
                        br, pb, b, tt, h0, nh, w, _, _ = jobs[i - 1]
                        m = (i - 1) % 4
                        dve.wait_ge(expd, base + i)
                        if swa:
                            step(dve.tensor_tensor(sums[:, m, 0:nh], sums[:, m, 0:nh], es[:, m, 0:nh], ALU.add))
                        step(dve.reciprocal(rg[:, m, 0:nh], sums[:, m, 0:nh]))
                        if not swa:
                            g_at = 16 * ("cmp", "slc", "win").index(br) + 4 * (2 * pb + b) + h0
                            step(dve.tensor_tensor(rg[:, m, 0:nh], rg[:, m, 0:nh], gates[:, tt, g_at:g_at + nh], ALU.mult))
                        e = ex[:, (i - 1) % 3, :].rearrange("p (k n) -> p k n", k=nh)
                        dve.tensor_tensor(e, e, rg[:, m, 0:nh].rearrange("p (k n) -> p k n", n=1).to_broadcast([P, nh, w]),
                                          ALU.mult).then_inc(normed, 1)
                    if 2 <= i < len(jobs) + 2 and (first + i - 2) % 2:
                        n = first + i - 2
                        dve.wait_ge(turned, n + 1)
                        if i >= 4:
                            dve.wait_ge(summed, base + i - 3)
                        dve.tensor_copy(pT[:, 1, :], bank[5][:, :]).then_inc(moved_v, 1)

            def norm(k, ready):
                dve.wait_ge(ln_landed, 32 * (k + 1))
                for tt in range(NT):
                    dve.bn_stats(stats[:, tt, 0, :], pre[:, tt, 0:512])
                    step(dve.bn_stats(stats[:, tt, 1, :], pre[:, tt, 512:1024]))
                    step(dve.bn_aggr(mv[:, tt, :], stats[:, tt, :, :].rearrange("p a b -> p (a b)")))
                    dve.tensor_scalar(std[:, tt, 1:2], mv[:, tt, 1:2], LN_EPS, None, ALU.add).then_inc(var_ready, 1)
                for tt in range(NT):
                    dve.wait_ge(std_ready, NT * k + tt + 1)
                    step(dve.reciprocal(std[:, tt, 1:2], std[:, tt, 0:1]))
                    step(dve.tensor_scalar(pre[:, tt, :], pre[:, tt, :], mv[:, tt, 0:1], std[:, tt, 1:2],
                                           ALU.subtract, ALU.mult))
                    step(dve.tensor_tensor(pre[:, tt, :], pre[:, tt, :], lnp[:, 0, :], ALU.mult))
                    dve.tensor_tensor(h[:, tt, :], pre[:, tt, :], lnp[:, 1, :], ALU.add).then_inc(h_ready, 1)

            def add_mix(banks, count):
                for n in range(4):
                    half, tt = n // 2, n % 2
                    dve.wait_ge(mixed, count + n + 1)
                    cols = slice(512 * half, 512 * half + 512)
                    step(dve.scalar_tensor_tensor(out=pre[:, tt, cols], in0=h[:, tt, cols], scalar=ALPHA,
                                                  in1=bank[banks + n][:, :], op0=ALU.mult, op1=ALU.add))

            attention(JOBS_A, 0, T_JA, False)
            add_mix(0, 0)
            norm(0, 0)
            turn_h(T_H1)
            for c in range(N_DENSE_IN):
                dve.wait_ge(silu_ready, c + 1)
                dve.tensor_tensor(actT[:, 2 * c:2 * c + 2, :], silu[:, c % 2, :].rearrange("p (a n) -> p a n", a=2),
                                  bank[2 * (c % 2) + 1][:, :].rearrange("p (a n) -> p a n", a=2), ALU.mult)\
                   .then_inc(act_ready, 1)
            add_mix(4, 4)
            norm(1, 0)
            turn_h(T_H2)
            for j in range(len(PROJ_B) + 1):
                if j < len(PROJ_B):
                    stage_part(j, PROJ_B, len(PROJ_A), first_b)
                if j >= 1:
                    take_turned(j - 1, PROJ_B, first_b)
            attention(JOBS_B, len(JOBS_A), T_JB, True)
            add_mix(0, 8)
            norm(2, 0)
            turn_h(T_H3)

            dve.tensor_scalar(pre[:, :, :], h[:, :, :], ALPHA, None, ALU.mult).then_inc(e_added, 1)
            logits, best, pick1, rest, pick2, sel, gw, tmp = (lg[:, k, :, :] for k in range(8))
            wide = [P, NT, NE]
            m1, x1, m2, x2 = (top[:, k, :, :] for k in range(4))
            gap, egap, g1, g2, den = (top[:, k, :, :] for k in range(4, 9))
            dve.wait_ge(routed, 1)
            step(dve.tensor_copy(logits, bank[6][:, 0:NT * NE].rearrange("p (t e) -> p t e", t=NT)))

            def pick_largest(values, m, x_, onehot):
                step(dve.tensor_reduce(m, values, X, ALU.max))
                step(dve.tensor_tensor(best, values, m.to_broadcast(wide), ALU.is_equal))
                step(dve.tensor_tensor(best, best, order[:, :, :], ALU.mult))
                step(dve.tensor_reduce(x_, best, X, ALU.max))
                step(dve.tensor_tensor(onehot, best, x_.to_broadcast(wide), ALU.is_equal))

            pick_largest(logits, m1, x1, pick1)
            step(dve.scalar_tensor_tensor(out=rest, in0=pick1, scalar=NEG, in1=logits, op0=ALU.mult, op1=ALU.add))
            pick_largest(rest, m2, x2, pick2)
            dve.tensor_tensor(gap, m2, m1, ALU.subtract).then_inc(gap_ready, 1)
            step(dve.tensor_tensor(sel, pick1, pick2, ALU.add))
            dve.tensor_copy(selb[:, :, :], sel).then_inc(sel_ready, 1)
            dve.wait_ge(gap_exp, 1)
            step(dve.tensor_scalar(den, egap, 1.0, None, ALU.add))
            step(dve.reciprocal(g1, den))
            step(dve.tensor_tensor(g2, egap, g1, ALU.mult))
            step(dve.tensor_tensor(gw, pick1, g1.to_broadcast(wide), ALU.mult))
            step(dve.tensor_tensor(tmp, pick2, g2.to_broadcast(wide), ALU.mult))
            dve.tensor_tensor(gatex[:, :, 0:NE], gw, tmp, ALU.add)
            step(dve.tensor_tensor(gatex[:, :, NE:2 * NE], gw, tmp, ALU.add))
            dve.wait_ge(ranked, 1)
            step(dve.tensor_scalar(tmp, bank[7][:, 0:NT * NE].rearrange("p (t e) -> p t e", t=NT), 1.0, None, ALU.add))
            step(dve.tensor_tensor(tmp, tmp, sel, ALU.mult))
            dve.tensor_scalar(slotx[:, :, 0:NE], tmp, -1.0, None, ALU.add)
            step(dve.tensor_scalar(slotx[:, :, NE:2 * NE], tmp, -1.0 - P, None, ALU.add))
            step(dve.tensor_reduce(cnt[:, 0:1], bank[7][:, 2 * NE:3 * NE], X, ALU.max))
            step(dve.tensor_scalar(cnt[:, 1:2], cnt[:, 0:1], float(P), None, ALU.is_gt))
            dve.tensor_scalar(turns_i[:, :], cnt[:, 1:2], float(NE), float(NE), ALU.mult, ALU.add)\
               .then_inc(plan_ready, 1)

            def build_pick(at, value):
                if value is not None:
                    dve.wait_ge(e_rows, value)
                for tt in range(NT):
                    ins = dve.tensor_scalar(pick[:, tt, :], slots[:, :], slotx[:, tt, at], None, ALU.is_equal)
                ins.then_inc(e_pick, 1)

            def take_rows(value):
                dve.wait_ge(e_rows, value)
                dve.tensor_copy(xgT[:, 4:8, :], bank[3][:, :].rearrange("p (c n) -> p c n", c=4)).then_inc(e_rows_v, 1)

            def add_back(i):
                dve.wait_ge(e_added, 4 * i - 3)
                for n in range(4):
                    tt, half = n // 2, n % 2
                    dve.wait_ge(e_back, 4 * i + n - 3)
                    cols = slice(512 * half, 512 * half + 512)
                    dve.tensor_tensor(pre[:, tt, cols], pre[:, tt, cols], bank[4 + n % 2][:, :], ALU.add)\
                       .then_inc(e_added, 1)

            dve.wait_ge(e_added, 1)
            dve.memset(ysb[:, 512:1024], 0.0).then_inc(e_y_v, 1)
            dve.memset(putT, 0.0).then_inc(e_putT_moved, 1)
            dve.sem_inc(e_act, 1)
            dve.wait_ge(plan_ready, 1)
            steps = dve.value_load(turns_i[0:1, 0:1], min_val=NE, max_val=2 * NE)
            build_pick(slice(0, 1), None)
            take_rows(1)
            with dve.Fori(0, steps) as i:
                for f in range(FT + 1):
                    if f < FT:
                        dve.wait_ge(e_silu, i * FT + f + 1)
                        dve.wait_ge(e_turned, i * FT + max(f - 1, 0) + 1)
                        dve.tensor_tensor(act[:, f % 2, :], esilu[:, f % 2, :], bank[2 * (f % 2) + 1][:, :], ALU.mult)\
                           .then_inc(e_act, 1)
                    if f == 0:
                        add_back(i + 1)
                    if f == 3:
                        build_pick(ds(i + 1, 1), i + 1)
                        dve.wait_ge(e_putT, i + 1)
                        for tt in range(NT):
                            ins = dve.tensor_scalar(put[:, tt, :], slots[:, :], slotx[:, tt, ds(i, 1)],
                                                    gatex[:, tt, ds(i, 1)], ALU.is_equal, ALU.mult)
                        ins.then_inc(e_put, 1)
                    if f >= 1 and (f - 1) % 2:
                        dve.wait_ge(e_turned, i * FT + f + 1)
                        dve.tensor_copy(eactT[:, 1, :, :], bank[5][:, :].rearrange("p (c n) -> p c n", c=4))\
                           .then_inc(e_moved_v, 1)
                dve.wait_ge(e_putT, i + 2)
                dve.tensor_copy(putT, bank[5][:, 0:2 * P].rearrange("p (t n) -> p t n", t=NT)).then_inc(e_putT_moved, 1)
                take_rows(i + 2)
                dve.wait_ge(e_y, i + 1)
                dve.tensor_copy(ysb[:, 512:1024], bank[7][:, :]).then_inc(e_y_v, 1)
            add_back(steps + 1)
            dve.wait_ge(e_added, 4 * steps + 5)
            norm(3, 0)


_INS = ['x', 'positions', 'w_in_a', 'w_out_a', 'cmp_pos', 'cmp_w1', 'cmp_w2', 'w_kv_shared', 'w_q_b', 'w_out_b',
        'sinks_b', 'ln_g', 'ln_b', 'dense_w_in', 'dense_w_out', 'moe_router', 'moe_w_in', 'moe_w_out']


def kernel(**inputs):
    import numpy as _np
    import concourse.bacc as _bacc
    from concourse import mybir as _mybir
    from concourse.bass_utils import run_bass_kernel_spmd as _run

    nc = _bacc.Bacc("TRN2", target_bir_lowering=False, num_devices=1)
    arrays, args = {}, []
    for name in _INS:
        a = _np.ascontiguousarray(inputs[name])
        arrays[f"in_{name}_dram"] = a
        args.append(nc.dram_tensor(f"in_{name}_dram", a.shape, _mybir.dt.from_np(a.dtype), kind="ExternalInput").ap())
    args.append(nc.dram_tensor("out_0_dram", (1, SEQ, D), F32, kind="ExternalOutput").ap())
    decoder_kernel(nc, *args)
    r = _run(nc, [arrays], core_ids=[0])
    return r.results[0]["out_0_dram"]
```

```python
from contextlib import ExitStack

import concourse.bass as bass
from concourse import mybir
from concourse.bass import ds

F32 = mybir.dt.float32
F32R = mybir.dt.float32r
BF16 = mybir.dt.bfloat16
I32 = mybir.dt.int32
ALU = mybir.AluOpType
ACT = mybir.ActivationFunctionType
X = mybir.AxisListType.X

P = 128
SEQ, D, HD = 256, 1024, 64
NT = SEQ // P
DC = D // P
ROT = HD // 4
ROPE_THETA = 500000.0
A_IN, A_KV = 2608, 256
CMP_STRIDE, CMP_HID = 16, 256
N_CMP = SEQ // CMP_STRIDE - 1
CMP_PAIRS = 16
FF, FFE, NE = 2816, 3584, 8
FT = FFE // 512
DEPTH = 2
ALPHA = float((2 * DEPTH) ** 0.25)
SCALE = HD ** -0.5
LN_EPS = 1e-5
NEG = -1e30
UNIT = 2048
RING = 7
SPLITS = 3
TWO_PI_PARTS = (6.28125, 1.9350051879882812e-03, 3.0199159819e-07)


def weight_items():
    items = [("in_a", c, k) for c in (2, 3, 4) for k in range(2)] + [("in_a", 5, 0)]
    items += [("in_a", c, k) for c in (0, 1) for k in range(2)]
    items += [("cmp", c, k) for c in range(2) for k in range(2)]
    items += [("out_a", c, k) for c in range(2) for k in range(2)]
    items += [("dense_in", c, part) for c in range(FF // 256) for part in range(2)]
    items += [("dense_out", 0, k) for k in range(FF // 256)]
    items += [("kv", 0, 0)] + [("q_b", c, k) for c in range(2) for k in range(2)]
    items += [("out_b", c, k) for c in range(2) for k in range(2)]
    return items


ITEMS = weight_items()
N_FIRST = len(ITEMS)
AT = {}
for _n, (_kind, _, _) in enumerate(ITEMS):
    AT.setdefault(_kind, _n)
EXPERT = []
for _f in range(FT):
    EXPERT += [("g", _f, 0), ("g", _f, 1), ("u", _f, 0), ("u", _f, 1)]
    if _f >= 2:
        EXPERT += [("o", _f - 2, 0), ("o", _f - 2, 1)]
for _f in (FT - 2, FT - 1):
    EXPERT += [("o", _f, 0), ("o", _f, 1)]
PER_EXPERT = len(EXPERT)
assert PER_EXPERT % RING == 0 and PER_EXPERT % SPLITS == 0


LAST_GU = [EXPERT.index(("u", f, 1)) for f in range(FT)]
TURN_AFTER = [LAST_GU[0] + 4, LAST_GU[1] + 4] + [LAST_GU[f] + 2 for f in range(2, FT)]
BACK_AFTER = (3, 5)
EXPERT_WORK = {PER_EXPERT + SPLITS - 1: [("y", 0)]}
for _f in range(FT):
    EXPERT_WORK.setdefault(LAST_GU[_f] + SPLITS, []).append(("act", _f))
for _f in range(FT):
    EXPERT_WORK.setdefault(TURN_AFTER[_f] + SPLITS, []).append(("turn", _f))
for _n in range(2):
    EXPERT_WORK.setdefault(BACK_AFTER[_n] + SPLITS, []).append(("back", _n))
EXPERT_WORK.setdefault(24, []).append(("build", 0))
EXPERT_WORK.setdefault(PER_EXPERT - 1, []).append(("rows", 0))


def attention_jobs(branches):
    jobs = []
    for pb in range(2):
        for b in range(2):
            for tt in range(NT):
                mine = []
                for br in branches:
                    if br == "cmp" or tt == 0:
                        mine.append((br, pb, b, tt, 0, 4, P))
                    else:
                        mine += [(br, pb, b, tt, 0, 2, SEQ), (br, pb, b, tt, 2, 2, SEQ)]
                jobs += [(*j, n == 0, n == len(mine) - 1) for n, j in enumerate(mine)]
    return jobs


JOBS_A = attention_jobs(("cmp", "slc", "win"))
JOBS_B = attention_jobs(("swa",))
PROJ_A = [(k, n, tt, w) for n, (k, w) in enumerate(
    [("cmpkv", 512), ("slckv", 512), ("winkv", 512), ("gate", 48), ("q0", 512), ("q1", 512)]) for tt in range(NT)]
PROJ_B = [(k, n, tt, w) for n, (k, w) in enumerate([("kv", 256), ("qb0", 512), ("qb1", 512)]) for tt in range(NT)]
LAST_A = [AT["in_a"] + n for n in (1, 3, 5, 6, 8, 10)]
LAST_B = [AT["kv"] + n for n in (0, 2, 4)]
N_DENSE = FF // 256
TURNS = {"cmpkv": 2, "slckv": 1, "winkv": 1, "gate": 0, "q0": 2, "q1": 2, "kv": 1, "qb0": 0, "qb1": 2}


def decoder_kernel(nc, x, positions, w_in_a, w_out_a, cmp_pos, cmp_w1, cmp_w2, w_kv_shared, w_q_b, w_out_b,
                   sinks_b, ln_g, ln_b, dense_w_in, dense_w_out, moe_router, moe_w_in, moe_w_out, out):
    ctx = ExitStack()
    with ctx:
        def sb(name, shape, dt=F32):
            return ctx.enter_context(nc.sbuf_tensor(name, shape, dt))

        def sem(name):
            return ctx.enter_context(nc.semaphore(name))

        ident = sb("ident", [P, P])
        identb = sb("identb", [P, P], BF16)
        onesb = sb("onesb", [P, P], BF16)
        earlier = sb("earlier", [P, P], BF16)
        causal = sb("causal", [P, 2, P], BF16)
        window = sb("window", [P, 2, P], BF16)
        cmpmask = sb("cmpmask", [P, NT, 4, P], BF16)
        seen = sb("seen", [P, NT])
        slots = sb("slots", [P, P])
        order = sb("order", [P, NT, NE])
        freq = sb("freq", [P, ROT // 2])
        pos_i = sb("pos_i", [P, NT], I32)
        pos_f = sb("pos_f", [P, NT])
        ang = sb("ang", [P, 3, NT, ROT // 2])
        cc = sb("cc", [P, NT, ROT])
        ss = sb("ss", [P, NT, ROT])
        rot1 = sb("rot1", [P, 8, ROT])
        rot2 = sb("rot2", [P, 8, ROT])
        posr = sb("posr", [16, 2, P])
        posT = sb("posT", [P, 2, 16])
        w2 = sb("w2", [P, 2, 2, 2, HD])
        router = sb("router", [P, DC, NE])
        routerh = sb("routerh", [P, DC, NE], F32R)
        routerl = sb("routerl", [P, DC, NE], F32R)
        lgT = sb("lgT", [NE, SEQ])
        sink = sb("sink", [P, 16])
        nsink = sb("nsink", [P, 16])
        gates = sb("gates", [P, NT, 48])
        mx = sb("mx", [P, 4, 4])
        nb = sb("nb", [P, 4, 4])
        sn = sb("sn", [P, 4, 4])
        es = sb("es", [P, 4, 4])
        sums = sb("sums", [P, 4, 4])
        rg = sb("rg", [P, 4, 4])
        stats = sb("stats", [P, NT, 2, 6])
        mv = sb("mv", [P, NT, 2])
        std = sb("std", [P, NT, 2])
        lg = sb("lg", [P, 8, NT, NE])
        selb = sb("selb", [P, NT, NE], BF16)
        top = sb("top", [P, 12, NT, 1])
        slotx = sb("slotx", [P, NT, 17])
        gatex = sb("gatex", [P, NT, 17])
        cnt = sb("cnt", [P, 2])
        turns_i = sb("turns_i", [P, 1], I32)

        base = [-(-nc.sbuf_base // 64) * 64]

        def place(*parts):
            size = 0
            found = []
            for name, shape, dt in parts:
                found.append(nc.alloc_sbuf_tensor_at(name, shape, dt, offset=base[0]))
                n = 4
                for x_ in shape[1:]:
                    n *= x_
                size = max(size, n)
            base[0] += size
            return found if len(found) > 1 else found[0]

        ring = place(("ring", [P, RING, UNIT], F32))
        wh = place(("wh", [P, SPLITS, UNIT], F32R))
        wl = place(("wl", [P, SPLITS, UNIT], F32R))
        h = place(("h", [P, NT, D], F32))
        pre, cmp_l = place(("pre", [P, NT, D], F32), ("cmp_l", [P, 2, CMP_PAIRS, 64], F32R))
        lnp, cmp_h = place(("lnp", [P, 2, D], F32), ("cmp_h", [P, 2, CMP_PAIRS, 64], F32R))
        hTh = place(("hTh", [P, DC, SEQ], F32R))
        hTl = place(("hTl", [P, DC, SEQ], F32R))
        arena, arena_r = place(("arena", [P, 12544], F32), ("arena_r", [P, 12544], F32R))

        def room(at, *shape, of=None):
            n = 1
            for x_ in shape:
                n *= x_
            v = (arena if of is None else of)[:, at:at + n]
            names = "abcd"[:len(shape)]
            if len(shape) > 1:
                v = v.rearrange(f"p ({' '.join(names)}) -> p {' '.join(names)}", **dict(zip(names[1:], shape[1:])))
            return v

        qT = room(0, 8, SEQ)
        qrT = room(2048, 8, SEQ)
        ksT = room(4096, 2, SEQ)
        kwT = room(4608, 2, SEQ)
        kcT = room(5120, P)
        vs = room(5248, NT, 256)
        vw = room(5760, NT, 256)
        vc = room(6272, P)
        stage = room(6400, 2, 1024)
        kcvT = room(8448, 2, 4, SEQ)
        cmp_in = room(10496, 2, CMP_PAIRS, 64)
        hid = room(8448, 2, CMP_HID)
        hidT = room(8960, 2, 2, P)
        ex = room(8448, 3, 512)
        pT = room(9984, 2, 512)
        actTh = room(0, FF // P, SEQ, of=arena_r)
        actTl = room(5632, FF // P, SEQ, of=arena_r)
        silu = room(11264, 2, 512)
        xgTh = room(0, DC, P, of=arena_r)
        xgTl = room(1024, DC, P, of=arena_r)
        eactTh = room(2048, 2, 4, P, of=arena_r)
        eactTl = room(3072, 2, 4, P, of=arena_r)
        act = room(4096, 2, 512)
        esilu = room(5120, 2, 512)
        ysb = room(6144, D)
        pick = room(7168, NT, P)
        put = room(7424, NT, P)
        putT = room(7680, NT, P)

        bank = [ctx.enter_context(nc.psum_tensor(f"bank{i}", [P, 512], F32)) for i in range(8)]

        landed = [sem(f"landed{i}") for i in range(RING)]
        rounded = sem("rounded")
        split = sem("split")
        used = sem("used")
        x_landed = sem("x_landed")
        pos_landed = sem("pos_landed")
        small_landed = sem("small_landed")
        ln_landed = sem("ln_landed")
        ident_ready = sem("ident_ready")
        consts = sem("consts")
        consts_step = sem("consts_step")
        dve_step = sem("dve_step")
        trig_in = sem("trig_in")
        trig = sem("trig")
        turned = sem("turned")
        moved_a = sem("moved_a")
        moved_v = sem("moved_v")
        high = sem("high")
        post = sem("post")
        post_moved = sem("post_moved")
        staged_a = sem("staged_a")
        staged_v = sem("staged_v")
        cmp_sum = sem("cmp_sum")
        cmp_high = sem("cmp_high")
        cmp_low = sem("cmp_low")
        cmp_act = sem("cmp_act")
        cmp_kv = sem("cmp_kv")
        kc_ready = sem("kc_ready")
        vc_ready = sem("vc_ready")
        scored = sem("scored")
        shifted = sem("shifted")
        expd = sem("expd")
        normed = sem("normed")
        summed = sem("summed")
        heads_high = sem("heads_high")
        heads_out = sem("heads_out")
        mixed = sem("mixed")
        var_ready = sem("var_ready")
        std_ready = sem("std_ready")
        h_ready = sem("h_ready")
        silu_ready = sem("silu_ready")
        act_ready = sem("act_ready")
        act_high = sem("act_high")
        act_low = sem("act_low")
        router_high = sem("router_high")
        router_low = sem("router_low")
        routed = sem("routed")
        logits_moved = sem("logits_moved")
        gap_ready = sem("gap_ready")
        gap_exp = sem("gap_exp")
        sel_ready = sem("sel_ready")
        ranked = sem("ranked")
        plan_ready = sem("plan_ready")
        e_pick = sem("e_pick")
        e_put = sem("e_put")
        e_silu = sem("e_silu")
        e_act = sem("e_act")
        e_turned = sem("e_turned")
        e_high = sem("e_high")
        e_low = sem("e_low")
        e_putT = sem("e_putT")
        e_putT_moved = sem("e_putT_moved")
        e_rows = sem("e_rows")
        e_rows_high = sem("e_rows_high")
        e_rows_low = sem("e_rows_low")
        e_y_a = sem("e_y_a")
        e_y_v = sem("e_y_v")
        e_back = sem("e_back")
        e_added = sem("e_added")
        done = sem("done")

        in_a = w_in_a[0].rearrange("(c p) n -> p c n", p=P)
        d_in = dense_w_in[0].rearrange("(c p) n -> p c n", p=P)
        d_out = dense_w_out[0].rearrange("(c p) n -> p c n", p=P)
        q_b = w_q_b[0].rearrange("(c p) n -> p c n", p=P)
        kv_w = w_kv_shared.rearrange("(c p) n -> p c n", p=P)
        e_in = moe_w_in[0].rearrange("e (c p) n -> e p c n", p=P)
        e_out = moe_w_out[0].rearrange("e (c p) n -> e p c n", p=P)
        out_a = w_out_a[0].rearrange("(a b r d) n -> b d a r n", a=2, b=2, r=4, d=HD)
        out_b = w_out_b[0].rearrange("(b r d) n -> b d r n", b=2, r=8, d=HD)

        def start_item(sp, n):
            kind, c, k = ITEMS[n]
            sig = landed[n % RING]
            slot = ring[:, n % RING, :]

            def rows(count):
                return slot[:, 0:UNIT if count is None else count]

            if kind == "in_a":
                w = min(512, A_IN - 512 * c)
                depth = 4 if w == 512 else DC
                sp.dma_start(slot[:, 0:depth * w].rearrange("p (c n) -> p c n", c=depth),
                             in_a[:, 4 * k:4 * k + depth, 512 * c:512 * c + w]).then_inc(sig, 32)
            elif kind == "cmp":
                sp.dma_start(slot.rearrange("p (j n) -> p j n", j=8),
                             cmp_w1[0, c].rearrange("(j p) n -> p j n", p=P)[:, 8 * k:8 * k + 8, :]).then_inc(sig, 32)
            elif kind in ("out_a", "out_b"):
                for b in range(2):
                    dst = slot[b * HD:(b + 1) * HD, :].rearrange("p (r n) -> p r n", r=4)
                    cols = slice(512 * c, 512 * c + 512)
                    src = out_a[b, :, k, :, cols] if kind == "out_a" else out_b[b, :, 4 * k:4 * k + 4, cols]
                    sp.dma_start(dst, src).then_inc(sig, 16)
            elif kind == "dense_in":
                at = k * FF + 256 * c
                sp.dma_start(slot.rearrange("p (c n) -> p c n", c=DC), d_in[:, :, at:at + 256]).then_inc(sig, 32)
            elif kind == "dense_out":
                sp.dma_start(slot.rearrange("p (c n) -> p c n", c=2), d_out[:, 2 * k:2 * k + 2, :]).then_inc(sig, 32)
            elif kind == "kv":
                sp.dma_start(slot.rearrange("p (c n) -> p c n", c=DC), kv_w).then_inc(sig, 32)
            else:
                sp.dma_start(slot.rearrange("p (c n) -> p c n", c=4),
                             q_b[:, 4 * k:4 * k + 4, 512 * c:512 * c + 512]).then_inc(sig, 32)

        def size_of(n):
            return DC * 48 if n < N_FIRST and ITEMS[n][:2] == ("in_a", 5) else UNIT

        BEFORE = [32 * sum(1 for n in range(N_FIRST) if n % RING == s) for s in range(RING)]

        def expert_landed(eng, i, k):
            s = (N_FIRST + k) % RING
            nth = sum(1 for j in range(k + 1) if (N_FIRST + j) % RING == s)
            eng.wait_ge(landed[s], BEFORE[s] + 16 * nth + 16 * (PER_EXPERT // RING) * i)

        def expert_used(eng, i, k):
            eng.wait_ge(used, N_FIRST + k + 1 + PER_EXPERT * i)

        def moved(eng, n):
            if n >= 0:
                mine = [m for m in range(n + 1) if MOVER[m] == MOVER[n]]
                eng.wait_ge(moved_v if MOVER[n] == "v" else moved_a, len(mine))

        T_X = 0
        T_A = T_X + 4
        first_a = [T_A + sum(TURNS[p[0]] for p in PROJ_A[:j]) for j in range(len(PROJ_A) + 1)]
        T_HID = first_a[-1]
        T_JA = T_HID + 1
        T_H1 = T_JA + len(JOBS_A)
        T_H2 = T_H1 + 4
        T_B = T_H2 + 4
        first_b = [T_B + sum(TURNS[p[0]] for p in PROJ_B[:j]) for j in range(len(PROJ_B) + 1)]
        T_JB = first_b[-1]
        T_H3 = T_JB + len(JOBS_B)
        T_END = T_H3 + 4

        MOVER = ["v" if n % 2 else "a" for n in range(T_END)]
        TBANK = [4 + n % 4 if n < T_HID or T_B <= n < T_JB else 4 + n % 2 for n in range(T_END)]
        for first, b in ((T_X, 4), (T_H1, 4), (T_H2, 0), (T_H3, 4)):
            MOVER[first:first + 4] = "vvvv"
            TBANK[first:first + 4] = range(b, b + 4)

        block = ctx.enter_context(nc.Block())

        @block.sync
        def _(sp):
            sp.wait_ge(x_landed, 16)
            for n in range(N_FIRST):
                if n >= RING:
                    sp.wait_ge(split, n - RING + 1)
                start_item(sp, n)

            def expert_item(i, k, expert):
                kind, f, half = EXPERT[k]
                s = (N_FIRST + k) % RING
                sp.wait_ge(split, N_FIRST + k - RING + 1 + PER_EXPERT * i)
                if kind == "o":
                    src = e_out[ds(expert, 1), :, 4 * f + 2 * half:4 * f + 2 * half + 2, :]
                    dst = ring[:, s, :].rearrange("p (c n) -> p c n", c=2)
                else:
                    at = (kind == "u") * FFE + 512 * f
                    src = e_in[ds(expert, 1), :, 4 * half:4 * half + 4, at:at + 512]
                    dst = ring[:, s, :].rearrange("p (c n) -> p c n", c=4)
                sp.dma_start(dst, src.rearrange("e p c n -> (e p) c n")).then_inc(landed[s], 16)

            for k in range(PER_EXPERT):
                expert_item(0, k, 0)
            sp.wait_ge(plan_ready, 1)
            steps = sp.value_load(turns_i[0:1, 0:1], min_val=NE, max_val=2 * NE)
            with sp.Fori(1, steps) as i:
                for k in range(PER_EXPERT):
                    expert_item(i, k, i % NE)
            for k in range(SPLITS):
                expert_item(steps, k, 0)
            for tt in range(NT):
                sp.wait_ge(h_ready, 12 + 2 * tt + 2)
                sp.dma_start(out[0, tt * P:tt * P + P, :], h[:, tt, :]).then_inc(done, 16)
            sp.wait_ge(done, 16 * NT)

        @block.gpsimd
        def _(pool):
            n = [0]

            def step(ins):
                n[0] += 1
                ins.then_inc(consts_step, 1)
                pool.wait_ge(consts_step, n[0])

            step(pool.memset(ident[:, :], 0.0))
            step(pool.affine_select(out=ident[:, :], in_=ident[:, :], compare_op=ALU.not_equal, fill=1.0, base=0,
                                    pattern=[[-1, P]], channel_multiplier=1))
            pool.sem_inc(ident_ready, 1)
            step(pool.tensor_copy(identb[:, :], ident[:, :]))
            for j in range(ROT // 2):
                step(pool.memset(freq[:, j:j + 1], float(ROPE_THETA ** (-2.0 * j / ROT))))
            step(pool.memset(causal[:, :, :], 0.0))
            step(pool.memset(window[:, :, :], 0.0))
            for m in (causal, window):
                step(pool.affine_select(out=m[:, 1, :], in_=m[:, 1, :], compare_op=ALU.is_ge, fill=NEG, base=0,
                                        pattern=[[-1, P]], channel_multiplier=1))
            step(pool.affine_select(out=window[:, 0, :], in_=window[:, 0, :], compare_op=ALU.is_ge, fill=NEG, base=-1,
                                    pattern=[[1, P]], channel_multiplier=-1))
            step(pool.memset(cmpmask[:, :, :, :], NEG))
            for tt in range(NT):
                for g in range(4):
                    part = cmpmask[:, tt, g, 16 * g:16 * g + 16]
                    step(pool.memset(part, 0.0))
                    step(pool.affine_select(out=part, in_=part, compare_op=ALU.is_ge, fill=NEG,
                                            base=P * tt - (2 * CMP_STRIDE - 1), pattern=[[-CMP_STRIDE, 16]],
                                            channel_multiplier=1))
            step(pool.memset(seen[:, :], 1.0))
            step(pool.affine_select(out=seen[:, 0:1], in_=seen[:, 0:1], compare_op=ALU.is_ge, fill=0.0,
                                    base=-(2 * CMP_STRIDE - 1), pattern=[[0, 1]], channel_multiplier=1))
            step(pool.memset(onesb[:, :], 1.0))
            step(pool.affine_select(out=earlier[:, :], in_=onesb[:, :], compare_op=ALU.is_ge, fill=0.0, base=-1,
                                    pattern=[[1, P]], channel_multiplier=-1))
            step(pool.iota(slots[:, :], [[1, P]], base=0, channel_multiplier=0, allow_small_or_imprecise_dtypes=True))
            step(pool.iota(order[:, :, :], [[0, NT], [-1, NE]], base=NE, channel_multiplier=0,
                           allow_small_or_imprecise_dtypes=True))
            step(pool.memset(cmp_in[:, :, :, :], 0.0))
            pool.memset(slotx[:, :, 16:17], -1.0).then_inc(consts, 1)
            pool.memset(gatex[:, :, 16:17], 0.0).then_inc(consts, 1)

            pool.wait_ge(h_ready, 12)
            pool.tensor_scalar(pre[:, :, :], h[:, :, :], ALPHA, None, ALU.mult).then_inc(e_added, 1)

        @block.scalar
        def _(act_e):
            act_e.dma_start(h[:, :, :], x[0].rearrange("(t p) d -> p t d", p=P)).then_inc(x_landed, 16)
            act_e.dma_start(pos_i[:, :], positions[0].rearrange("(t p) -> p t", p=P),
                            allow_slow_non_contiguous=True).then_inc(pos_landed, 16)
            act_e.dma_start(posr[:, :, :], cmp_pos[0].rearrange("v (j a) d -> j v (a d)", a=2)).then_inc(small_landed, 16)
            for kv in range(2):
                for twice in range(2):
                    act_e.dma_start(w2[:, kv, :, twice, :], cmp_w2[0, kv].rearrange("(c p) d -> p c d", p=P))\
                         .then_inc(small_landed, 16)
            act_e.dma_start(router[:, :, :], moe_router[0].rearrange("(c p) e -> p c e", p=P),
                            allow_slow_non_contiguous=True).then_inc(small_landed, 16)
            act_e.dma_start(sink[:, :], sinks_b[0:1, :].to_broadcast([P, 16])).then_inc(small_landed, 16)

            def load_norm(k):
                for part, src in enumerate((ln_g, ln_b)):
                    act_e.dma_start(lnp[:, part, :], src[k // 2, k % 2:k % 2 + 1, :].to_broadcast([P, D]))\
                         .then_inc(ln_landed, 16)

            n_round = [0]

            def split_weights(upto):
                for n in range(n_round[0], upto):
                    if n < N_FIRST:
                        act_e.wait_ge(landed[n % RING], 32 * (n // RING + 1))
                    else:
                        expert_landed(act_e, 0, n - N_FIRST)
                    if n >= SPLITS:
                        act_e.wait_ge(used, n - SPLITS + 1)
                    size = size_of(n)
                    act_e.activation(wh[:, n % SPLITS, 0:size], ring[:, n % RING, 0:size], ACT.Copy).then_inc(rounded, 1)
                n_round[0] = max(n_round[0], upto)

            def turn_h(first, tt):
                for q in range(2):
                    n = 2 * tt + q
                    act_e.wait_ge(turned, first + n + 1)
                    act_e.activation(hTh[:, 4 * q:4 * q + 4, tt * P:tt * P + P],
                                     bank[TBANK[first + n]][:, :].rearrange("p (c n) -> p c n", c=4), ACT.Copy)\
                         .then_inc(high, 1)

            for tt in range(NT):
                turn_h(T_X, tt)
            split_weights(SPLITS)
            act_e.wait_ge(trig_in, 1)
            act_e.activation(ss[:, :, 0:8], ang[:, 1, :, :], ACT.Sin).then_inc(trig, 1)
            act_e.activation(cc[:, :, 0:8], ang[:, 2, :, :], ACT.Sin).then_inc(trig, 1)
            act_e.wait_ge(small_landed, 16 * 7)
            act_e.activation(routerh[:, :, :], router[:, :, :], ACT.Copy).then_inc(router_high, 1)

            def stage_part(j, proj, base, nturn, last):
                kind, _, tt, w = proj[j]
                act_e.wait_ge(used, last[j // NT] + 1)
                src = bank[j % 4]
                s = stage[:, j % 2, :]
                if j >= 2:
                    act_e.wait_ge(turned, nturn[j - 1])
                if kind == "cmpkv":
                    act_e.activation(s.rearrange("p (g a d) -> p g a d", g=8, a=2)[:, :, 0, :],
                                     src[:, :].rearrange("p (g d) -> p g d", g=8), ACT.Copy).then_inc(staged_a, 1)
                elif kind in ("slckv", "winkv", "kv"):
                    nk = w // 2
                    v = vw if kind == "winkv" else vs
                    act_e.activation(v[:, tt, 0:nk], src[:, nk:w], ACT.Copy)
                    act_e.activation(s[:, 0:nk].rearrange("p (g d) -> p g d", d=HD)[:, :, ROT:],
                                     src[:, 0:nk].rearrange("p (g d) -> p g d", d=HD)[:, :, ROT:], ACT.Copy)\
                         .then_inc(staged_a, 1)
                elif kind == "gate":
                    act_e.activation(gates[:, tt, :], src[:, 0:48], ACT.Sigmoid).then_inc(staged_a, 1)
                elif kind in ("q0", "q1"):
                    act_e.activation(s[:, 0:512].rearrange("p (r b d) -> p b r d", r=4, b=2),
                                     src[:, :].rearrange("p (b r d) -> p b r d", b=2, r=4), ACT.Copy)\
                         .then_inc(staged_a, 1)
                else:
                    b = int(kind[-1])
                    act_e.activation(s.rearrange("p (r b d) -> p b r d", r=8, b=2)[:, b, :, ROT:],
                                     src[:, :].rearrange("p (r d) -> p r d", r=8)[:, :, ROT:], ACT.Copy)\
                         .then_inc(staged_a, 1)

            def take_turned(j, proj, first):
                for t, n in enumerate(range(first[j], first[j + 1])):
                    if n % 2 == 0:
                        copy_projection(act_e, n, proj[j], t)

            def copy_projection(eng, n, p, t):
                kind, _, tt, _ = p
                eng.wait_ge(turned, n + 1)
                src = bank[TBANK[n]]
                cols = slice(tt * P, tt * P + P)
                if kind == "cmpkv":
                    act_e.activation(kcvT[0:64, t, :, cols], src[0:64, :].rearrange("p (g n) -> p g n", g=4), ACT.Copy)
                    lo = 1 if tt == 0 else 0
                    act_e.activation(kcvT[64:128, t, :, tt * P + lo - 1:tt * P + P - 1],
                                     src[64:128, :].rearrange("p (g n) -> p g n", g=4)[:, :, lo:], ACT.Copy)\
                         .then_inc(moved_a, 1)
                elif kind in ("slckv", "winkv"):
                    act_e.activation((ksT if kind == "slckv" else kwT)[:, :, cols],
                                     src[:, 0:256].rearrange("p (g n) -> p g n", g=2), ACT.Copy).then_inc(moved_a, 1)
                elif kind in ("q0", "q1"):
                    pb = int(kind[-1])
                    act_e.activation((qrT if t else qT)[:, 4 * pb:4 * pb + 4, cols],
                                     src[:, :].rearrange("p (g n) -> p g n", g=4), ACT.Copy).then_inc(moved_a, 1)
                elif kind == "kv":
                    act_e.activation(ksT[:, 0, cols], src[:, 0:P], ACT.Copy).then_inc(moved_a, 1)
                else:
                    act_e.activation(qrT[:, 4 * t:4 * t + 4, cols],
                                     src[:, :].rearrange("p (g n) -> p g n", g=4), ACT.Copy).then_inc(moved_a, 1)

            def projections(proj, base, first, last):
                for m in range(len(last) + 1):
                    if m < len(last):
                        split_weights(last[m] + SPLITS)
                    if m >= 1:
                        for tt in range(NT):
                            take_turned(NT * (m - 1) + tt, proj, first)
                    if m < len(last):
                        for tt in range(NT):
                            stage_part(NT * m + tt, proj, base, first, last)
                    if m == 1 and proj is PROJ_A:
                        act_e.wait_ge(cmp_sum, 1)
                        act_e.activation(cmp_h[:, :, :, :], cmp_in, ACT.Copy).then_inc(cmp_high, 1)

            projections(PROJ_A, 0, first_a, LAST_A)

            n_cmp = AT["cmp"] + 3
            split_weights(n_cmp + SPLITS)
            act_e.wait_ge(used, n_cmp + 1)
            act_e.activation(hid[0:64, :, :].rearrange("p a b -> p (a b)"), bank[0][0:64, :], ACT.Gelu_apprx_tanh)\
                 .then_inc(cmp_act, 1)
            load_norm(0)
            split_weights(n_cmp + SPLITS + 1)
            if T_HID % 2 == 0:
                act_e.wait_ge(turned, T_HID + 1)
                for twice in range(2):
                    ins = act_e.activation(hidT.rearrange("p a c n -> p (a c) n")[:, :, 64 * twice:64 * twice + 64],
                                           bank[TBANK[T_HID]][:, 0:256].rearrange("p (g n) -> p g n", g=4), ACT.Copy)
                ins.then_inc(moved_a, 1)
            act_e.wait_ge(cmp_kv, 1)
            act_e.activation(kcT, bank[1][:, 0:P], ACT.Copy).then_inc(kc_ready, 1)

            def attention(jobs, base, first, acc_base, swa):
                accs = acc_base
                for i in range(len(jobs) + 4):
                    if i < len(jobs):
                        _, pb, b, tt, h0, nh, w, _, _ = jobs[i]
                        act_e.wait_ge(shifted, base + i + 1)
                        if i >= 3:
                            act_e.wait_ge(turned, first + i - 2)
                        for k in range(nh):
                            ins = act_e.activation(ex[:, i % 3, k * w:k * w + w], bank[i % 4][:, k * w:k * w + w],
                                                   ACT.Exp, bias=nb[:, i % 4, k:k + 1], scale=SCALE,
                                                   accum_out=sums[:, i % 4, k:k + 1])
                        if swa:
                            ins = act_e.activation(es[:, i % 4, 0:nh], sn[:, i % 4, 0:nh], ACT.Exp)
                        ins.then_inc(expd, 1)
                    if 2 <= i < len(jobs) + 2 and (first + i - 2) % 2 == 0:
                        n = first + i - 2
                        act_e.wait_ge(turned, n + 1)
                        if i >= 4:
                            act_e.wait_ge(summed, base + i - 3)
                        act_e.activation(pT[:, n % 2, :], bank[4 + n % 2][:, :], ACT.Copy).then_inc(moved_a, 1)
                    if i >= 4:
                        _, pb, b, tt, _, _, _, _, closes = jobs[i - 4]
                        if closes:
                            act_e.wait_ge(summed, base + i - 3)
                            act_e.activation(hTh[b * 64:b * 64 + 64, 4 * pb:4 * pb + 4, tt * P:tt * P + P],
                                             bank[6 + accs % 2][b * 64:b * 64 + 64, :].rearrange("p (r n) -> p r n", r=4),
                                             ACT.Copy).then_inc(heads_high, 1)
                            accs += 1

            def norm_part(k, first):
                for tt in range(NT):
                    act_e.wait_ge(var_ready, NT * k + tt + 1)
                    act_e.activation(std[:, tt, 0:1], std[:, tt, 1:2], ACT.Sqrt).then_inc(std_ready, 1)
                    if k < 3:
                        turn_h(first, tt)
                if k < 3:
                    load_norm(k + 1)

            attention(JOBS_A, 0, T_JA, 0, False)
            split_weights(AT["out_a"] + 5)
            norm_part(0, T_H1)

            for c in range(N_DENSE + 1):
                if c < N_DENSE:
                    n = AT["dense_in"] + 2 * c
                    split_weights(n + 1 + SPLITS)
                    act_e.wait_ge(used, n + 1)
                    if c >= 2:
                        act_e.wait_ge(act_low, c - 1)
                    act_e.activation(silu[:, c % 2, :], bank[2 * (c % 2)][:, :], ACT.Silu).then_inc(silu_ready, 1)
                if c >= 1:
                    act_e.wait_ge(act_ready, c)
                    act_e.activation(actTh[:, 2 * c - 2:2 * c, :],
                                     silu[:, (c - 1) % 2, :].rearrange("p (a n) -> p a n", a=2), ACT.Copy)\
                         .then_inc(act_high, 1)
            split_weights(AT["dense_out"] + N_DENSE + 1)
            norm_part(1, T_H2)
            projections(PROJ_B, len(PROJ_A), first_b, LAST_B)
            split_weights(AT["out_b"] + SPLITS)
            attention(JOBS_B, len(JOBS_A), T_JB, 8, True)
            split_weights(N_FIRST + 1)

            def split_expert(i, k):
                expert_landed(act_e, i, k)
                expert_used(act_e, i, k - SPLITS)
                n = N_FIRST + k
                act_e.activation(wh[:, n % SPLITS, :], ring[:, n % RING, :], ACT.Copy).then_inc(rounded, 1)

            norm_part(2, T_H3)
            split_weights(N_FIRST + SPLITS)
            act_e.sem_inc(e_y_a, 1)
            act_e.wait_ge(gap_ready, 1)
            act_e.activation(top[:, 5, :, :], top[:, 4, :, :], ACT.Exp).then_inc(gap_exp, 1)

            def take_rows(value):
                act_e.wait_ge(e_rows, value)
                for q in range(2):
                    ins = act_e.activation(xgTh[:, 4 * q:4 * q + 4, :],
                                           bank[2 + q][:, :].rearrange("p (c n) -> p c n", c=4), ACT.Copy)
                ins.then_inc(e_rows_high, 1)

            def expert_step(i):
                for k in range(SPLITS, PER_EXPERT + SPLITS):
                    for what, f in EXPERT_WORK.get(k, ()):
                        if what == "act":
                            expert_used(act_e, i, EXPERT.index(("g", f, 1)))
                            act_e.wait_ge(e_act, i * FT + max(f - 1, 0) + 1)
                            act_e.activation(esilu[:, f % 2, :], bank[2 * (f % 2)][:, :], ACT.Silu).then_inc(e_silu, 1)
                        elif what == "turn":
                            act_e.wait_ge(e_turned, i * FT + f + 2)
                            act_e.activation(eactTh[:, f % 2, :, :],
                                             bank[4 + f % 2][:, :].rearrange("p (c n) -> p c n", c=4), ACT.Copy)\
                                 .then_inc(e_high, 1)
                        elif what == "y":
                            expert_used(act_e, i, PER_EXPERT - 1)
                            act_e.activation(ysb[:, 0:512], bank[6][:, :], ACT.Copy).then_inc(e_y_a, 1)
                        elif what == "rows":
                            take_rows(i + 2)
                    split_expert(i, k)

            take_rows(1)
            act_e.wait_ge(plan_ready, 1)
            steps = act_e.value_load(turns_i[0:1, 0:1], min_val=NE, max_val=2 * NE)
            with act_e.Fori(0, steps) as i:
                expert_step(i)
            norm_part(3, None)

        @block.tensor
        def _(pe):
            def ready(n):
                pe.wait_ge(split, n + 1)

            def part(n, tile, size=UNIT):
                return tile[:, n % SPLITS, 0:size]

            def product(out_, lhs, rhs, start, stop):
                (lh, ll), (rh, rl) = lhs, rhs
                pe.matmul(out_, lh, rh, start=start, stop=False, skip_group_check=True)
                pe.matmul(out_, ll, rh, start=False, stop=False, skip_group_check=True)
                return pe.matmul(out_, lh, rl, start=False, stop=stop, skip_group_check=True)

            def both(n, depth, size=UNIT):
                return [part(n, tile, size).rearrange("p (c n) -> p c n", c=depth) for tile in (wh, wl)]

            def turn(n, sources):
                before = [m for m in range(n) if TBANK[m] == TBANK[n]]
                if before:
                    moved(pe, before[-1])
                b = bank[TBANK[n]]
                at = 0
                for src in sources:
                    rows, cols = src.shape[0], 1
                    ins = pe.transpose(b[:, at:at + rows], src, ident[0:rows, 0:rows])
                    at += rows
                ins.then_inc(turned, 1)

            def turn_h(first):
                for n in range(4):
                    tt, q = n // 2, n % 2
                    turn(first + n, [h[:, tt, (4 * q + c) * P:(4 * q + c + 1) * P] for c in range(4)])

            pe.wait_ge(ident_ready, 1)
            pe.wait_ge(x_landed, 16)
            turn_h(T_X)
            pe.wait_ge(small_landed, 16 * 7)
            for kv in range(2):
                ins = pe.transpose(bank[3][:, 16 * kv:16 * kv + 16], posr[:, kv, :], ident[0:16, 0:16])
            ins.then_inc(post, 1)
            moved(pe, T_X + 3)

            def project(m, proj, base, last):
                _, _, _, w = proj[NT * m]
                first_item = (last[m - 1] if m else last[0] - (1 if w == 512 else 0) - 1) + 1
                depth = 4 if w == 512 else DC
                if base + NT * m == NT:
                    pe.wait_ge(post_moved, 1)
                if base + NT * m >= 4:
                    pe.wait_ge(staged_v, base + NT * m - 2)
                for n in range(first_item, last[m] + 1):
                    ready(n)
                    wts = both(n, depth, DC * w if w < 256 else UNIT)
                    for tt in range(NT):
                        for c in range(depth):
                            cc_ = (n - first_item) * depth + c
                            lhs = [t[:, cc_, tt * P:tt * P + P] for t in (hTh, hTl)]
                            ins = product(bank[(NT * m + tt) % 4][:, 0:w], lhs, [t[:, c, :] for t in wts],
                                          cc_ == 0, cc_ == DC - 1)
                    ins.then_inc(used, 1)

            def turn_projection(j, proj, base, first):
                kind, _, tt, w = proj[j]
                pe.wait_ge(staged_a, base + j + 1)
                pe.wait_ge(staged_v, base + j + 1)
                s = stage[:, j % 2, :]
                if kind == "cmpkv":
                    for kv in range(2):
                        turn(first[j] + kv, [s[:, (4 * kv + g) * P:(4 * kv + g + 1) * P] for g in range(4)])
                elif kind in ("slckv", "winkv"):
                    turn(first[j], [s[:, g * P:(g + 1) * P] for g in range(2)])
                elif kind in ("q0", "q1"):
                    for t in range(2):
                        turn(first[j] + t, [s[:, 512 * t + r * P:512 * t + (r + 1) * P] for r in range(4)])
                elif kind == "kv":
                    turn(first[j], [s[:, 0:P]])
                elif kind == "qb1":
                    for t in range(2):
                        turn(first[j] + t, [s[:, (4 * t + r) * P:(4 * t + r + 1) * P] for r in range(4)])

            def projections(proj, base, first, last):
                for m in range(len(last) + 1):
                    if m < len(last):
                        project(m, proj, base, last)
                    if m >= 1:
                        for tt in range(NT):
                            turn_projection(NT * (m - 1) + tt, proj, base, first)

            projections(PROJ_A, 0, first_a, LAST_A)

            pe.wait_ge(cmp_low, 1)
            for kv in range(2):
                for k in range(2):
                    n = AT["cmp"] + 2 * kv + k
                    ready(n)
                    wts = both(n, 8)
                    for j in range(8):
                        ins = product(bank[0][0:64, 256 * kv:256 * kv + 256],
                                      [t[:, kv, 8 * k + j, :] for t in (cmp_h, cmp_l)], [t[:, j, :] for t in wts],
                                      (k == 0 and j == 0), (k == 1 and j == 7))
                    ins.then_inc(used, 1)
            pe.wait_ge(cmp_act, 1)
            turn(T_HID, [hid[0:64, kv, c * P:c * P + P] for kv in range(2) for c in range(2)])
            moved(pe, T_HID)
            for c in range(2):
                pe.matmul(bank[1][:, 0:P], w2[:, 0, c, :, :].rearrange("p a d -> p (a d)"), hidT[:, 0, c, :],
                          start=(c == 0), stop=(c == 1))
            for c in range(2):
                ins = pe.matmul(bank[1][:, P:2 * P], hidT[:, 1, c, :], w2[:, 1, c, :, :].rearrange("p a d -> p (a d)"),
                                start=(c == 0), stop=(c == 1))
            ins.then_inc(cmp_kv, 1)

            def attention(jobs, base, first, acc_base):
                accs = acc_base
                for i in range(len(jobs) + 3):
                    if i < len(jobs):
                        br, pb, b, tt, h0, nh, w, _, _ = jobs[i]
                        if base + i >= 4:
                            pe.wait_ge(expd, base + i - 3)
                        sc = bank[i % 4]
                        if br == "cmp":
                            mask = cmpmask[:, tt, 2 * pb + b, :]
                        else:
                            m = window if br == "swa" else causal
                            mask = m[:, 1, :] if tt == 0 else m[:, :, :].rearrange("p a n -> p (a n)")
                        mask = mask.rearrange("p (a n) -> p a n", a=1).to_broadcast([P, nh, w])
                        pe.matmul(sc[:, :], identb[:, :], mask, start=True, stop=False, skip_group_check=True)
                        q = qT if br == "cmp" else qrT
                        half = slice(64 * b, 64 * b + 64)
                        keys = {"cmp": kcT[half, :], "slc": ksT[half, pb, 0:w], "win": kwT[half, pb, 0:w],
                                "swa": ksT[half, 0, 0:w]}[br]
                        for k in range(nh):
                            ins = pe.matmul(sc[:, k * w:k * w + w], q[half, 4 * pb + h0 + k, tt * P:tt * P + P], keys,
                                            start=False, stop=(k == nh - 1), skip_group_check=True)
                        ins.then_inc(scored, 1)
                    if 2 <= i < len(jobs) + 2:
                        pe.wait_ge(normed, base + i - 1)
                        turn(first + i - 2, [ex[:, (i - 2) % 3, c * P:c * P + P] for c in range(4)])
                    if i >= 3:
                        br, pb, b, tt, h0, nh, w, opens, closes = jobs[i - 3]
                        n = first + i - 3
                        moved(pe, n)
                        if opens and accs >= 2:
                            pe.wait_ge(heads_out, accs - 1)
                        acc = bank[6 + accs % 2]
                        v = {"cmp": vc, "slc": vs, "win": vw, "swa": vs}[br]
                        cols = slice(0, P) if br in ("cmp", "swa") else slice(P * pb, P * pb + P)
                        if w == P:
                            lhs = v if br == "cmp" else v[:, 0, cols]
                            ins = pe.matmul(acc[:, :], lhs, pT[:, n % 2, :], start=opens, stop=closes,
                                            skip_group_check=True)
                        else:
                            p4 = pT[:, n % 2, :].rearrange("p (k c n) -> p c k n", k=2, c=2)
                            for c in range(2):
                                ins = pe.matmul(acc[:, h0 * P:h0 * P + 2 * P], v[:, c, cols], p4[:, c, :, :],
                                                start=(opens and c == 0), stop=(closes and c == 1),
                                                skip_group_check=True)
                        ins.then_inc(summed, 1)
                        accs += closes

            def mix_out(n0, heads):
                pe.wait_ge(heads_out, heads)
                for half, k, tt in [(0, k, tt) for k in range(2) for tt in range(NT)] +\
                        [(1, k, tt) for tt in range(NT) for k in range(2)]:
                    n = n0 + 2 * half + k
                    if tt == 0:
                        ready(n)
                    wts = both(n, 4)
                    for r in range(4):
                        lhs = [t[:, 4 * k + r, tt * P:tt * P + P] for t in (hTh, hTl)]
                        ins = product(bank[2 * half + tt][:, :], lhs, [t[:, r, :] for t in wts],
                                      (k == 0 and r == 0), (k == 1 and r == 3))
                    if tt == NT - 1:
                        ins.then_inc(used, 1)
                    elif half == 1 and k == 1:
                        ins.then_inc(mixed, 1)

            def next_h(k, first):
                for n in range(4):
                    pe.wait_ge(h_ready, 4 * k + n + 1)
                    tt, q = n // 2, n % 2
                    turn(first + n, [h[:, tt, (4 * q + c) * P:(4 * q + c + 1) * P] for c in range(4)])
                moved(pe, first + 3)

            pe.wait_ge(kc_ready, 1)
            pe.wait_ge(vc_ready, 1)
            attention(JOBS_A, 0, T_JA, 0)
            mix_out(AT["out_a"], 8)
            next_h(0, T_H1)

            for c in range(N_DENSE):
                if c >= 2:
                    pe.wait_ge(act_ready, c - 1)
                for gu in range(2):
                    n = AT["dense_in"] + 2 * c + gu
                    ready(n)
                    wts = both(n, DC)
                    for j in range(2):
                        for k in range(DC):
                            ins = product(bank[2 * (c % 2) + gu][:, 256 * j:256 * j + 256],
                                          [t[:, k, P * j:P * j + P] for t in wts], [t[:, k, :] for t in (hTh, hTl)],
                                          k == 0, k == DC - 1)
                    ins.then_inc(used, 1)
            moved(pe, T_H1 + 3)
            for c, tt in [(c, tt) for c in range(N_DENSE - 2) for tt in range(NT)] +\
                    [(c, tt) for tt in range(NT) for c in range(N_DENSE - 2, N_DENSE)]:
                n = AT["dense_out"] + c
                if tt == 0:
                    ready(n)
                    pe.wait_ge(act_low, c + 1)
                wts = both(n, 2)
                for j in range(2):
                    for half in range(2):
                        ins = product(bank[4 + 2 * half + tt][:, :],
                                      [t[:, 2 * c + j, tt * P:tt * P + P] for t in (actTh, actTl)],
                                      [t[:, j, 512 * half:512 * half + 512] for t in wts],
                                      (c == 0 and j == 0), (c == N_DENSE - 1 and j == 1))
                if tt == NT - 1:
                    ins.then_inc(used, 1)
                elif c == N_DENSE - 1:
                    ins.then_inc(mixed, 1)
            next_h(1, T_H2)

            projections(PROJ_B, len(PROJ_A), first_b, LAST_B)
            moved(pe, T_JB - 1)
            moved(pe, T_JB - 2)
            attention(JOBS_B, len(JOBS_A), T_JB, 8)
            mix_out(AT["out_b"], 16)
            next_h(2, T_H3)

            pe.wait_ge(router_low, 1)
            for c in range(DC):
                ins = product(bank[6][0:NE, 0:SEQ], [t[:, c, :] for t in (routerh, routerl)],
                              [t[:, c, :] for t in (hTh, hTl)], c == 0, c == DC - 1)
            ins.then_inc(routed, 1)
            pe.wait_ge(logits_moved, 1)
            for tt in range(NT):
                ins = pe.transpose(bank[6][:, 256 + NE * tt:256 + NE * tt + NE], lgT[:, tt * P:tt * P + P],
                                   ident[0:NE, 0:NE])
            ins.then_inc(routed, 1)
            pe.wait_ge(sel_ready, 1)
            pe.matmul(bank[7][:, 0:NE], earlier[:, :], selb[:, 0, :], start=True, stop=True)
            pe.matmul(bank[7][:, NE:2 * NE], onesb[:, :], selb[:, 0, :], start=True, stop=False)
            pe.matmul(bank[7][:, NE:2 * NE], earlier[:, :], selb[:, 1, :], start=False, stop=True)
            pe.matmul(bank[7][:, 2 * NE:3 * NE], onesb[:, :], selb[:, 0, :], start=True, stop=False)
            pe.matmul(bank[7][:, 2 * NE:3 * NE], onesb[:, :], selb[:, 1, :], start=False, stop=True)\
              .then_inc(ranked, 1)

            def gather(value):
                pe.wait_ge(e_pick, value)
                for c in range(DC):
                    for tt in range(NT):
                        ins = pe.matmul(bank[2 + c // 4][:, (c % 4) * P:(c % 4) * P + P], h[:, tt, c * P:c * P + P],
                                        pick[:, tt, :], start=(tt == 0), stop=(tt == NT - 1))
                ins.then_inc(e_rows, 1)

            def scatter(v, n):
                if n == 0:
                    pe.wait_ge(e_putT_moved, v)
                    pe.wait_ge(e_y_a, v)
                    pe.wait_ge(e_y_v, v)
                tt, half = n // 2, n % 2
                if n >= 2:
                    pe.wait_ge(e_added, 4 * v + n - 4)
                pe.matmul(bank[4 + n % 2][:, :], putT[:, tt, :], ysb[:, 512 * half:512 * half + 512],
                          start=True, stop=True).then_inc(e_back, 1)

            pe.sem_inc(e_turned, 1)
            pe.sem_inc(e_putT, 1)
            gather(1)
            pe.wait_ge(plan_ready, 1)
            steps = pe.value_load(turns_i[0:1, 0:1], min_val=NE, max_val=2 * NE)
            with pe.Fori(0, steps) as i:
                for k, (kind, f, half) in enumerate(EXPERT):
                    n = N_FIRST + k
                    if k == 0:
                        pe.wait_ge(e_rows_low, i + 1)
                    if kind == "g" and half == 0:
                        pe.wait_ge(e_act, i * FT + max(f - 1, 0) + 1)
                    if kind == "o" and half == 0:
                        pe.wait_ge(e_low, i * FT + f + 1)
                    pe.wait_ge(split, n + 1 + PER_EXPERT * i)
                    if kind == "o":
                        wts = both(n, 2)
                        for j in range(2):
                            for side in range(2):
                                ins = product(bank[6 + side][:, :],
                                              [t[:, f % 2, 2 * half + j, :] for t in (eactTh, eactTl)],
                                              [t[:, j, 512 * side:512 * side + 512] for t in wts],
                                              (f == 0 and half == 0 and j == 0), (f == FT - 1 and half == 1 and j == 1))
                    else:
                        wts = both(n, 4)
                        for c in range(4):
                            ins = product(bank[2 * (f % 2) + (kind == "u")][:, :],
                                          [t[:, 4 * half + c, :] for t in (xgTh, xgTl)], [t[:, c, :] for t in wts],
                                          (half == 0 and c == 0), (half == 1 and c == 3))
                    ins.then_inc(used, 1)
                    if k in BACK_AFTER:
                        for m in range(2):
                            scatter(i + 1, 2 * BACK_AFTER.index(k) + m)
                    if k in TURN_AFTER:
                        t = TURN_AFTER.index(k)
                        pe.wait_ge(e_act, i * FT + t + 2)
                        if t < 2:
                            pe.wait_ge(e_added, 4 * i + 5)
                        else:
                            pe.wait_ge(e_low, i * FT + t - 1)
                        for j in range(4):
                            ins = pe.transpose(bank[4 + t % 2][:, j * P:j * P + P], act[:, t % 2, j * P:j * P + P],
                                               ident[:, :])
                        ins.then_inc(e_turned, 1)
                        if t == FT - 1:
                            pe.wait_ge(e_put, i + 1)
                            for tt in range(NT):
                                ins = pe.transpose(bank[5][:, tt * P:tt * P + P], put[:, tt, :], ident[:, :])
                            ins.then_inc(e_putT, 1)
                            gather(i + 2)
            for n in range(4):
                scatter(steps + 1, n)

        @block.vector
        def _(dve):
            n_step = [0]

            def step(ins):
                n_step[0] += 1
                ins.then_inc(dve_step, 1)
                dve.wait_ge(dve_step, n_step[0])

            n_split = [0]

            def split_weights(upto):
                for n in range(n_split[0], upto):
                    dve.wait_ge(rounded, n + 1)
                    size = size_of(n)
                    dve.tensor_tensor(wl[:, n % SPLITS, 0:size], ring[:, n % RING, 0:size],
                                      wh[:, n % SPLITS, 0:size].bitcast(F32), ALU.subtract).then_inc(split, 1)
                n_split[0] = max(n_split[0], upto)

            n_high = [0]

            def turn_h(first):
                for n in range(4):
                    tt, q = n // 2, n % 2
                    n_high[0] += 1
                    dve.wait_ge(high, n_high[0])
                    there = (slice(None), slice(4 * q, 4 * q + 4), slice(tt * P, tt * P + P))
                    dve.tensor_tensor(hTl[there], bank[TBANK[first + n]][:, :].rearrange("p (c n) -> p c n", c=4),
                                      hTh[there].bitcast(F32), ALU.subtract).then_inc(moved_v, 1)

            turn_h(T_X)
            split_weights(SPLITS)

            dve.wait_ge(pos_landed, 16)
            dve.wait_ge(consts, 2)
            step(dve.tensor_copy(pos_f[:, :], pos_i[:, :]))
            for tt in range(NT):
                step(dve.tensor_scalar(ang[:, 0, tt, :], freq[:, :], pos_f[:, tt:tt + 1], None, ALU.mult))
            a, turns, r = ang[:, 0, :, :], ang[:, 1, :, :], ang[:, 2, :, :]
            step(dve.tensor_scalar(turns, a, 0.15915494309189535, 12582912.0, ALU.mult, ALU.add))
            step(dve.tensor_scalar(turns, turns, 12582912.0, None, ALU.subtract))
            for part in TWO_PI_PARTS:
                step(dve.scalar_tensor_tensor(out=a, in0=turns, scalar=-part, in1=a, op0=ALU.mult, op1=ALU.add))
            step(dve.tensor_scalar(turns, a, 3.1415925, -3.1415925, ALU.min, ALU.max))
            step(dve.tensor_scalar(r, turns, -1.0, None, ALU.mult))
            step(dve.tensor_tensor(r, turns, r, ALU.max))
            dve.tensor_scalar(r, r, -1.0, 1.5707963267948966, ALU.mult, ALU.add).then_inc(trig_in, 1)
            dve.wait_ge(trig, 2)
            dve.tensor_copy(cc[:, :, 8:16], cc[:, :, 0:8])
            step(dve.tensor_scalar(ss[:, :, 8:16], ss[:, :, 0:8], -1.0, None, ALU.mult))
            dve.wait_ge(post, 1)
            dve.tensor_copy(posT[:, :, :], bank[3][:, 0:32].rearrange("p (v j) -> p v j", v=2)).then_inc(post_moved, 1)
            dve.wait_ge(small_landed, 16 * 7)
            step(dve.tensor_scalar(nsink[:, :], sink[:, :], -1.0, None, ALU.mult))
            dve.wait_ge(router_high, 1)
            dve.tensor_tensor(routerl[:, :, :], router[:, :, :], routerh[:, :, :].bitcast(F32), ALU.subtract)\
               .then_inc(router_low, 1)

            def rotate(src, dst, tt, heads):
                wide = [P, heads, ROT]
                c = cc[:, tt, :].rearrange("p (a n) -> p a n", a=1).to_broadcast(wide)
                s = ss[:, tt, :].rearrange("p (a n) -> p a n", a=1).to_broadcast(wide)
                dve.tensor_tensor(rot1[:, 0:heads, :], src, c, ALU.mult)
                step(dve.tensor_tensor(rot2[:, 0:heads, :], src, s, ALU.mult))
                dve.tensor_tensor(dst[..., 0:8], rot1_of(dst, heads, 0), rot2_of(dst, heads, 8), ALU.add)
                return dve.tensor_tensor(dst[..., 8:16], rot1_of(dst, heads, 8), rot2_of(dst, heads, 0), ALU.add)

            def rot1_of(dst, heads, at):
                v = rot1[:, 0:heads, at:at + 8]
                return v.rearrange("p (b r) d -> p b r d", b=2) if len(dst.shape) == 4 else v

            def rot2_of(dst, heads, at):
                v = rot2[:, 0:heads, at:at + 8]
                return v.rearrange("p (b r) d -> p b r d", b=2) if len(dst.shape) == 4 else v

            def stage_part(j, proj, base, nturn):
                kind, _, tt, w = proj[j]
                if j >= 1:
                    dve.wait_ge(staged_v, base + j)
                dve.wait_ge(staged_a, base + j + 1)
                src = bank[j % 4]
                s = stage[:, j % 2, :]
                if j >= 2:
                    dve.wait_ge(turned, nturn[j - 1])
                if kind == "cmpkv":
                    dve.tensor_copy(s.rearrange("p (g a d) -> p g a d", g=8, a=2)[:, :, 1, :],
                                    src[:, :].rearrange("p (g d) -> p g d", g=8)).then_inc(staged_v, 1)
                elif kind in ("slckv", "winkv", "kv"):
                    nk = w // 2
                    rotate(src[:, 0:nk].rearrange("p (g d) -> p g d", d=HD)[:, :, 0:ROT],
                           s[:, 0:nk].rearrange("p (g d) -> p g d", d=HD)[:, :, 0:ROT], tt, nk // HD)\
                        .then_inc(staged_v, 1)
                elif kind == "gate":
                    dve.tensor_scalar(gates[:, tt, 0:16], gates[:, tt, 0:16], seen[:, tt:tt + 1], None, ALU.mult)\
                       .then_inc(staged_v, 1)
                elif kind in ("q0", "q1"):
                    dst = s[:, 512:1024].rearrange("p (r b d) -> p b r d", r=4, b=2)
                    dve.tensor_copy(dst[:, :, :, ROT:],
                                    src[:, :].rearrange("p (b r d) -> p b r d", b=2, r=4)[:, :, :, ROT:])
                    rotate(src[:, :].rearrange("p (r d) -> p r d", r=8)[:, :, 0:ROT], dst[:, :, :, 0:ROT], tt, 8)\
                        .then_inc(staged_v, 1)
                else:
                    b = int(kind[-1])
                    rotate(src[:, :].rearrange("p (r d) -> p r d", r=8)[:, :, 0:ROT],
                           s.rearrange("p (r b d) -> p b r d", r=8, b=2)[:, b, :, 0:ROT], tt, 8).then_inc(staged_v, 1)

            def take_turned(j, proj, first):
                kind, _, tt, _ = proj[j]
                cols = slice(tt * P, tt * P + P)
                for t, n in enumerate(range(first[j], first[j + 1])):
                    if n % 2 == 0:
                        continue
                    dve.wait_ge(turned, n + 1)
                    src = bank[TBANK[n]]
                    four = src[:, :].rearrange("p (g n) -> p g n", g=4)
                    if kind == "cmpkv":
                        lo = 1 if tt == 0 else 0
                        dve.tensor_copy(kcvT[0:64, t, :, cols], four[0:64])
                        ins = dve.tensor_copy(kcvT[64:128, t, :, tt * P + lo - 1:tt * P + P - 1], four[64:128, :, lo:])
                    elif kind in ("slckv", "winkv"):
                        ins = dve.tensor_copy((ksT if kind == "slckv" else kwT)[:, :, cols],
                                              src[:, 0:256].rearrange("p (g n) -> p g n", g=2))
                    elif kind in ("q0", "q1"):
                        pb = int(kind[-1])
                        ins = dve.tensor_copy((qrT if t else qT)[:, 4 * pb:4 * pb + 4, cols], four)
                    elif kind == "kv":
                        ins = dve.tensor_copy(ksT[:, 0, cols], src[:, 0:P])
                    else:
                        ins = dve.tensor_copy(qrT[:, 4 * t:4 * t + 4, cols], four)
                    ins.then_inc(moved_v, 1)

            def build_cmp_in():
                moved(dve, first_a[2] - 1)
                moved(dve, first_a[2] - 2)
                for kv in range(2):
                    for g in range(4):
                        by_row = kcvT[:, kv, g, :].rearrange("p (n s two) -> p s n two", s=8, two=2)[:, :, :, 0]
                        for upper in range(2):
                            pos = posT[:, kv, 8 * upper:8 * upper + 8].rearrange("p (j n) -> p j n", n=1)\
                                .to_broadcast([P, 8, N_CMP])
                            ins = dve.tensor_tensor(cmp_in[:, kv, 8 * upper:8 * upper + 8, 16 * g:16 * g + N_CMP],
                                                    by_row[:, :, upper:upper + N_CMP], pos, ALU.add)
                ins.then_inc(cmp_sum, 1)

            def projections(proj, base, first, last):
                for m in range(len(last) + 1):
                    if m < len(last):
                        split_weights(last[m] + SPLITS)
                    if m >= 1:
                        for tt in range(NT):
                            take_turned(NT * (m - 1) + tt, proj, first)
                    if m < len(last):
                        for tt in range(NT):
                            stage_part(NT * m + tt, proj, base, first)
                    if proj is PROJ_A:
                        if m == 1:
                            build_cmp_in()
                        if m == 2:
                            dve.wait_ge(cmp_high, 1)
                            dve.tensor_tensor(cmp_l[:, :, :, :], cmp_in, cmp_h[:, :, :, :].bitcast(F32), ALU.subtract)\
                               .then_inc(cmp_low, 1)

            projections(PROJ_A, 0, first_a, LAST_A)
            split_weights(AT["cmp"] + 3 + SPLITS + 1)
            if T_HID % 2:
                dve.wait_ge(turned, T_HID + 1)
                for twice in range(2):
                    ins = dve.tensor_copy(hidT.rearrange("p a c n -> p (a c) n")[:, :, 64 * twice:64 * twice + 64],
                                          bank[TBANK[T_HID]][:, 0:256].rearrange("p (g n) -> p g n", g=4))
                ins.then_inc(moved_v, 1)
            dve.wait_ge(kc_ready, 1)
            dve.tensor_copy(vc, bank[1][:, P:2 * P]).then_inc(vc_ready, 1)

            def attention(jobs, base, first, swa, heads):
                for i in range(len(jobs) + 4):
                    if i < len(jobs):
                        br, pb, b, tt, h0, nh, w, _, _ = jobs[i]
                        dve.wait_ge(scored, base + i + 1)
                        step(dve.tensor_reduce(mx[:, i % 4, 0:nh], bank[i % 4][:, :].rearrange("p (k n) -> p k n", k=nh),
                                               X, ALU.max))
                        if swa:
                            h_at = 8 * b + 4 * pb + h0
                            step(dve.scalar_tensor_tensor(out=nb[:, i % 4, 0:nh], in0=mx[:, i % 4, 0:nh], scalar=-SCALE,
                                                          in1=nsink[:, h_at:h_at + nh], op0=ALU.mult, op1=ALU.min))
                            dve.tensor_tensor(sn[:, i % 4, 0:nh], sink[:, h_at:h_at + nh], nb[:, i % 4, 0:nh], ALU.add)\
                               .then_inc(shifted, 1)
                        else:
                            dve.tensor_scalar(nb[:, i % 4, 0:nh], mx[:, i % 4, 0:nh], -SCALE, None, ALU.mult)\
                               .then_inc(shifted, 1)
                    if 1 <= i <= len(jobs):
                        br, pb, b, tt, h0, nh, w, _, _ = jobs[i - 1]
                        m = (i - 1) % 4
                        dve.wait_ge(expd, base + i)
                        if swa:
                            step(dve.tensor_tensor(sums[:, m, 0:nh], sums[:, m, 0:nh], es[:, m, 0:nh], ALU.add))
                        step(dve.reciprocal(rg[:, m, 0:nh], sums[:, m, 0:nh]))
                        if not swa:
                            g_at = 16 * ("cmp", "slc", "win").index(br) + 4 * (2 * pb + b) + h0
                            step(dve.tensor_tensor(rg[:, m, 0:nh], rg[:, m, 0:nh], gates[:, tt, g_at:g_at + nh], ALU.mult))
                        e = ex[:, (i - 1) % 3, :].rearrange("p (k n) -> p k n", k=nh)
                        dve.tensor_tensor(e, e, rg[:, m, 0:nh].rearrange("p (k n) -> p k n", n=1).to_broadcast([P, nh, w]),
                                          ALU.mult).then_inc(normed, 1)
                    if 2 <= i < len(jobs) + 2 and (first + i - 2) % 2:
                        n = first + i - 2
                        dve.wait_ge(turned, n + 1)
                        if i >= 4:
                            dve.wait_ge(summed, base + i - 3)
                        dve.tensor_copy(pT[:, 1, :], bank[5][:, :]).then_inc(moved_v, 1)
                    if i >= 4 and jobs[i - 4][8]:
                        _, pb, b, tt, _, _, _, _, _ = jobs[i - 4]
                        heads += 1
                        dve.wait_ge(heads_high, heads)
                        there = (slice(64 * b, 64 * b + 64), slice(4 * pb, 4 * pb + 4), slice(tt * P, tt * P + P))
                        dve.tensor_tensor(hTl[there], bank[6 + (heads - 1) % 2][64 * b:64 * b + 64, :]
                                          .rearrange("p (r n) -> p r n", r=4), hTh[there].bitcast(F32), ALU.subtract)\
                           .then_inc(heads_out, 1)

            def chained(ins):
                n_step[0] += 1
                ins.then_inc(dve_step, 1)

            def add_mix(b, tt, half):
                cols = slice(512 * half, 512 * half + 512)
                step(dve.scalar_tensor_tensor(out=pre[:, tt, cols], in0=h[:, tt, cols], scalar=ALPHA,
                                              in1=bank[b][:, :], op0=ALU.mult, op1=ALU.add))
                chained(dve.bn_stats(stats[:, tt, half, :], pre[:, tt, cols]))

            def center(tt):
                dve.wait_ge(dve_step, n_step[0])
                step(dve.bn_aggr(mv[:, tt, :], stats[:, tt, :, :].rearrange("p a b -> p (a b)")))
                dve.tensor_scalar(std[:, tt, 1:2], mv[:, tt, 1:2], LN_EPS, None, ALU.add).then_inc(var_ready, 1)
                chained(dve.scalar_tensor_tensor(out=pre[:, tt, :], in0=pre[:, tt, :], scalar=mv[:, tt, 0:1],
                                                 in1=lnp[:, 0, :], op0=ALU.subtract, op1=ALU.mult))

            def scale(k, tt):
                dve.wait_ge(std_ready, NT * k + tt + 1)
                step(dve.reciprocal(std[:, tt, 1:2], std[:, tt, 0:1]))
                for q in range(2):
                    cols = slice(512 * q, 512 * q + 512)
                    dve.scalar_tensor_tensor(out=h[:, tt, cols], in0=pre[:, tt, cols], scalar=std[:, tt, 1:2],
                                             in1=lnp[:, 1, cols], op0=ALU.mult, op1=ALU.add).then_inc(h_ready, 1)

            def norm(k, after, banks, early, first):
                if early is not None:
                    dve.wait_ge(used, early + 1)
                    for tt in range(NT):
                        add_mix(banks[0][tt], tt, 0)
                split_weights(after + 2)
                dve.wait_ge(ln_landed, 32 * (k + 1))
                left = range(2) if early is None else (1,)
                dve.wait_ge(mixed, k + 1)
                for half in left:
                    add_mix(banks[half][0], 0, half)
                center(0)
                scale(k, 0)
                dve.wait_ge(used, after + 1)
                for half in left:
                    add_mix(banks[half][1], 1, half)
                center(1)
                scale(k, 1)
                turn_h(first)

            attention(JOBS_A, 0, T_JA, False, 0)
            split_weights(AT["out_a"] + 4)
            norm(0, AT["out_a"] + 3, ((0, 1), (2, 3)), AT["out_a"] + 1, T_H1)
            for c in range(N_DENSE + 1):
                if c < N_DENSE:
                    n = AT["dense_in"] + 2 * c + 1
                    split_weights(n + SPLITS)
                    dve.wait_ge(silu_ready, c + 1)
                    dve.wait_ge(used, n + 1)
                    dve.tensor_tensor(silu[:, c % 2, :], silu[:, c % 2, :], bank[2 * (c % 2) + 1][:, :], ALU.mult)\
                       .then_inc(act_ready, 1)
                if c >= 1:
                    dve.wait_ge(act_high, c)
                    there = (slice(None), slice(2 * c - 2, 2 * c), slice(None))
                    dve.tensor_tensor(actTl[there], silu[:, (c - 1) % 2, :].rearrange("p (a n) -> p a n", a=2),
                                      actTh[there].bitcast(F32), ALU.subtract).then_inc(act_low, 1)
            norm(1, AT["dense_out"] + N_DENSE - 1, ((4, 5), (6, 7)), None, T_H2)
            projections(PROJ_B, len(PROJ_A), first_b, LAST_B)
            split_weights(AT["out_b"] + SPLITS)
            attention(JOBS_B, len(JOBS_A), T_JB, True, 8)
            split_weights(N_FIRST)
            norm(2, AT["out_b"] + 3, ((0, 1), (2, 3)), AT["out_b"] + 1, T_H3)
            split_weights(N_FIRST + SPLITS)

            def build_pick(at, value):
                if value is not None:
                    dve.wait_ge(e_rows, value)
                for tt in range(NT):
                    ins = dve.tensor_scalar(pick[:, tt, :], slots[:, :], slotx[:, tt, at], None, ALU.is_equal)
                ins.then_inc(e_pick, 1)

            logits, best, pick1, rest, pick2, sel, gw, tmp = (lg[:, k, :, :] for k in range(8))
            wide = [P, NT, NE]
            m1, x1, m2, x2 = (top[:, k, :, :] for k in range(4))
            gap, egap, g1, g2, den = (top[:, k, :, :] for k in range(4, 9))
            dve.wait_ge(routed, 1)
            dve.tensor_copy(lgT[:, :], bank[6][0:NE, 0:SEQ]).then_inc(logits_moved, 1)
            dve.wait_ge(routed, 2)
            step(dve.tensor_copy(logits, bank[6][:, 256:256 + NT * NE].rearrange("p (t e) -> p t e", t=NT)))

            def pick_largest(values, m, x_, onehot):
                step(dve.tensor_reduce(m, values, X, ALU.max))
                step(dve.tensor_tensor(best, values, m.to_broadcast(wide), ALU.is_equal))
                step(dve.tensor_tensor(best, best, order[:, :, :], ALU.mult))
                step(dve.tensor_reduce(x_, best, X, ALU.max))
                step(dve.tensor_tensor(onehot, best, x_.to_broadcast(wide), ALU.is_equal))

            pick_largest(logits, m1, x1, pick1)
            step(dve.scalar_tensor_tensor(out=rest, in0=pick1, scalar=NEG, in1=logits, op0=ALU.mult, op1=ALU.add))
            pick_largest(rest, m2, x2, pick2)
            dve.tensor_tensor(gap, m2, m1, ALU.subtract).then_inc(gap_ready, 1)
            step(dve.tensor_tensor(sel, pick1, pick2, ALU.add))
            dve.tensor_copy(selb[:, :, :], sel).then_inc(sel_ready, 1)
            dve.wait_ge(gap_exp, 1)
            step(dve.tensor_scalar(den, egap, 1.0, None, ALU.add))
            step(dve.reciprocal(g1, den))
            step(dve.tensor_tensor(g2, egap, g1, ALU.mult))
            step(dve.tensor_tensor(gw, pick1, g1.to_broadcast(wide), ALU.mult))
            step(dve.tensor_tensor(tmp, pick2, g2.to_broadcast(wide), ALU.mult))
            dve.tensor_tensor(gatex[:, :, 0:NE], gw, tmp, ALU.add)
            step(dve.tensor_tensor(gatex[:, :, NE:2 * NE], gw, tmp, ALU.add))
            dve.wait_ge(ranked, 1)
            step(dve.tensor_scalar(tmp, bank[7][:, 0:NT * NE].rearrange("p (t e) -> p t e", t=NT), 1.0, None, ALU.add))
            step(dve.tensor_tensor(tmp, tmp, sel, ALU.mult))
            step(dve.tensor_scalar(slotx[:, :, 0:NE], tmp, -1.0, None, ALU.add))
            build_pick(slice(0, 1), None)
            step(dve.tensor_scalar(slotx[:, :, NE:2 * NE], tmp, -1.0 - P, None, ALU.add))
            step(dve.tensor_reduce(cnt[:, 0:1], bank[7][:, 2 * NE:3 * NE], X, ALU.max))
            step(dve.tensor_scalar(cnt[:, 1:2], cnt[:, 0:1], float(P), None, ALU.is_gt))
            dve.tensor_scalar(turns_i[:, :], cnt[:, 1:2], float(NE), float(NE), ALU.mult, ALU.add)\
               .then_inc(plan_ready, 1)

            def take_rows(value):
                dve.wait_ge(e_rows_high, value)
                for q in range(2):
                    there = (slice(None), slice(4 * q, 4 * q + 4), slice(None))
                    ins = dve.tensor_tensor(xgTl[there], bank[2 + q][:, :].rearrange("p (c n) -> p c n", c=4),
                                            xgTh[there].bitcast(F32), ALU.subtract)
                ins.then_inc(e_rows_low, 1)

            def add_back(v, parts):
                dve.wait_ge(e_added, 4 * v - 3)
                for n in parts:
                    tt, half = n // 2, n % 2
                    dve.wait_ge(e_back, 4 * v + n - 3)
                    cols = slice(512 * half, 512 * half + 512)
                    dve.tensor_tensor(pre[:, tt, cols], pre[:, tt, cols], bank[4 + n % 2][:, :], ALU.add)\
                       .then_inc(e_added, 1)

            dve.memset(putT, 0.0).then_inc(e_putT_moved, 1)
            dve.memset(ysb, 0.0).then_inc(e_y_v, 1)
            dve.sem_inc(e_act, 1)
            take_rows(1)
            dve.wait_ge(plan_ready, 1)
            steps = dve.value_load(turns_i[0:1, 0:1], min_val=NE, max_val=2 * NE)
            with dve.Fori(0, steps) as i:
                for k in range(SPLITS, PER_EXPERT + SPLITS):
                    for what, f in EXPERT_WORK.get(k, ()):
                        if what == "act":
                            dve.wait_ge(e_silu, i * FT + f + 1)
                            expert_used(dve, i, LAST_GU[f])
                            dve.wait_ge(e_turned, i * FT + max(f - 1, 0) + 1)
                            dve.tensor_tensor(act[:, f % 2, :], esilu[:, f % 2, :], bank[2 * (f % 2) + 1][:, :], ALU.mult)\
                               .then_inc(e_act, 1)
                        elif what == "turn":
                            dve.wait_ge(e_high, i * FT + f + 1)
                            dve.tensor_tensor(eactTl[:, f % 2, :, :], bank[4 + f % 2][:, :].rearrange("p (c n) -> p c n", c=4),
                                              eactTh[:, f % 2, :, :].bitcast(F32), ALU.subtract).then_inc(e_low, 1)
                        elif what == "back":
                            add_back(i + 1, range(2 * f, 2 * f + 2))
                        elif what == "y":
                            expert_used(dve, i, PER_EXPERT - 1)
                            dve.tensor_copy(ysb[:, 512:1024], bank[7][:, :]).then_inc(e_y_v, 1)
                        elif what == "build":
                            build_pick(ds(i + 1, 1), i + 1)
                            dve.wait_ge(e_putT, i + 1)
                            for tt in range(NT):
                                ins = dve.tensor_scalar(put[:, tt, :], slots[:, :], slotx[:, tt, ds(i, 1)],
                                                        gatex[:, tt, ds(i, 1)], ALU.is_equal, ALU.mult)
                            ins.then_inc(e_put, 1)
                        else:
                            dve.wait_ge(e_putT, i + 2)
                            dve.tensor_copy(putT, bank[5][:, 0:2 * P].rearrange("p (t n) -> p t n", t=NT))\
                               .then_inc(e_putT_moved, 1)
                            take_rows(i + 2)
                    n = N_FIRST + k
                    dve.wait_ge(rounded, n + 1 + PER_EXPERT * i)
                    dve.tensor_tensor(wl[:, n % SPLITS, :], ring[:, n % RING, :], wh[:, n % SPLITS, :].bitcast(F32),
                                      ALU.subtract).then_inc(split, 1)

            dve.wait_ge(ln_landed, 32 * 4)
            for tt in range(NT):
                add_back(steps + 1, range(2 * tt, 2 * tt + 2))
                dve.wait_ge(e_added, 4 * steps + 3 + 2 * tt)
                for half in range(2):
                    chained(dve.bn_stats(stats[:, tt, half, :], pre[:, tt, 512 * half:512 * half + 512]))
                center(tt)
            for tt in range(NT):
                scale(3, tt)


_INS = ['x', 'positions', 'w_in_a', 'w_out_a', 'cmp_pos', 'cmp_w1', 'cmp_w2', 'w_kv_shared', 'w_q_b', 'w_out_b',
        'sinks_b', 'ln_g', 'ln_b', 'dense_w_in', 'dense_w_out', 'moe_router', 'moe_w_in', 'moe_w_out']


def kernel(**inputs):
    import numpy as _np
    import concourse.bacc as _bacc
    from concourse import mybir as _mybir
    from concourse.bass_utils import run_bass_kernel_spmd as _run

    nc = _bacc.Bacc("TRN2", target_bir_lowering=False, num_devices=1)
    arrays, args = {}, []
    for name in _INS:
        a = _np.ascontiguousarray(inputs[name])
        arrays[f"in_{name}_dram"] = a
        args.append(nc.dram_tensor(f"in_{name}_dram", a.shape, _mybir.dt.from_np(a.dtype), kind="ExternalInput").ap())
    args.append(nc.dram_tensor("out_0_dram", (1, SEQ, D), F32, kind="ExternalOutput").ap())
    decoder_kernel(nc, *args)
    r = _run(nc, [arrays], core_ids=[0])
    return r.results[0]["out_0_dram"]
```

```python
from contextlib import ExitStack

import concourse.bass as bass
from concourse import mybir
from concourse.bass import ds

F32 = mybir.dt.float32
F32R = mybir.dt.float32r
BF16 = mybir.dt.bfloat16
I32 = mybir.dt.int32
ALU = mybir.AluOpType
ACT = mybir.ActivationFunctionType
X = mybir.AxisListType.X

P = 128
SEQ, D, HD = 256, 1024, 64
NT = SEQ // P
DC = D // P
ROT = HD // 4
ROPE_THETA = 500000.0
A_IN, A_KV = 2608, 256
CMP_STRIDE, CMP_HID = 16, 256
N_CMP = SEQ // CMP_STRIDE - 1
CMP_PAIRS = 16
FF, FFE, NE = 2816, 3584, 8
FT = FFE // 512
DEPTH = 2
ALPHA = float((2 * DEPTH) ** 0.25)
SCALE = HD ** -0.5
LN_EPS = 1e-5
NEG = -1e30
UNIT = 2048
RING = 7
SPLITS = 3
LAGS_A, LAGS_B = (3, 5), (2, 4)
TWO_PI_PARTS = (6.28125, 1.9350051879882812e-03, 3.0199159819e-07)


def weight_items():
    items = [("in_a", c, k) for c in (2, 3, 4) for k in range(2)] + [("in_a", 5, 0)]
    items += [("in_a", c, k) for c in (0, 1) for k in range(2)]
    items += [("cmp", c, k) for c in range(2) for k in range(2)]
    items += [("out_a", c, k) for k in range(2) for c in range(2)]
    items += [("dense_in", c, part) for c in range(FF // 256) for part in range(2)]
    items += [("dense_out", 0, k) for k in range(FF // 256)]
    items += [("kv", 0, 0)] + [("q_b", c, k) for c in range(2) for k in range(2)]
    items += [("out_b", c, k) for k in range(2) for c in range(2)]
    return items


ITEMS = weight_items()
N_FIRST = len(ITEMS)
AT = {}
for _n, (_kind, _, _) in enumerate(ITEMS):
    AT.setdefault(_kind, _n)
EXPERT = []
for _f in range(FT):
    EXPERT += [("g", _f, 0), ("g", _f, 1), ("u", _f, 0), ("u", _f, 1)]
    if _f >= 2:
        EXPERT += [("o", _f - 2, 0), ("o", _f - 2, 1)]
for _f in (FT - 2, FT - 1):
    EXPERT += [("o", _f, 0), ("o", _f, 1)]
PER_EXPERT = len(EXPERT)
SLOTS = RING + 4
_ORDER = [(N_FIRST + n) % RING for n in range(RING)] + list(range(RING, SLOTS))
_SHORT = -PER_EXPERT % SLOTS
_ROUNDS = -(-PER_EXPERT // SLOTS)
SLOT = [s for r in range(_ROUNDS) for s in _ORDER[:SLOTS - (r >= _ROUNDS - _SHORT)]]
assert len(SLOT) == PER_EXPERT and PER_EXPERT % SPLITS == 0


def last_in_slot(k):
    return next(j for j in range(k - 1, k - 1 - PER_EXPERT, -1) if SLOT[j % PER_EXPERT] == SLOT[k])


LAST_GU = [EXPERT.index(("u", f, 1)) for f in range(FT)]
TURN_AFTER = [LAST_GU[0] + 4, LAST_GU[1] + 4] + [LAST_GU[f] + 2 for f in range(2, FT)]
BACK_AFTER = (3, 5)
EXPERT_WORK = {PER_EXPERT + SPLITS - 1: [("y", 0)]}
for _f in range(FT):
    EXPERT_WORK.setdefault(LAST_GU[_f] + SPLITS, []).append(("act", _f))
for _f in range(FT):
    EXPERT_WORK.setdefault(TURN_AFTER[_f] + SPLITS, []).append(("turn", _f))
for _n in range(2):
    EXPERT_WORK.setdefault(BACK_AFTER[_n] + SPLITS, []).append(("back", _n))
EXPERT_WORK.setdefault(24, []).append(("build", 0))
EXPERT_WORK.setdefault(PER_EXPERT - 1, []).append(("rows", 0))


def attention_jobs(branches):
    jobs = []
    for pb in range(2):
        for b in range(2):
            for tt in range(NT):
                mine = []
                for br in branches:
                    if br == "cmp" or tt == 0:
                        mine.append((br, pb, b, tt, 0, 4, P))
                    else:
                        mine += [(br, pb, b, tt, 0, 2, SEQ), (br, pb, b, tt, 2, 2, SEQ)]
                jobs += [(*j, n == 0, n == len(mine) - 1) for n, j in enumerate(mine)]
    return jobs


JOBS_A = attention_jobs(("slc", "win", "cmp"))
JOBS_B = attention_jobs(("swa",))
PROJ_A = [(k, n, tt, w) for n, (k, w) in enumerate(
    [("cmpkv", 512), ("slckv", 512), ("winkv", 512), ("gate", 48), ("q0", 512), ("q1", 512)]) for tt in range(NT)]
PROJ_B = [(k, n, tt, w) for n, (k, w) in enumerate([("kv", 256), ("qb0", 512), ("qb1", 512)]) for tt in range(NT)]
LAST_A = [AT["in_a"] + n for n in (1, 3, 5, 6, 8, 10)]
LAST_B = [AT["kv"] + n for n in (0, 2, 4)]
N_DENSE = FF // 256
TURNS = {"cmpkv": 2, "slckv": 1, "winkv": 1, "gate": 0, "q0": 2, "q1": 2, "kv": 1, "qb0": 1, "qb1": 1}


def decoder_kernel(nc, x, positions, w_in_a, w_out_a, cmp_pos, cmp_w1, cmp_w2, w_kv_shared, w_q_b, w_out_b,
                   sinks_b, ln_g, ln_b, dense_w_in, dense_w_out, moe_router, moe_w_in, moe_w_out, out):
    ctx = ExitStack()
    with ctx:
        def sb(name, shape, dt=F32):
            return ctx.enter_context(nc.sbuf_tensor(name, shape, dt))

        def sem(name):
            return ctx.enter_context(nc.semaphore(name))

        ident = sb("ident", [P, P])
        identb = sb("identb", [P, P], BF16)
        onesb = sb("onesb", [P, P], BF16)
        earlier = sb("earlier", [P, P], BF16)
        causal = sb("causal", [P, 2, P], BF16)
        window = sb("window", [P, 2, P], BF16)
        cmpmask = sb("cmpmask", [P, NT, 4, P], BF16)
        seen = sb("seen", [P, NT])
        slots = sb("slots", [P, P])
        order = sb("order", [P, NT, NE])
        freq = sb("freq", [P, ROT // 2])
        pos_i = sb("pos_i", [P, NT], I32)
        pos_f = sb("pos_f", [P, NT])
        ang = sb("ang", [P, 3, NT, ROT // 2])
        cc = sb("cc", [P, NT, ROT])
        ss = sb("ss", [P, NT, ROT])
        rot1 = sb("rot1", [P, 8, ROT])
        rot2 = sb("rot2", [P, 8, ROT])
        posr = sb("posr", [16, 2, P])
        posT = sb("posT", [P, 2, 16])
        w2 = sb("w2", [P, 2, 2, 2, HD])
        router = sb("router", [P, DC, NE])
        routerh = sb("routerh", [P, DC, NE], F32R)
        routerl = sb("routerl", [P, DC, NE], F32R)
        lgT = sb("lgT", [NE, SEQ])
        sink = sb("sink", [P, 16])
        nsink = sb("nsink", [P, 16])
        gates = sb("gates", [P, NT, 48])
        mx = sb("mx", [P, 4, 4])
        nb = sb("nb", [P, 4, 4])
        sn = sb("sn", [P, 4, 4])
        es = sb("es", [P, 4, 4])
        sums = sb("sums", [P, 4, 4])
        rg = sb("rg", [P, 4, 4])
        stats = sb("stats", [P, NT, 2, 6])
        mv = sb("mv", [P, NT, 2])
        std = sb("std", [P, NT, 2])
        lg = sb("lg", [P, 7, NT, NE])
        selb = sb("selb", [P, NT, NE], BF16)
        top = sb("top", [P, 12, NT, 1])
        slotx = sb("slotx", [P, NT, 17])
        gatex = sb("gatex", [P, NT, 17])
        cnt = sb("cnt", [P, 2])
        turns_i = sb("turns_i", [P, 1], I32)

        base = [-(-nc.sbuf_base // 64) * 64]

        def place(*parts):
            size = 0
            found = []
            for name, shape, dt in parts:
                found.append(nc.alloc_sbuf_tensor_at(name, shape, dt, offset=base[0]))
                n = 4
                for x_ in shape[1:]:
                    n *= x_
                size = max(size, n)
            base[0] += size
            return found if len(found) > 1 else found[0]

        ring = place(("ring", [P, RING, UNIT], F32))
        wh = place(("wh", [P, SPLITS, UNIT], F32R))
        wl = place(("wl", [P, SPLITS, UNIT], F32R))
        h = place(("h", [P, NT, D], F32))
        pre, cmp_l = place(("pre", [P, NT, D], F32), ("cmp_l", [P, 2, CMP_PAIRS, 64], F32R))
        lnp, cmp_h = place(("lnp", [P, 2, D], F32), ("cmp_h", [P, 2, CMP_PAIRS, 64], F32R))
        hTh, slot9 = place(("hTh", [P, DC, SEQ], F32R), ("slot9", [P, UNIT], F32))
        hTl, slot10 = place(("hTl", [P, DC, SEQ], F32R), ("slot10", [P, UNIT], F32))
        arena, arena_r = place(("arena", [P, 12544], F32), ("arena_r", [P, 12544], F32R))

        def room(at, *shape, of=None):
            n = 1
            for x_ in shape:
                n *= x_
            v = (arena if of is None else of)[:, at:at + n]
            names = "abcd"[:len(shape)]
            if len(shape) > 1:
                v = v.rearrange(f"p ({' '.join(names)}) -> p {' '.join(names)}", **dict(zip(names[1:], shape[1:])))
            return v

        qT = room(0, 8, SEQ)
        qrT = room(2048, 8, SEQ)
        ksT = room(4096, 2, SEQ)
        kwT = room(4608, 2, SEQ)
        kcT = room(5120, P)
        vs = room(5248, NT, 256)
        vw = room(5760, NT, 256)
        vc = room(6272, P)
        stage = room(6400, 2, 1024)
        kcvT = room(8448, 2, 4, SEQ)
        cmp_in = room(10496, 2, CMP_PAIRS, 64)
        hid = room(10496, 2, CMP_HID)
        hidT = room(11008, 2, 2, P)
        ex = room(8448, LAGS_A[0] + 1, 512)
        pT = room(8448 + 512 * (LAGS_A[0] + 1), LAGS_A[1] - LAGS_A[0] + 1, 512)
        actTh = room(0, FF // P, SEQ, of=arena_r)
        actTl = room(5632, FF // P, SEQ, of=arena_r)
        silu = room(11264, 2, 512)
        xgTh = room(0, DC, P, of=arena_r)
        xgTl = room(1024, DC, P, of=arena_r)
        eactTh = room(2048, 2, 4, P, of=arena_r)
        eactTl = room(3072, 2, 4, P, of=arena_r)
        act = room(4096, 2, 512)
        esilu = room(5120, 2, 512)
        ysb = room(6144, D)
        pick = room(7168, NT, P)
        put = room(7424, NT, P)
        putT = room(7680, NT, P)
        slot_at = [ring[:, s, :] for s in range(RING)] + [room(8192, UNIT), room(10240, UNIT), slot9[:, :], slot10[:, :]]

        bank = [ctx.enter_context(nc.psum_tensor(f"bank{i}", [P, 512], F32)) for i in range(8)]

        landed = [sem(f"landed{i}") for i in range(SLOTS)]
        rounded = sem("rounded")
        split = sem("split")
        used = sem("used")
        x_landed = sem("x_landed")
        pos_landed = sem("pos_landed")
        small_landed = sem("small_landed")
        ln_landed = sem("ln_landed")
        ident_ready = sem("ident_ready")
        consts = sem("consts")
        consts_step = sem("consts_step")
        dve_step = sem("dve_step")
        trig_in = sem("trig_in")
        trig = sem("trig")
        turned = sem("turned")
        moved_a = sem("moved_a")
        moved_v = sem("moved_v")
        high = sem("high")
        post = sem("post")
        post_moved = sem("post_moved")
        staged_a = sem("staged_a")
        staged_v = sem("staged_v")
        cmp_sum = sem("cmp_sum")
        cmp_high = sem("cmp_high")
        cmp_low = sem("cmp_low")
        cmp_act = sem("cmp_act")
        cmp_kv = sem("cmp_kv")
        kc_ready = sem("kc_ready")
        vc_ready = sem("vc_ready")
        scored = sem("scored")
        shifted = sem("shifted")
        expd = sem("expd")
        normed = sem("normed")
        summed = sem("summed")
        heads_high = sem("heads_high")
        heads_out = sem("heads_out")
        mixed = sem("mixed")
        var_ready = sem("var_ready")
        std_ready = sem("std_ready")
        h_ready = sem("h_ready")
        silu_ready = sem("silu_ready")
        act_ready = sem("act_ready")
        act_high = sem("act_high")
        act_low = sem("act_low")
        router_high = sem("router_high")
        router_low = sem("router_low")
        routed = sem("routed")
        logits_moved = sem("logits_moved")
        gap_ready = sem("gap_ready")
        gap_exp = sem("gap_exp")
        sel_ready = sem("sel_ready")
        ranked = sem("ranked")
        plan_ready = sem("plan_ready")
        e_pick = sem("e_pick")
        e_put = sem("e_put")
        e_silu = sem("e_silu")
        e_act = sem("e_act")
        e_turned = sem("e_turned")
        e_high = sem("e_high")
        e_low = sem("e_low")
        e_putT = sem("e_putT")
        e_putT_moved = sem("e_putT_moved")
        e_rows = sem("e_rows")
        e_rows_high = sem("e_rows_high")
        e_rows_low = sem("e_rows_low")
        e_y_a = sem("e_y_a")
        e_y_v = sem("e_y_v")
        e_back = sem("e_back")
        e_added = sem("e_added")
        done = sem("done")

        in_a = w_in_a[0].rearrange("(c p) n -> p c n", p=P)
        d_in = dense_w_in[0].rearrange("(c p) n -> p c n", p=P)
        d_out = dense_w_out[0].rearrange("(c p) n -> p c n", p=P)
        q_b = w_q_b[0].rearrange("(c p) (b a n) -> p c b a n", p=P, b=2, a=2)
        kv_w = w_kv_shared.rearrange("(c p) n -> p c n", p=P)
        e_in = moe_w_in[0].rearrange("e (c p) n -> e p c n", p=P)
        e_out = moe_w_out[0].rearrange("e (c p) n -> e p c n", p=P)
        out_a = w_out_a[0].rearrange("(a b r d) n -> b d a r n", a=2, b=2, r=4, d=HD)
        out_b = w_out_b[0].rearrange("(b r d) n -> b d r n", b=2, r=8, d=HD)

        def start_item(sp, n):
            kind, c, k = ITEMS[n]
            sig = landed[n % RING]
            slot = ring[:, n % RING, :]

            if kind == "in_a":
                w = min(512, A_IN - 512 * c)
                depth = 4 if w == 512 else DC
                sp.dma_start(slot[:, 0:depth * w].rearrange("p (c n) -> p c n", c=depth),
                             in_a[:, 4 * k:4 * k + depth, 512 * c:512 * c + w]).then_inc(sig, 32)
            elif kind == "cmp":
                sp.dma_start(slot.rearrange("p (j n) -> p j n", j=8),
                             cmp_w1[0, c].rearrange("(j p) n -> p j n", p=P)[:, 8 * k:8 * k + 8, :]).then_inc(sig, 32)
            elif kind in ("out_a", "out_b"):
                for b in range(2):
                    dst = slot[b * HD:(b + 1) * HD, :].rearrange("p (r n) -> p r n", r=4)
                    cols = slice(512 * c, 512 * c + 512)
                    src = out_a[b, :, k, :, cols] if kind == "out_a" else out_b[b, :, 4 * k:4 * k + 4, cols]
                    sp.dma_start(dst, src).then_inc(sig, 16)
            elif kind == "dense_in":
                at = k * FF + 256 * c
                sp.dma_start(slot.rearrange("p (c n) -> p c n", c=DC), d_in[:, :, at:at + 256]).then_inc(sig, 32)
            elif kind == "dense_out":
                sp.dma_start(slot.rearrange("p (c n) -> p c n", c=2), d_out[:, 2 * k:2 * k + 2, :]).then_inc(sig, 32)
            elif kind == "kv":
                sp.dma_start(slot.rearrange("p (c n) -> p c n", c=DC), kv_w).then_inc(sig, 32)
            else:
                for b in range(2):
                    sp.dma_start(slot.rearrange("p (c b n) -> p c b n", c=4, b=2)[:, :, b, :],
                                 q_b[:, 4 * k:4 * k + 4, b, c, :]).then_inc(sig, 16)

        def size_of(n):
            return DC * 48 if n < N_FIRST and ITEMS[n][:2] == ("in_a", 5) else UNIT

        BEFORE = [32 * sum(1 for n in range(N_FIRST) if n % RING == s) for s in range(RING)] + [0] * 4

        def out_bank(proj, j):
            return (j - len(proj)) % 4

        def slot_of(n):
            return slot_at[n % RING if n < N_FIRST else SLOT[n - N_FIRST]]

        def expert_landed(eng, i, k):
            s = SLOT[k % PER_EXPERT]
            nth = sum(1 for j in range(k + 1) if SLOT[j % PER_EXPERT] == s)
            eng.wait_ge(landed[s], BEFORE[s] + 16 * nth + 16 * SLOT.count(s) * i)

        def expert_used(eng, i, k):
            eng.wait_ge(used, N_FIRST + k + 1 + PER_EXPERT * i)

        def moved(eng, n):
            if n >= 0:
                mine = [m for m in range(n + 1) if MOVER[m] == MOVER[n]]
                eng.wait_ge(moved_v if MOVER[n] == "v" else moved_a, len(mine))

        T_X = 0
        T_A = T_X + 4
        first_a = [T_A + sum(TURNS[p[0]] for p in PROJ_A[:j]) for j in range(len(PROJ_A) + 1)]
        T_HID = first_a[-1]
        T_JA = T_HID + 1
        T_H1 = T_JA + len(JOBS_A)
        T_H2 = T_H1 + 4
        T_B = T_H2 + 4
        first_b = [T_B + sum(TURNS[p[0]] for p in PROJ_B[:j]) for j in range(len(PROJ_B) + 1)]
        T_JB = first_b[-1]
        T_H3 = T_JB + len(JOBS_B)
        T_END = T_H3 + 4

        MOVER = ["v" if n % 2 else "a" for n in range(T_END)]
        TBANK = [4 + n % 4 if n < first_a[-3] or T_B <= n < T_JB else 4 + n % 2 for n in range(T_END)]
        TBANK[first_a[-3]:T_HID] = (4, 5, 7, 4)
        for first, b in ((T_X, 4), (T_H1, 4), (T_H2, 0), (T_H3, 4)):
            MOVER[first:first + 4] = "vvvv"
            TBANK[first:first + 4] = range(b, b + 4)

        block = ctx.enter_context(nc.Block())

        @block.sync
        def _(sp):
            sp.wait_ge(x_landed, 16)
            for n in range(N_FIRST):
                if n >= RING:
                    sp.wait_ge(split, n - RING + 1)
                start_item(sp, n)

            def expert_item(i, k, expert, first=False):
                kind, f, half = EXPERT[k]
                s = SLOT[k]
                before = last_in_slot(k)
                if not first or before >= 0:
                    sp.wait_ge(split, N_FIRST + before + 1 + PER_EXPERT * i)
                elif s < RING:
                    sp.wait_ge(split, max(n for n in range(N_FIRST) if n % RING == s) + 1)
                elif s < RING + 2:
                    sp.wait_ge(heads_out, 16)
                else:
                    sp.wait_ge(routed, 1)
                if kind == "o":
                    src = e_out[ds(expert, 1), :, 4 * f + 2 * half:4 * f + 2 * half + 2, :]
                    dst = slot_at[s].rearrange("p (c n) -> p c n", c=2)
                else:
                    at = (kind == "u") * FFE + 512 * f
                    src = e_in[ds(expert, 1), :, 4 * half:4 * half + 4, at:at + 512]
                    dst = slot_at[s].rearrange("p (c n) -> p c n", c=4)
                sp.dma_start(dst, src.rearrange("e p c n -> (e p) c n")).then_inc(landed[s], 16)

            for k in range(PER_EXPERT):
                expert_item(0, k, 0, first=True)
            sp.wait_ge(plan_ready, 1)
            steps = sp.value_load(turns_i[0:1, 0:1], min_val=NE, max_val=2 * NE)
            with sp.Fori(1, steps) as i:
                for k in range(PER_EXPERT):
                    expert_item(i, k, i % NE)
            for k in range(SPLITS):
                expert_item(steps, k, 0)
            for n in range(4):
                sp.wait_ge(h_ready, 12 + n + 1)
                tt, cols = n // 2, slice(512 * (n % 2), 512 * (n % 2) + 512)
                sp.dma_start(out[0, tt * P:tt * P + P, cols], h[:, tt, cols]).then_inc(done, 16)
            sp.wait_ge(done, 16 * 4)

        @block.gpsimd
        def _(pool):
            n = [0]

            def step(ins):
                n[0] += 1
                ins.then_inc(consts_step, 1)
                pool.wait_ge(consts_step, n[0])

            step(pool.memset(ident[:, :], 0.0))
            step(pool.affine_select(out=ident[:, :], in_=ident[:, :], compare_op=ALU.not_equal, fill=1.0, base=0,
                                    pattern=[[-1, P]], channel_multiplier=1))
            pool.sem_inc(ident_ready, 1)
            step(pool.tensor_copy(identb[:, :], ident[:, :]))
            for j in range(ROT // 2):
                step(pool.memset(freq[:, j:j + 1], float(ROPE_THETA ** (-2.0 * j / ROT))))
            step(pool.memset(causal[:, :, :], 0.0))
            step(pool.memset(window[:, :, :], 0.0))
            for m in (causal, window):
                step(pool.affine_select(out=m[:, 1, :], in_=m[:, 1, :], compare_op=ALU.is_ge, fill=NEG, base=0,
                                        pattern=[[-1, P]], channel_multiplier=1))
            step(pool.affine_select(out=window[:, 0, :], in_=window[:, 0, :], compare_op=ALU.is_ge, fill=NEG, base=-1,
                                    pattern=[[1, P]], channel_multiplier=-1))
            step(pool.memset(cmpmask[:, :, :, :], NEG))
            for tt in range(NT):
                for g in range(4):
                    part = cmpmask[:, tt, g, 16 * g:16 * g + 16]
                    step(pool.memset(part, 0.0))
                    step(pool.affine_select(out=part, in_=part, compare_op=ALU.is_ge, fill=NEG,
                                            base=P * tt - (2 * CMP_STRIDE - 1), pattern=[[-CMP_STRIDE, 16]],
                                            channel_multiplier=1))
            step(pool.memset(seen[:, :], 1.0))
            step(pool.affine_select(out=seen[:, 0:1], in_=seen[:, 0:1], compare_op=ALU.is_ge, fill=0.0,
                                    base=-(2 * CMP_STRIDE - 1), pattern=[[0, 1]], channel_multiplier=1))
            step(pool.memset(onesb[:, :], 1.0))
            step(pool.affine_select(out=earlier[:, :], in_=onesb[:, :], compare_op=ALU.is_ge, fill=0.0, base=-1,
                                    pattern=[[1, P]], channel_multiplier=-1))
            step(pool.iota(slots[:, :], [[1, P]], base=0, channel_multiplier=0, allow_small_or_imprecise_dtypes=True))
            step(pool.iota(order[:, :, :], [[0, NT], [-1, NE]], base=NE, channel_multiplier=0,
                           allow_small_or_imprecise_dtypes=True))
            step(pool.memset(cmp_in[:, :, :, :], 0.0))
            pool.memset(slotx[:, :, 16:17], -1.0).then_inc(consts, 1)
            pool.memset(gatex[:, :, 16:17], 0.0).then_inc(consts, 1)

            pool.wait_ge(h_ready, 12)
            pool.tensor_scalar(pre[:, :, :], h[:, :, :], ALPHA, None, ALU.mult).then_inc(e_added, 1)

        @block.scalar
        def _(act_e):
            act_e.dma_start(h[:, :, :], x[0].rearrange("(t p) d -> p t d", p=P)).then_inc(x_landed, 16)
            act_e.dma_start(pos_i[:, :], positions[0].rearrange("(t p) -> p t", p=P),
                            allow_slow_non_contiguous=True).then_inc(pos_landed, 16)
            act_e.dma_start(posr[:, :, :], cmp_pos[0].rearrange("v (j a) d -> j v (a d)", a=2)).then_inc(small_landed, 16)
            for kv in range(2):
                for twice in range(2):
                    act_e.dma_start(w2[:, kv, :, twice, :], cmp_w2[0, kv].rearrange("(c p) d -> p c d", p=P))\
                         .then_inc(small_landed, 16)
            act_e.dma_start(router[:, :, :], moe_router[0].rearrange("(c p) e -> p c e", p=P),
                            allow_slow_non_contiguous=True).then_inc(small_landed, 16)
            act_e.dma_start(sink[:, :], sinks_b[0:1, :].to_broadcast([P, 16])).then_inc(small_landed, 16)

            def load_norm(k):
                for part, src in enumerate((ln_g, ln_b)):
                    act_e.dma_start(lnp[:, part, :], src[k // 2, k % 2:k % 2 + 1, :].to_broadcast([P, D]))\
                         .then_inc(ln_landed, 16)

            n_round = [0]

            def split_weights(upto):
                for n in range(n_round[0], upto):
                    if n < N_FIRST:
                        act_e.wait_ge(landed[n % RING], 32 * (n // RING + 1))
                    else:
                        expert_landed(act_e, 0, n - N_FIRST)
                    if n >= SPLITS:
                        act_e.wait_ge(used, n - SPLITS + 1)
                    size = size_of(n)
                    act_e.activation(wh[:, n % SPLITS, 0:size], slot_of(n)[:, 0:size], ACT.Copy).then_inc(rounded, 1)
                n_round[0] = max(n_round[0], upto)

            def turn_h(first, tt):
                for q in range(2):
                    n = 2 * tt + q
                    act_e.wait_ge(turned, first + n + 1)
                    act_e.activation(hTh[:, 4 * q:4 * q + 4, tt * P:tt * P + P],
                                     bank[TBANK[first + n]][:, :].rearrange("p (c n) -> p c n", c=4), ACT.Copy)\
                         .then_inc(high, 1)

            for tt in range(NT):
                turn_h(T_X, tt)
            split_weights(SPLITS)
            act_e.wait_ge(trig_in, 1)
            act_e.activation(ss[:, :, 0:8], ang[:, 1, :, :], ACT.Sin).then_inc(trig, 1)
            act_e.activation(cc[:, :, 0:8], ang[:, 2, :, :], ACT.Sin).then_inc(trig, 1)
            act_e.wait_ge(small_landed, 16 * 7)
            act_e.activation(routerh[:, :, :], router[:, :, :], ACT.Copy).then_inc(router_high, 1)

            def stage_part(j, proj, base, nturn, last):
                kind, _, tt, w = proj[j]
                act_e.wait_ge(used, last[j // NT] + 1)
                src = bank[out_bank(proj, j)]
                s = stage[:, j % 2, :]
                if j >= 2:
                    act_e.wait_ge(turned, nturn[j - 1])
                if kind == "cmpkv":
                    act_e.activation(s.rearrange("p (g a d) -> p g a d", g=8, a=2)[:, :, 0, :],
                                     src[:, :].rearrange("p (g d) -> p g d", g=8), ACT.Copy).then_inc(staged_a, 1)
                elif kind in ("slckv", "winkv", "kv"):
                    nk = w // 2
                    v = vw if kind == "winkv" else vs
                    act_e.activation(v[:, tt, 0:nk], src[:, nk:w], ACT.Copy)
                    act_e.activation(s[:, 0:nk].rearrange("p (g d) -> p g d", d=HD)[:, :, ROT:],
                                     src[:, 0:nk].rearrange("p (g d) -> p g d", d=HD)[:, :, ROT:], ACT.Copy)\
                         .then_inc(staged_a, 1)
                elif kind == "gate":
                    act_e.activation(gates[:, tt, :], src[:, 0:48], ACT.Sigmoid).then_inc(staged_a, 1)
                elif kind in ("q0", "q1"):
                    act_e.activation(s[:, 0:512].rearrange("p (r b d) -> p b r d", r=4, b=2),
                                     src[:, :].rearrange("p (b r d) -> p b r d", b=2, r=4), ACT.Copy)\
                         .then_inc(staged_a, 1)
                else:
                    act_e.activation(s[:, 0:512].rearrange("p (r b d) -> p b r d", r=4, b=2)[:, :, :, ROT:],
                                     src[:, :].rearrange("p (b r d) -> p b r d", b=2, r=4)[:, :, :, ROT:], ACT.Copy)\
                         .then_inc(staged_a, 1)

            def take_turned(j, proj, first):
                for t, n in enumerate(range(first[j], first[j + 1])):
                    if n % 2 == 0:
                        copy_projection(act_e, n, proj[j], t)

            def copy_projection(eng, n, p, t):
                kind, _, tt, _ = p
                eng.wait_ge(turned, n + 1)
                src = bank[TBANK[n]]
                cols = slice(tt * P, tt * P + P)
                if kind == "cmpkv":
                    act_e.activation(kcvT[0:64, t, :, cols], src[0:64, :].rearrange("p (g n) -> p g n", g=4), ACT.Copy)
                    lo = 1 if tt == 0 else 0
                    act_e.activation(kcvT[64:128, t, :, tt * P + lo - 1:tt * P + P - 1],
                                     src[64:128, :].rearrange("p (g n) -> p g n", g=4)[:, :, lo:], ACT.Copy)\
                         .then_inc(moved_a, 1)
                elif kind in ("slckv", "winkv"):
                    act_e.activation((ksT if kind == "slckv" else kwT)[:, :, cols],
                                     src[:, 0:256].rearrange("p (g n) -> p g n", g=2), ACT.Copy).then_inc(moved_a, 1)
                elif kind in ("q0", "q1"):
                    pb = int(kind[-1])
                    act_e.activation((qrT if t else qT)[:, 4 * pb:4 * pb + 4, cols],
                                     src[:, :].rearrange("p (g n) -> p g n", g=4), ACT.Copy).then_inc(moved_a, 1)
                elif kind == "kv":
                    act_e.activation(ksT[:, 0, cols], src[:, 0:P], ACT.Copy).then_inc(moved_a, 1)
                else:
                    pb = int(kind[-1])
                    act_e.activation(qrT[:, 4 * pb:4 * pb + 4, cols],
                                     src[:, :].rearrange("p (g n) -> p g n", g=4), ACT.Copy).then_inc(moved_a, 1)

            def projections(proj, base, first, last):
                for m in range(len(last)):
                    split_weights(last[m] + SPLITS)
                    if m >= 1:
                        for tt in range(NT):
                            take_turned(NT * (m - 1) + tt, proj, first)
                    for tt in range(NT):
                        stage_part(NT * m + tt, proj, base, first, last)
                    if m == 1 and proj is PROJ_A:
                        act_e.wait_ge(cmp_sum, 1)
                        act_e.activation(cmp_h[:, :, :, :], cmp_in, ACT.Copy).then_inc(cmp_high, 1)

            projections(PROJ_A, 0, first_a, LAST_A)

            n_cmp = AT["cmp"] + 3
            split_weights(n_cmp + SPLITS)
            act_e.wait_ge(used, n_cmp + 1)
            act_e.activation(hid[0:64, :, :].rearrange("p a b -> p (a b)"), bank[6][0:64, :], ACT.Gelu_apprx_tanh)\
                 .then_inc(cmp_act, 1)
            load_norm(0)
            split_weights(n_cmp + SPLITS + 1)
            for tt in range(NT):
                take_turned(len(PROJ_A) - NT + tt, PROJ_A, first_a)

            def compress():
                if T_HID % 2 == 0:
                    act_e.wait_ge(turned, T_HID + 1)
                    for twice in range(2):
                        ins = act_e.activation(hidT.rearrange("p a c n -> p (a c) n")[:, :, 64 * twice:64 * twice + 64],
                                               bank[TBANK[T_HID]][:, 0:256].rearrange("p (g n) -> p g n", g=4), ACT.Copy)
                    ins.then_inc(moved_a, 1)
                act_e.wait_ge(cmp_kv, 1)
                act_e.activation(kcT, bank[7][:, 0:P], ACT.Copy).then_inc(kc_ready, 1)

            def take_last_b():
                for tt in range(NT):
                    take_turned(len(PROJ_B) - NT + tt, PROJ_B, first_b)

            def attention(jobs, base, first, acc_base, swa, prepare, lags):
                accs = acc_base
                lag, lag_v = lags
                for i in range(len(jobs) + lag_v + 1):
                    if i == 1:
                        prepare()
                    if i < len(jobs):
                        _, pb, b, tt, h0, nh, w, _, _ = jobs[i]
                        act_e.wait_ge(shifted, base + i + 1)
                        if i > lag:
                            act_e.wait_ge(turned, first + i - lag)
                        for k in range(nh):
                            ins = act_e.activation(ex[:, i % (lag + 1), k * w:k * w + w], bank[i % 4][:, k * w:k * w + w],
                                                   ACT.Exp, bias=nb[:, i % 4, k:k + 1], scale=SCALE,
                                                   accum_out=sums[:, i % 4, k:k + 1])
                        if swa:
                            ins = act_e.activation(es[:, i % 4, 0:nh], sn[:, i % 4, 0:nh], ACT.Exp)
                        ins.then_inc(expd, 1)
                    if lag <= i < len(jobs) + lag and (first + i - lag) % 2 == 0:
                        n = first + i - lag
                        act_e.wait_ge(turned, n + 1)
                        if i > lag_v:
                            act_e.wait_ge(summed, base + i - lag_v)
                        act_e.activation(pT[:, n % (lag_v - lag + 1), :], bank[4 + n % 2][:, :], ACT.Copy).then_inc(moved_a, 1)
                    if i > lag_v:
                        _, pb, b, tt, _, _, _, _, closes = jobs[i - lag_v - 1]
                        if closes:
                            act_e.wait_ge(summed, base + i - lag_v)
                            act_e.activation(hTh[b * 64:b * 64 + 64, 4 * pb:4 * pb + 4, tt * P:tt * P + P],
                                             bank[6 + accs % 2][b * 64:b * 64 + 64, :].rearrange("p (r n) -> p r n", r=4),
                                             ACT.Copy).then_inc(heads_high, 1)
                            accs += 1

            def norm_part(k, first):
                for tt in range(NT):
                    act_e.wait_ge(var_ready, NT * k + tt + 1)
                    act_e.activation(std[:, tt, 0:1], std[:, tt, 1:2], ACT.Sqrt).then_inc(std_ready, 1)
                    if k < 3:
                        turn_h(first, tt)
                if k < 3:
                    load_norm(k + 1)

            attention(JOBS_A, 0, T_JA, 0, False, compress, LAGS_A)
            split_weights(AT["out_a"] + 5)
            norm_part(0, T_H1)

            for c in range(N_DENSE + 1):
                if c < N_DENSE:
                    n = AT["dense_in"] + 2 * c
                    split_weights(n + 1 + SPLITS)
                    act_e.wait_ge(used, n + 1)
                    if c >= 2:
                        act_e.wait_ge(act_low, c - 1)
                    act_e.activation(silu[:, c % 2, :], bank[2 * (c % 2)][:, :], ACT.Silu).then_inc(silu_ready, 1)
                if c >= 1:
                    act_e.wait_ge(act_ready, c)
                    act_e.activation(actTh[:, 2 * c - 2:2 * c, :],
                                     silu[:, (c - 1) % 2, :].rearrange("p (a n) -> p a n", a=2), ACT.Copy)\
                         .then_inc(act_high, 1)
            split_weights(AT["dense_out"] + N_DENSE + 1)
            norm_part(1, T_H2)
            projections(PROJ_B, len(PROJ_A), first_b, LAST_B)
            split_weights(AT["out_b"] + SPLITS)
            attention(JOBS_B, len(JOBS_A), T_JB, 8, True, take_last_b, LAGS_B)
            split_weights(N_FIRST + 1)

            def split_expert(i, k):
                expert_landed(act_e, i, k)
                expert_used(act_e, i, k - SPLITS)
                n = N_FIRST + k
                act_e.activation(wh[:, n % SPLITS, :], slot_at[SLOT[k % PER_EXPERT]], ACT.Copy).then_inc(rounded, 1)

            norm_part(2, T_H3)
            split_weights(N_FIRST + SPLITS)
            act_e.sem_inc(e_y_a, 1)
            act_e.wait_ge(gap_ready, 1)
            act_e.activation(top[:, 5, :, :], top[:, 4, :, :], ACT.Exp).then_inc(gap_exp, 1)

            def take_rows(value):
                for q in range(2):
                    act_e.wait_ge(e_rows, 2 * value + q - 1)
                    act_e.activation(xgTh[:, 4 * q:4 * q + 4, :],
                                     bank[2 + q][:, :].rearrange("p (c n) -> p c n", c=4), ACT.Copy)\
                         .then_inc(e_rows_high, 1)

            def expert_step(i):
                for k in range(SPLITS, PER_EXPERT + SPLITS):
                    for what, f in EXPERT_WORK.get(k, ()):
                        if what == "act":
                            expert_used(act_e, i, EXPERT.index(("g", f, 1)))
                            act_e.wait_ge(e_act, i * FT + max(f - 1, 0) + 1)
                            act_e.activation(esilu[:, f % 2, :], bank[2 * (f % 2)][:, :], ACT.Silu).then_inc(e_silu, 1)
                        elif what == "turn":
                            act_e.wait_ge(e_turned, i * FT + f + 2)
                            act_e.activation(eactTh[:, f % 2, :, :],
                                             bank[4 + f % 2][:, :].rearrange("p (c n) -> p c n", c=4), ACT.Copy)\
                                 .then_inc(e_high, 1)
                        elif what == "y":
                            expert_used(act_e, i, PER_EXPERT - 1)
                            act_e.activation(ysb[:, 0:512], bank[6][:, :], ACT.Copy).then_inc(e_y_a, 1)
                        elif what == "rows":
                            take_rows(i + 2)
                    split_expert(i, k)

            take_rows(1)
            act_e.wait_ge(plan_ready, 1)
            steps = act_e.value_load(turns_i[0:1, 0:1], min_val=NE, max_val=2 * NE)
            with act_e.Fori(0, steps) as i:
                expert_step(i)
            norm_part(3, None)

        @block.tensor
        def _(pe):
            def ready(n):
                pe.wait_ge(split, n + 1)

            def part(n, tile, size=UNIT):
                return tile[:, n % SPLITS, 0:size]

            def product(out_, lhs, rhs, start, stop):
                (lh, ll), (rh, rl) = lhs, rhs
                pe.matmul(out_, lh, rh, start=start, stop=False, skip_group_check=True)
                pe.matmul(out_, ll, rh, start=False, stop=False, skip_group_check=True)
                return pe.matmul(out_, lh, rl, start=False, stop=stop, skip_group_check=True)

            def both(n, depth, size=UNIT):
                return [part(n, tile, size).rearrange("p (c n) -> p c n", c=depth) for tile in (wh, wl)]

            def turn(n, sources):
                before = [m for m in range(n) if TBANK[m] == TBANK[n]]
                if before:
                    moved(pe, before[-1])
                b = bank[TBANK[n]]
                at = 0
                for src in sources:
                    rows = src.shape[0]
                    ins = pe.transpose(b[:, at:at + rows], src, ident[0:rows, 0:rows])
                    at += rows
                ins.then_inc(turned, 1)

            def turn_h(first):
                for n in range(4):
                    tt, q = n // 2, n % 2
                    turn(first + n, [h[:, tt, (4 * q + c) * P:(4 * q + c + 1) * P] for c in range(4)])

            pe.wait_ge(ident_ready, 1)
            pe.wait_ge(x_landed, 16)
            turn_h(T_X)
            pe.wait_ge(small_landed, 16 * 7)
            for kv in range(2):
                ins = pe.transpose(bank[3][:, 16 * kv:16 * kv + 16], posr[:, kv, :], ident[0:16, 0:16])
            ins.then_inc(post, 1)
            moved(pe, T_X + 3)

            def project(m, proj, base, last):
                _, _, _, w = proj[NT * m]
                first_item = (last[m - 1] if m else last[0] - (1 if w == 512 else 0) - 1) + 1
                depth = 4 if w == 512 else DC
                if base + NT * m == NT:
                    pe.wait_ge(post_moved, 1)
                if base + NT * m >= 4:
                    pe.wait_ge(staged_v, base + NT * m - 2)
                for n in range(first_item, last[m] + 1):
                    ready(n)
                    wts = both(n, depth, DC * w if w < 256 else UNIT)
                    for tt in range(NT):
                        for c in range(depth):
                            cc_ = (n - first_item) * depth + c
                            lhs = [t[:, cc_, tt * P:tt * P + P] for t in (hTh, hTl)]
                            ins = product(bank[out_bank(proj, NT * m + tt)][:, 0:w], lhs, [t[:, c, :] for t in wts],
                                          cc_ == 0, cc_ == DC - 1)
                    ins.then_inc(used, 1)

            def turn_projection(j, proj, base, first):
                kind, _, tt, w = proj[j]
                pe.wait_ge(staged_a, base + j + 1)
                pe.wait_ge(staged_v, base + j + 1)
                s = stage[:, j % 2, :]
                if kind == "cmpkv":
                    for kv in range(2):
                        turn(first[j] + kv, [s[:, (4 * kv + g) * P:(4 * kv + g + 1) * P] for g in range(4)])
                elif kind in ("slckv", "winkv"):
                    turn(first[j], [s[:, g * P:(g + 1) * P] for g in range(2)])
                elif kind in ("q0", "q1"):
                    for t in range(2):
                        turn(first[j] + t, [s[:, 512 * t + r * P:512 * t + (r + 1) * P] for r in range(4)])
                elif kind == "kv":
                    turn(first[j], [s[:, 0:P]])
                elif kind in ("qb0", "qb1"):
                    turn(first[j], [s[:, r * P:(r + 1) * P] for r in range(4)])

            def projections(proj, base, first, last):
                for m in range(len(last)):
                    project(m, proj, base, last)
                    if m >= 1:
                        for tt in range(NT):
                            turn_projection(NT * (m - 1) + tt, proj, base, first)

            projections(PROJ_A, 0, first_a, LAST_A)

            pe.wait_ge(cmp_low, 1)
            for n in range(first_a[-3] - 4, first_a[-3]):
                moved(pe, n)
            for kv in range(2):
                for k in range(2):
                    n = AT["cmp"] + 2 * kv + k
                    ready(n)
                    wts = both(n, 8)
                    for j in range(8):
                        ins = product(bank[6][0:64, 256 * kv:256 * kv + 256],
                                      [t[:, kv, 8 * k + j, :] for t in (cmp_h, cmp_l)], [t[:, j, :] for t in wts],
                                      (k == 0 and j == 0), (k == 1 and j == 7))
                    ins.then_inc(used, 1)
            for tt in range(NT):
                turn_projection(len(PROJ_A) - NT + tt, PROJ_A, 0, first_a)

            def compress():
                pe.wait_ge(cmp_act, 1)
                turn(T_HID, [hid[0:64, kv, c * P:c * P + P] for kv in range(2) for c in range(2)])
                moved(pe, T_HID)
                for c in range(2):
                    pe.matmul(bank[7][:, 0:P], w2[:, 0, c, :, :].rearrange("p a d -> p (a d)"), hidT[:, 0, c, :],
                              start=(c == 0), stop=(c == 1))
                for c in range(2):
                    ins = pe.matmul(bank[7][:, P:2 * P], hidT[:, 1, c, :], w2[:, 1, c, :, :].rearrange("p a d -> p (a d)"),
                                    start=(c == 0), stop=(c == 1))
                ins.then_inc(cmp_kv, 1)
                pe.wait_ge(kc_ready, 1)
                pe.wait_ge(vc_ready, 1)

            def turn_last_b():
                for tt in range(NT):
                    turn_projection(len(PROJ_B) - NT + tt, PROJ_B, len(PROJ_A), first_b)

            def attention(jobs, base, first, acc_base, n_out, prepare, lags):
                accs = acc_base
                lag, lag_v = lags
                for i in range(len(jobs) + lag_v):
                    if i == 2:
                        prepare()
                    if i == len(jobs):
                        pe.wait_ge(heads_out, acc_base + 4)
                    if len(jobs) <= i < len(jobs) + NT:
                        pe.wait_ge(expd, base + i - 3)
                        mix_part(n_out, 0, 0, i - len(jobs))
                    if i == len(jobs) // 2:
                        for n in range(first - 3, first):
                            moved(pe, n)
                    if i < len(jobs):
                        br, pb, b, tt, h0, nh, w, _, _ = jobs[i]
                        if base + i >= 4:
                            pe.wait_ge(expd, base + i - 3)
                        sc = bank[i % 4]
                        if br == "cmp":
                            mask = cmpmask[:, tt, 2 * pb + b, :]
                        else:
                            m = window if br == "swa" else causal
                            mask = m[:, :, :].rearrange("p a n -> p (a n)") if br == "swa" and tt else m[:, 1, :]
                        wm = mask.shape[1]
                        mask = mask.rearrange("p (a n) -> p a n", a=1).to_broadcast([P, nh, wm])
                        pe.matmul(sc[:, :].rearrange("p (k n) -> p k n", k=nh)[:, :, w - wm:], identb[:, :], mask,
                                  start=True, stop=False, skip_group_check=True)
                        q = qT if br == "cmp" else qrT
                        half = slice(64 * b, 64 * b + 64)
                        keys = {"cmp": kcT[half, :], "slc": ksT[half, pb, 0:w], "win": kwT[half, pb, 0:w],
                                "swa": ksT[half, 0, 0:w]}[br]
                        for k in range(nh):
                            ins = pe.matmul(sc[:, k * w:k * w + w], q[half, 4 * pb + h0 + k, tt * P:tt * P + P], keys,
                                            start=False, stop=(k == nh - 1), skip_group_check=True)
                        ins.then_inc(scored, 1)
                    if lag <= i < len(jobs) + lag:
                        pe.wait_ge(normed, base + i - lag + 1)
                        turn(first + i - lag, [ex[:, (i - lag) % (lag + 1), c * P:c * P + P] for c in range(4)])
                    if i >= lag_v:
                        br, pb, b, tt, h0, nh, w, opens, closes = jobs[i - lag_v]
                        n = first + i - lag_v
                        p_at = pT[:, n % (lag_v - lag + 1), :]
                        moved(pe, n)
                        if opens and accs >= 2:
                            pe.wait_ge(heads_out, accs - 1)
                        acc = bank[6 + accs % 2]
                        v = {"cmp": vc, "slc": vs, "win": vw, "swa": vs}[br]
                        cols = slice(0, P) if br in ("cmp", "swa") else slice(P * pb, P * pb + P)
                        if w == P:
                            lhs = v if br == "cmp" else v[:, 0, cols]
                            ins = pe.matmul(acc[:, :], lhs, p_at, start=opens, stop=closes,
                                            skip_group_check=True)
                        else:
                            p4 = p_at.rearrange("p (k c n) -> p c k n", k=2, c=2)
                            for c in range(2):
                                ins = pe.matmul(acc[:, h0 * P:h0 * P + 2 * P], v[:, c, cols], p4[:, c, :, :],
                                                start=(opens and c == 0), stop=(closes and c == 1),
                                                skip_group_check=True)
                        ins.then_inc(summed, 1)
                        accs += closes
                pe.wait_ge(expd, base + len(jobs))
                for tt in range(NT):
                    mix_part(n_out, 0, 1, tt)

            def mix_part(n0, k, half, tt):
                n = n0 + 2 * k + half
                if tt == 0:
                    ready(n)
                wts = both(n, 4)
                for r in range(4):
                    lhs = [t[:, 4 * k + r, tt * P:tt * P + P] for t in (hTh, hTl)]
                    ins = product(bank[2 * half + tt][:, :], lhs, [t[:, r, :] for t in wts],
                                  (k == 0 and r == 0), (k == 1 and r == 3))
                if tt == NT - 1:
                    ins.then_inc(used, 1)
                elif k == 1:
                    ins.then_inc(mixed, 1)

            def mix_out(n0, heads):
                pe.wait_ge(heads_out, heads)
                for tt in range(NT):
                    for half in range(2):
                        mix_part(n0, 1, half, tt)

            def next_h(k, first):
                for n in range(4):
                    pe.wait_ge(h_ready, 4 * k + n + 1)
                    tt, q = n // 2, n % 2
                    turn(first + n, [h[:, tt, (4 * q + c) * P:(4 * q + c + 1) * P] for c in range(4)])
                moved(pe, first + 3)

            moved(pe, T_HID - 3)
            moved(pe, T_HID - 4)
            attention(JOBS_A, 0, T_JA, 0, AT["out_a"], compress, LAGS_A)
            mix_out(AT["out_a"], 8)
            next_h(0, T_H1)

            for c in range(N_DENSE):
                if c >= 2:
                    pe.wait_ge(act_ready, c - 1)
                for gu in range(2):
                    n = AT["dense_in"] + 2 * c + gu
                    ready(n)
                    wts = both(n, DC)
                    for j in range(2):
                        for k in range(DC):
                            ins = product(bank[2 * (c % 2) + gu][:, 256 * j:256 * j + 256],
                                          [t[:, k, P * j:P * j + P] for t in wts], [t[:, k, :] for t in (hTh, hTl)],
                                          k == 0, k == DC - 1)
                    ins.then_inc(used, 1)
            moved(pe, T_H1 + 3)
            for c, tt in [(c, tt) for c in range(N_DENSE - 2) for tt in range(NT)] +\
                    [(c, tt) for tt in range(NT) for c in range(N_DENSE - 2, N_DENSE)]:
                n = AT["dense_out"] + c
                if tt == 0:
                    ready(n)
                    pe.wait_ge(act_low, c + 1)
                wts = both(n, 2)
                for half in range(2):
                    for j in range(2):
                        ins = product(bank[4 + 2 * half + tt][:, :],
                                      [t[:, 2 * c + j, tt * P:tt * P + P] for t in (actTh, actTl)],
                                      [t[:, j, 512 * half:512 * half + 512] for t in wts],
                                      (c == 0 and j == 0), (c == N_DENSE - 1 and j == 1))
                    if tt == NT - 1 and half == 1:
                        ins.then_inc(used, 1)
                    elif c == N_DENSE - 1:
                        ins.then_inc(mixed, 1)
            next_h(1, T_H2)

            projections(PROJ_B, len(PROJ_A), first_b, LAST_B)
            moved(pe, first_b[-3] - 1)
            moved(pe, first_b[-3] - 2)
            attention(JOBS_B, len(JOBS_A), T_JB, 8, AT["out_b"], turn_last_b, LAGS_B)
            mix_out(AT["out_b"], 16)
            next_h(2, T_H3)

            pe.wait_ge(router_low, 1)
            for c in range(DC):
                ins = product(bank[6][0:NE, 0:SEQ], [t[:, c, :] for t in (routerh, routerl)],
                              [t[:, c, :] for t in (hTh, hTl)], c == 0, c == DC - 1)
            ins.then_inc(routed, 1)
            pe.wait_ge(logits_moved, 1)
            for tt in range(NT):
                ins = pe.transpose(bank[6][:, 256 + NE * tt:256 + NE * tt + NE], lgT[:, tt * P:tt * P + P],
                                   ident[0:NE, 0:NE])
            ins.then_inc(routed, 1)
            pe.wait_ge(sel_ready, 1)
            pe.matmul(bank[7][:, 0:NE], earlier[:, :], selb[:, 0, :], start=True, stop=True)
            pe.matmul(bank[7][:, NE:2 * NE], onesb[:, :], selb[:, 0, :], start=True, stop=False)
            pe.matmul(bank[7][:, NE:2 * NE], earlier[:, :], selb[:, 1, :], start=False, stop=True)
            pe.matmul(bank[7][:, 2 * NE:3 * NE], onesb[:, :], selb[:, 0, :], start=True, stop=False)
            pe.matmul(bank[7][:, 2 * NE:3 * NE], onesb[:, :], selb[:, 1, :], start=False, stop=True)\
              .then_inc(ranked, 1)

            def gather(value):
                pe.wait_ge(e_pick, value)
                for c in range(DC):
                    for tt in range(NT):
                        ins = pe.matmul(bank[2 + c // 4][:, (c % 4) * P:(c % 4) * P + P], h[:, tt, c * P:c * P + P],
                                        pick[:, tt, :], start=(tt == 0), stop=(tt == NT - 1))
                    if c % 4 == 3:
                        ins.then_inc(e_rows, 1)

            def scatter(v, n, last=False):
                if n == 0:
                    pe.wait_ge(e_putT_moved, v)
                    pe.wait_ge(e_y_a, v)
                if n == 1:
                    pe.wait_ge(e_y_v, v)
                tt, half = n // 2, n % 2
                if n >= 2 and not last:
                    pe.wait_ge(e_added, 4 * v + n - 4)
                pe.matmul(bank[n if last and n >= 2 else 4 + n % 2][:, :], putT[:, tt, :], ysb[:, 512 * half:512 * half + 512],
                          start=True, stop=True).then_inc(e_back, 1)

            pe.sem_inc(e_turned, 1)
            pe.sem_inc(e_putT, 1)
            gather(1)
            pe.wait_ge(plan_ready, 1)
            steps = pe.value_load(turns_i[0:1, 0:1], min_val=NE, max_val=2 * NE)
            with pe.Fori(0, steps) as i:
                for k, (kind, f, half) in enumerate(EXPERT):
                    n = N_FIRST + k
                    if k < 2:
                        pe.wait_ge(e_rows_low, 2 * i + k + 1)
                    if kind == "g" and half == 0:
                        pe.wait_ge(e_act, i * FT + max(f - 1, 0) + 1)
                    if kind == "o" and half == 0:
                        pe.wait_ge(e_low, i * FT + f + 1)
                    pe.wait_ge(split, n + 1 + PER_EXPERT * i)
                    if kind == "o":
                        wts = both(n, 2)
                        for j in range(2):
                            for side in range(2):
                                ins = product(bank[6 + side][:, :],
                                              [t[:, f % 2, 2 * half + j, :] for t in (eactTh, eactTl)],
                                              [t[:, j, 512 * side:512 * side + 512] for t in wts],
                                              (f == 0 and half == 0 and j == 0), (f == FT - 1 and half == 1 and j == 1))
                    else:
                        wts = both(n, 4)
                        for c in range(4):
                            ins = product(bank[2 * (f % 2) + (kind == "u")][:, :],
                                          [t[:, 4 * half + c, :] for t in (xgTh, xgTl)], [t[:, c, :] for t in wts],
                                          (half == 0 and c == 0), (half == 1 and c == 3))
                    ins.then_inc(used, 1)
                    if k in BACK_AFTER:
                        for m in range(2):
                            scatter(i + 1, 2 * BACK_AFTER.index(k) + m)
                    if k in TURN_AFTER:
                        t = TURN_AFTER.index(k)
                        pe.wait_ge(e_act, i * FT + t + 2)
                        if t < 2:
                            pe.wait_ge(e_added, 4 * i + 5)
                        else:
                            pe.wait_ge(e_low, i * FT + t - 1)
                        for j in range(4):
                            ins = pe.transpose(bank[4 + t % 2][:, j * P:j * P + P], act[:, t % 2, j * P:j * P + P],
                                               ident[:, :])
                        ins.then_inc(e_turned, 1)
                        if t == FT - 1:
                            pe.wait_ge(e_put, i + 1)
                            for tt in range(NT):
                                ins = pe.transpose(bank[5][:, tt * P:tt * P + P], put[:, tt, :], ident[:, :])
                            ins.then_inc(e_putT, 1)
                            gather(i + 2)
            for n in range(4):
                scatter(steps + 1, n, last=True)

        @block.vector
        def _(dve):
            n_step = [0]

            def step(ins):
                n_step[0] += 1
                ins.then_inc(dve_step, 1)
                dve.wait_ge(dve_step, n_step[0])

            n_split = [0]

            def split_weights(upto):
                for n in range(n_split[0], upto):
                    dve.wait_ge(rounded, n + 1)
                    size = size_of(n)
                    dve.tensor_tensor(wl[:, n % SPLITS, 0:size], slot_of(n)[:, 0:size],
                                      wh[:, n % SPLITS, 0:size].bitcast(F32), ALU.subtract).then_inc(split, 1)
                n_split[0] = max(n_split[0], upto)

            n_high = [0]

            def turn_h(first):
                for n in range(4):
                    tt, q = n // 2, n % 2
                    n_high[0] += 1
                    dve.wait_ge(high, n_high[0])
                    there = (slice(None), slice(4 * q, 4 * q + 4), slice(tt * P, tt * P + P))
                    dve.tensor_tensor(hTl[there], bank[TBANK[first + n]][:, :].rearrange("p (c n) -> p c n", c=4),
                                      hTh[there].bitcast(F32), ALU.subtract).then_inc(moved_v, 1)

            turn_h(T_X)
            split_weights(SPLITS)

            dve.wait_ge(pos_landed, 16)
            dve.wait_ge(consts, 2)
            step(dve.tensor_copy(pos_f[:, :], pos_i[:, :]))
            for tt in range(NT):
                step(dve.tensor_scalar(ang[:, 0, tt, :], freq[:, :], pos_f[:, tt:tt + 1], None, ALU.mult))
            a, turns, r = ang[:, 0, :, :], ang[:, 1, :, :], ang[:, 2, :, :]
            step(dve.tensor_scalar(turns, a, 0.15915494309189535, 12582912.0, ALU.mult, ALU.add))
            step(dve.tensor_scalar(turns, turns, 12582912.0, None, ALU.subtract))
            for part in TWO_PI_PARTS:
                step(dve.scalar_tensor_tensor(out=a, in0=turns, scalar=-part, in1=a, op0=ALU.mult, op1=ALU.add))
            step(dve.tensor_scalar(turns, a, 3.1415925, -3.1415925, ALU.min, ALU.max))
            step(dve.tensor_scalar(r, turns, -1.0, None, ALU.mult))
            step(dve.tensor_tensor(r, turns, r, ALU.max))
            dve.tensor_scalar(r, r, -1.0, 1.5707963267948966, ALU.mult, ALU.add).then_inc(trig_in, 1)
            dve.wait_ge(trig, 2)
            dve.tensor_copy(cc[:, :, 8:16], cc[:, :, 0:8])
            step(dve.tensor_scalar(ss[:, :, 8:16], ss[:, :, 0:8], -1.0, None, ALU.mult))
            dve.wait_ge(post, 1)
            dve.tensor_copy(posT[:, :, :], bank[3][:, 0:32].rearrange("p (v j) -> p v j", v=2)).then_inc(post_moved, 1)
            dve.wait_ge(small_landed, 16 * 7)
            step(dve.tensor_scalar(nsink[:, :], sink[:, :], -1.0, None, ALU.mult))
            dve.wait_ge(router_high, 1)
            dve.tensor_tensor(routerl[:, :, :], router[:, :, :], routerh[:, :, :].bitcast(F32), ALU.subtract)\
               .then_inc(router_low, 1)

            def rotate(src, dst, tt, heads):
                wide = [P, heads, ROT]
                c = cc[:, tt, :].rearrange("p (a n) -> p a n", a=1).to_broadcast(wide)
                s = ss[:, tt, :].rearrange("p (a n) -> p a n", a=1).to_broadcast(wide)
                dve.tensor_tensor(rot1[:, 0:heads, :], src, c, ALU.mult)
                step(dve.tensor_tensor(rot2[:, 0:heads, :], src, s, ALU.mult))
                dve.tensor_tensor(dst[..., 0:8], rot1_of(dst, heads, 0), rot2_of(dst, heads, 8), ALU.add)
                return dve.tensor_tensor(dst[..., 8:16], rot1_of(dst, heads, 8), rot2_of(dst, heads, 0), ALU.add)

            def rot1_of(dst, heads, at):
                v = rot1[:, 0:heads, at:at + 8]
                return v.rearrange("p (b r) d -> p b r d", b=2) if len(dst.shape) == 4 else v

            def rot2_of(dst, heads, at):
                v = rot2[:, 0:heads, at:at + 8]
                return v.rearrange("p (b r) d -> p b r d", b=2) if len(dst.shape) == 4 else v

            def stage_part(j, proj, base, nturn):
                kind, _, tt, w = proj[j]
                if j >= 1:
                    dve.wait_ge(staged_v, base + j)
                dve.wait_ge(staged_a, base + j + 1)
                src = bank[out_bank(proj, j)]
                s = stage[:, j % 2, :]
                if j >= 2:
                    dve.wait_ge(turned, nturn[j - 1])
                if kind == "cmpkv":
                    dve.tensor_copy(s.rearrange("p (g a d) -> p g a d", g=8, a=2)[:, :, 1, :],
                                    src[:, :].rearrange("p (g d) -> p g d", g=8)).then_inc(staged_v, 1)
                elif kind in ("slckv", "winkv", "kv"):
                    nk = w // 2
                    rotate(src[:, 0:nk].rearrange("p (g d) -> p g d", d=HD)[:, :, 0:ROT],
                           s[:, 0:nk].rearrange("p (g d) -> p g d", d=HD)[:, :, 0:ROT], tt, nk // HD)\
                        .then_inc(staged_v, 1)
                elif kind == "gate":
                    dve.tensor_scalar(gates[:, tt, 0:16], gates[:, tt, 0:16], seen[:, tt:tt + 1], None, ALU.mult)\
                       .then_inc(staged_v, 1)
                elif kind in ("q0", "q1"):
                    dst = s[:, 512:1024].rearrange("p (r b d) -> p b r d", r=4, b=2)
                    dve.tensor_copy(dst[:, :, :, ROT:],
                                    src[:, :].rearrange("p (b r d) -> p b r d", b=2, r=4)[:, :, :, ROT:])
                    rotate(src[:, :].rearrange("p (r d) -> p r d", r=8)[:, :, 0:ROT], dst[:, :, :, 0:ROT], tt, 8)\
                        .then_inc(staged_v, 1)
                else:
                    rotate(src[:, :].rearrange("p (r d) -> p r d", r=8)[:, :, 0:ROT],
                           s[:, 0:512].rearrange("p (r b d) -> p b r d", r=4, b=2)[:, :, :, 0:ROT], tt, 8)\
                        .then_inc(staged_v, 1)

            def take_turned(j, proj, first):
                kind, _, tt, _ = proj[j]
                cols = slice(tt * P, tt * P + P)
                for t, n in enumerate(range(first[j], first[j + 1])):
                    if n % 2 == 0:
                        continue
                    dve.wait_ge(turned, n + 1)
                    src = bank[TBANK[n]]
                    four = src[:, :].rearrange("p (g n) -> p g n", g=4)
                    if kind == "cmpkv":
                        lo = 1 if tt == 0 else 0
                        dve.tensor_copy(kcvT[0:64, t, :, cols], four[0:64])
                        ins = dve.tensor_copy(kcvT[64:128, t, :, tt * P + lo - 1:tt * P + P - 1], four[64:128, :, lo:])
                    elif kind in ("slckv", "winkv"):
                        ins = dve.tensor_copy((ksT if kind == "slckv" else kwT)[:, :, cols],
                                              src[:, 0:256].rearrange("p (g n) -> p g n", g=2))
                    elif kind in ("q0", "q1"):
                        pb = int(kind[-1])
                        ins = dve.tensor_copy((qrT if t else qT)[:, 4 * pb:4 * pb + 4, cols], four)
                    elif kind == "kv":
                        ins = dve.tensor_copy(ksT[:, 0, cols], src[:, 0:P])
                    else:
                        pb = int(kind[-1])
                        ins = dve.tensor_copy(qrT[:, 4 * pb:4 * pb + 4, cols], four)
                    ins.then_inc(moved_v, 1)

            def build_cmp_in():
                moved(dve, first_a[2] - 1)
                moved(dve, first_a[2] - 2)
                for kv in range(2):
                    for g in range(4):
                        by_row = kcvT[:, kv, g, :].rearrange("p (n s two) -> p s n two", s=8, two=2)[:, :, :, 0]
                        for upper in range(2):
                            pos = posT[:, kv, 8 * upper:8 * upper + 8].rearrange("p (j n) -> p j n", n=1)\
                                .to_broadcast([P, 8, N_CMP])
                            ins = dve.tensor_tensor(cmp_in[:, kv, 8 * upper:8 * upper + 8, 16 * g:16 * g + N_CMP],
                                                    by_row[:, :, upper:upper + N_CMP], pos, ALU.add)
                ins.then_inc(cmp_sum, 1)

            def projections(proj, base, first, last):
                for m in range(len(last)):
                    split_weights(last[m] + SPLITS)
                    if m >= 1:
                        for tt in range(NT):
                            take_turned(NT * (m - 1) + tt, proj, first)
                    for tt in range(NT):
                        stage_part(NT * m + tt, proj, base, first)
                    if proj is PROJ_A:
                        if m == 1:
                            build_cmp_in()
                        if m == 2:
                            dve.wait_ge(cmp_high, 1)
                            dve.tensor_tensor(cmp_l[:, :, :, :], cmp_in, cmp_h[:, :, :, :].bitcast(F32), ALU.subtract)\
                               .then_inc(cmp_low, 1)

            projections(PROJ_A, 0, first_a, LAST_A)
            split_weights(AT["cmp"] + 3 + SPLITS + 1)
            for tt in range(NT):
                take_turned(len(PROJ_A) - NT + tt, PROJ_A, first_a)

            def compress():
                if T_HID % 2:
                    dve.wait_ge(turned, T_HID + 1)
                    for twice in range(2):
                        ins = dve.tensor_copy(hidT.rearrange("p a c n -> p (a c) n")[:, :, 64 * twice:64 * twice + 64],
                                              bank[TBANK[T_HID]][:, 0:256].rearrange("p (g n) -> p g n", g=4))
                    ins.then_inc(moved_v, 1)
                dve.wait_ge(kc_ready, 1)
                dve.tensor_copy(vc, bank[7][:, P:2 * P]).then_inc(vc_ready, 1)

            def take_last_b():
                for tt in range(NT):
                    take_turned(len(PROJ_B) - NT + tt, PROJ_B, first_b)

            def attention(jobs, base, first, swa, heads, prepare, lags):
                lag, lag_v = lags
                for i in range(len(jobs) + lag_v + 1):
                    if i == 1:
                        prepare()
                    if i < len(jobs):
                        br, pb, b, tt, h0, nh, w, _, _ = jobs[i]
                        dve.wait_ge(scored, base + i + 1)
                        step(dve.tensor_reduce(mx[:, i % 4, 0:nh], bank[i % 4][:, :].rearrange("p (k n) -> p k n", k=nh),
                                               X, ALU.max))
                        if swa:
                            h_at = 8 * b + 4 * pb + h0
                            step(dve.scalar_tensor_tensor(out=nb[:, i % 4, 0:nh], in0=mx[:, i % 4, 0:nh], scalar=-SCALE,
                                                          in1=nsink[:, h_at:h_at + nh], op0=ALU.mult, op1=ALU.min))
                            dve.tensor_tensor(sn[:, i % 4, 0:nh], sink[:, h_at:h_at + nh], nb[:, i % 4, 0:nh], ALU.add)\
                               .then_inc(shifted, 1)
                        else:
                            dve.tensor_scalar(nb[:, i % 4, 0:nh], mx[:, i % 4, 0:nh], -SCALE, None, ALU.mult)\
                               .then_inc(shifted, 1)
                    if 1 <= i <= len(jobs):
                        br, pb, b, tt, h0, nh, w, _, _ = jobs[i - 1]
                        m = (i - 1) % 4
                        dve.wait_ge(expd, base + i)
                        if swa:
                            step(dve.tensor_tensor(sums[:, m, 0:nh], sums[:, m, 0:nh], es[:, m, 0:nh], ALU.add))
                        step(dve.reciprocal(rg[:, m, 0:nh], sums[:, m, 0:nh]))
                        if not swa:
                            g_at = 16 * ("cmp", "slc", "win").index(br) + 4 * (2 * pb + b) + h0
                            step(dve.tensor_tensor(rg[:, m, 0:nh], rg[:, m, 0:nh], gates[:, tt, g_at:g_at + nh], ALU.mult))
                        e = ex[:, (i - 1) % (lag + 1), :].rearrange("p (k n) -> p k n", k=nh)
                        dve.tensor_tensor(e, e, rg[:, m, 0:nh].rearrange("p (k n) -> p k n", n=1).to_broadcast([P, nh, w]),
                                          ALU.mult).then_inc(normed, 1)
                    if lag <= i < len(jobs) + lag and (first + i - lag) % 2:
                        n = first + i - lag
                        dve.wait_ge(turned, n + 1)
                        if i > lag_v:
                            dve.wait_ge(summed, base + i - lag_v)
                        dve.tensor_copy(pT[:, n % (lag_v - lag + 1), :], bank[5][:, :]).then_inc(moved_v, 1)
                    if i > lag_v and jobs[i - lag_v - 1][8]:
                        _, pb, b, tt, _, _, _, _, _ = jobs[i - lag_v - 1]
                        heads += 1
                        dve.wait_ge(heads_high, heads)
                        there = (slice(64 * b, 64 * b + 64), slice(4 * pb, 4 * pb + 4), slice(tt * P, tt * P + P))
                        dve.tensor_tensor(hTl[there], bank[6 + (heads - 1) % 2][64 * b:64 * b + 64, :]
                                          .rearrange("p (r n) -> p r n", r=4), hTh[there].bitcast(F32), ALU.subtract)\
                           .then_inc(heads_out, 1)

            def chained(ins):
                n_step[0] += 1
                ins.then_inc(dve_step, 1)

            def add_mix(b, tt, half):
                cols = slice(512 * half, 512 * half + 512)
                step(dve.scalar_tensor_tensor(out=pre[:, tt, cols], in0=h[:, tt, cols], scalar=ALPHA,
                                              in1=bank[b][:, :], op0=ALU.mult, op1=ALU.add))
                chained(dve.bn_stats(stats[:, tt, half, :], pre[:, tt, cols]))

            def center(tt):
                dve.wait_ge(dve_step, n_step[0])
                step(dve.bn_aggr(mv[:, tt, :], stats[:, tt, :, :].rearrange("p a b -> p (a b)")))
                dve.tensor_scalar(std[:, tt, 1:2], mv[:, tt, 1:2], LN_EPS, None, ALU.add).then_inc(var_ready, 1)
                chained(dve.scalar_tensor_tensor(out=pre[:, tt, :], in0=pre[:, tt, :], scalar=mv[:, tt, 0:1],
                                                 in1=lnp[:, 0, :], op0=ALU.subtract, op1=ALU.mult))

            def scale(k, tt):
                dve.wait_ge(std_ready, NT * k + tt + 1)
                step(dve.reciprocal(std[:, tt, 1:2], std[:, tt, 0:1]))
                for q in range(2):
                    cols = slice(512 * q, 512 * q + 512)
                    dve.scalar_tensor_tensor(out=h[:, tt, cols], in0=pre[:, tt, cols], scalar=std[:, tt, 1:2],
                                             in1=lnp[:, 1, cols], op0=ALU.mult, op1=ALU.add).then_inc(h_ready, 1)

            def norm(k, banks, mixes, after, first):
                split_weights(after + 2)
                dve.wait_ge(ln_landed, 32 * (k + 1))
                for half in range(2):
                    dve.wait_ge(mixed, mixes + half + 1)
                    add_mix(banks[half][0], 0, half)
                center(0)
                scale(k, 0)
                if k == 1:
                    dve.wait_ge(mixed, mixes + 3)
                else:
                    dve.wait_ge(used, after)
                add_mix(banks[0][1], 1, 0)
                dve.wait_ge(used, after + 1)
                add_mix(banks[1][1], 1, 1)
                center(1)
                scale(k, 1)
                turn_h(first)

            attention(JOBS_A, 0, T_JA, False, 0, compress, LAGS_A)
            split_weights(AT["out_a"] + 4)
            norm(0, ((0, 1), (2, 3)), 0, AT["out_a"] + 3, T_H1)
            for c in range(N_DENSE + 1):
                if c < N_DENSE:
                    n = AT["dense_in"] + 2 * c + 1
                    split_weights(n + SPLITS)
                    dve.wait_ge(silu_ready, c + 1)
                    dve.wait_ge(used, n + 1)
                    dve.tensor_tensor(silu[:, c % 2, :], silu[:, c % 2, :], bank[2 * (c % 2) + 1][:, :], ALU.mult)\
                       .then_inc(act_ready, 1)
                if c >= 1:
                    dve.wait_ge(act_high, c)
                    there = (slice(None), slice(2 * c - 2, 2 * c), slice(None))
                    dve.tensor_tensor(actTl[there], silu[:, (c - 1) % 2, :].rearrange("p (a n) -> p a n", a=2),
                                      actTh[there].bitcast(F32), ALU.subtract).then_inc(act_low, 1)
            norm(1, ((4, 5), (6, 7)), 2, AT["dense_out"] + N_DENSE - 1, T_H2)
            projections(PROJ_B, len(PROJ_A), first_b, LAST_B)
            split_weights(AT["out_b"] + SPLITS)
            attention(JOBS_B, len(JOBS_A), T_JB, True, 8, take_last_b, LAGS_B)
            split_weights(N_FIRST)
            norm(2, ((0, 1), (2, 3)), 5, AT["out_b"] + 3, T_H3)
            split_weights(N_FIRST + SPLITS)

            def build_pick(at, value):
                if value is not None:
                    dve.wait_ge(e_rows, 2 * value)
                for tt in range(NT):
                    ins = dve.tensor_scalar(pick[:, tt, :], slots[:, :], slotx[:, tt, at], None, ALU.is_equal)
                ins.then_inc(e_pick, 1)

            logits = bank[6][:, 256:256 + NT * NE].rearrange("p (t e) -> p t e", t=NT)
            best, pick1, rest, pick2, sel, gw, tmp = (lg[:, k, :, :] for k in range(7))
            wide = [P, NT, NE]
            m1, x1, m2, x2 = (top[:, k, :, :] for k in range(4))
            gap, egap, g1, g2, den = (top[:, k, :, :] for k in range(4, 9))
            dve.wait_ge(routed, 1)
            dve.tensor_copy(lgT[:, :], bank[6][0:NE, 0:SEQ]).then_inc(logits_moved, 1)
            dve.wait_ge(routed, 2)

            def pick_largest(values, m, x_, onehot):
                step(dve.tensor_reduce(m, values, X, ALU.max))
                step(dve.tensor_tensor(best, values, m.to_broadcast(wide), ALU.is_equal))
                step(dve.tensor_tensor(best, best, order[:, :, :], ALU.mult))
                step(dve.tensor_reduce(x_, best, X, ALU.max))
                step(dve.tensor_tensor(onehot, best, x_.to_broadcast(wide), ALU.is_equal))

            pick_largest(logits, m1, x1, pick1)
            step(dve.scalar_tensor_tensor(out=rest, in0=pick1, scalar=NEG, in1=logits, op0=ALU.mult, op1=ALU.add))
            pick_largest(rest, m2, x2, pick2)
            dve.tensor_tensor(gap, m2, m1, ALU.subtract).then_inc(gap_ready, 1)
            step(dve.tensor_tensor(sel, pick1, pick2, ALU.add))
            dve.tensor_copy(selb[:, :, :], sel).then_inc(sel_ready, 1)
            dve.wait_ge(ranked, 1)
            step(dve.tensor_scalar(tmp, bank[7][:, 0:NT * NE].rearrange("p (t e) -> p t e", t=NT), 1.0, None, ALU.add))
            step(dve.tensor_tensor(tmp, tmp, sel, ALU.mult))
            step(dve.tensor_scalar(slotx[:, :, 0:NE], tmp, -1.0, None, ALU.add))
            build_pick(slice(0, 1), None)
            step(dve.tensor_scalar(slotx[:, :, NE:2 * NE], tmp, -1.0 - P, None, ALU.add))
            step(dve.tensor_reduce(cnt[:, 0:1], bank[7][:, 2 * NE:3 * NE], X, ALU.max))
            step(dve.tensor_scalar(cnt[:, 1:2], cnt[:, 0:1], float(P), None, ALU.is_gt))
            dve.tensor_scalar(turns_i[:, :], cnt[:, 1:2], float(NE), float(NE), ALU.mult, ALU.add)\
               .then_inc(plan_ready, 1)

            dve.wait_ge(gap_exp, 1)
            step(dve.tensor_scalar(den, egap, 1.0, None, ALU.add))
            step(dve.reciprocal(g1, den))
            step(dve.tensor_tensor(g2, egap, g1, ALU.mult))
            step(dve.tensor_tensor(gw, pick1, g1.to_broadcast(wide), ALU.mult))
            step(dve.tensor_tensor(tmp, pick2, g2.to_broadcast(wide), ALU.mult))
            dve.tensor_tensor(gatex[:, :, 0:NE], gw, tmp, ALU.add)
            step(dve.tensor_tensor(gatex[:, :, NE:2 * NE], gw, tmp, ALU.add))

            def take_rows(value):
                for q in range(2):
                    dve.wait_ge(e_rows_high, 2 * value + q - 1)
                    there = (slice(None), slice(4 * q, 4 * q + 4), slice(None))
                    dve.tensor_tensor(xgTl[there], bank[2 + q][:, :].rearrange("p (c n) -> p c n", c=4),
                                      xgTh[there].bitcast(F32), ALU.subtract).then_inc(e_rows_low, 1)

            def add_back(v, parts, last=False):
                dve.wait_ge(e_added, 4 * v - 3)
                for n in parts:
                    tt, half = n // 2, n % 2
                    dve.wait_ge(e_back, 4 * v + n - 3)
                    cols = slice(512 * half, 512 * half + 512)
                    dve.tensor_tensor(pre[:, tt, cols], pre[:, tt, cols],
                                      bank[n if last and n >= 2 else 4 + n % 2][:, :], ALU.add)\
                       .then_inc(e_added, 1)

            dve.memset(putT, 0.0).then_inc(e_putT_moved, 1)
            dve.memset(ysb, 0.0).then_inc(e_y_v, 1)
            dve.sem_inc(e_act, 1)
            take_rows(1)
            dve.wait_ge(plan_ready, 1)
            steps = dve.value_load(turns_i[0:1, 0:1], min_val=NE, max_val=2 * NE)
            with dve.Fori(0, steps) as i:
                for k in range(SPLITS, PER_EXPERT + SPLITS):
                    for what, f in EXPERT_WORK.get(k, ()):
                        if what == "act":
                            dve.wait_ge(e_silu, i * FT + f + 1)
                            expert_used(dve, i, LAST_GU[f])
                            dve.wait_ge(e_turned, i * FT + max(f - 1, 0) + 1)
                            dve.tensor_tensor(act[:, f % 2, :], esilu[:, f % 2, :], bank[2 * (f % 2) + 1][:, :], ALU.mult)\
                               .then_inc(e_act, 1)
                        elif what == "turn":
                            dve.wait_ge(e_high, i * FT + f + 1)
                            dve.tensor_tensor(eactTl[:, f % 2, :, :], bank[4 + f % 2][:, :].rearrange("p (c n) -> p c n", c=4),
                                              eactTh[:, f % 2, :, :].bitcast(F32), ALU.subtract).then_inc(e_low, 1)
                        elif what == "back":
                            add_back(i + 1, range(2 * f, 2 * f + 2))
                        elif what == "y":
                            expert_used(dve, i, PER_EXPERT - 1)
                            dve.tensor_copy(ysb[:, 512:1024], bank[7][:, :]).then_inc(e_y_v, 1)
                        elif what == "build":
                            build_pick(ds(i + 1, 1), i + 1)
                            dve.wait_ge(e_putT, i + 1)
                            for tt in range(NT):
                                ins = dve.tensor_scalar(put[:, tt, :], slots[:, :], slotx[:, tt, ds(i, 1)],
                                                        gatex[:, tt, ds(i, 1)], ALU.is_equal, ALU.mult)
                            ins.then_inc(e_put, 1)
                        else:
                            dve.wait_ge(e_putT, i + 2)
                            dve.tensor_copy(putT, bank[5][:, 0:2 * P].rearrange("p (t n) -> p t n", t=NT))\
                               .then_inc(e_putT_moved, 1)
                            take_rows(i + 2)
                    n = N_FIRST + k
                    dve.wait_ge(rounded, n + 1 + PER_EXPERT * i)
                    dve.tensor_tensor(wl[:, n % SPLITS, :], slot_at[SLOT[k % PER_EXPERT]], wh[:, n % SPLITS, :].bitcast(F32),
                                      ALU.subtract).then_inc(split, 1)

            dve.wait_ge(ln_landed, 32 * 4)
            for tt in range(NT):
                add_back(steps + 1, range(2 * tt, 2 * tt + 2), last=True)
                dve.wait_ge(e_added, 4 * steps + 3 + 2 * tt)
                for half in range(2):
                    chained(dve.bn_stats(stats[:, tt, half, :], pre[:, tt, 512 * half:512 * half + 512]))
                center(tt)
            for tt in range(NT):
                scale(3, tt)


_INS = ['x', 'positions', 'w_in_a', 'w_out_a', 'cmp_pos', 'cmp_w1', 'cmp_w2', 'w_kv_shared', 'w_q_b', 'w_out_b',
        'sinks_b', 'ln_g', 'ln_b', 'dense_w_in', 'dense_w_out', 'moe_router', 'moe_w_in', 'moe_w_out']


def kernel(**inputs):
    import numpy as _np
    import concourse.bacc as _bacc
    from concourse import mybir as _mybir
    from concourse.bass_utils import run_bass_kernel_spmd as _run

    nc = _bacc.Bacc("TRN2", target_bir_lowering=False, num_devices=1)
    arrays, args = {}, []
    for name in _INS:
        a = _np.ascontiguousarray(inputs[name])
        arrays[f"in_{name}_dram"] = a
        args.append(nc.dram_tensor(f"in_{name}_dram", a.shape, _mybir.dt.from_np(a.dtype), kind="ExternalInput").ap())
    args.append(nc.dram_tensor("out_0_dram", (1, SEQ, D), F32, kind="ExternalOutput").ap())
    decoder_kernel(nc, *args)
    r = _run(nc, [arrays], core_ids=[0])
    return r.results[0]["out_0_dram"]
```
